# Optimizing a Trainium2 kernel written in Bass

```python
import jax, jax.numpy as jnp
from jax import lax
import numpy as np
import math

D_MODEL = 1024
BATCH = 1
SEQ = 512
DEPTH = 1

CHUNK = 64
N_META = 16
PAD = CHUNK - N_META
A_KDIM = 128
A_HEADS = D_MODEL // A_KDIM
A_FDIM = A_HEADS * A_KDIM
A_WIDTH = D_MODEL // 2
A_VDIM = A_WIDTH // A_HEADS
POOL_WINDOWS = (2, 4, 8, 16)
B_GROUPS = 4
B_WIDTH = D_MODEL // 2
B_GDIM = B_WIDTH // B_GROUPS
N_BRANCH = 2
SPLITS = (A_FDIM, 2 * A_FDIM, 2 * A_FDIM + A_WIDTH, 2 * A_FDIM + 2 * A_WIDTH,
          2 * A_FDIM + 2 * A_WIDTH + B_WIDTH, 2 * A_FDIM + 2 * A_WIDTH + B_WIDTH + D_MODEL)
IN_COLS = 2 * A_FDIM + 2 * A_WIDTH + B_WIDTH + N_BRANCH * D_MODEL
D_FF = ((8 * D_MODEL // 3 + 127) // 128) * 128
CONV_W = 3
EPS = 1e-6


def rmsnorm(x, g):
    xf = x.astype(jnp.float32)
    y = xf * lax.rsqrt(jnp.mean(xf * xf, axis=-1, keepdims=True) + EPS)
    return (y * g.astype(jnp.float32)).astype(x.dtype)

def hgrn2_mixer(q, f_logit, i, og, lb, head_g):
    dt = i.dtype
    f32 = jnp.float32
    B_, T, _ = q.shape
    n_chunks = (T + PAD) // CHUNK
    lbf = lb.astype(f32)
    f = lbf + (1.0 - lbf) * jax.nn.sigmoid(f_logit.astype(f32))
    k = 1.0 - f
    logf = jnp.log(f)
    qf = jax.nn.silu(q.astype(f32))
    vf = i.astype(f32)

    def to_chunks(t, d):
        t = jnp.pad(t, ((0, 0), (PAD, 0), (0, 0)))
        return t.reshape(B_, n_chunks, CHUNK, A_HEADS, d).transpose(1, 0, 3, 2, 4)

    qc = to_chunks(qf, A_KDIM)
    kc = to_chunks(k, A_KDIM)
    vc = to_chunks(vf, A_VDIM)
    ac = jnp.cumsum(to_chunks(logf, A_KDIM), axis=3)
    causal = jnp.tril(jnp.ones((CHUNK, CHUNK), dtype=bool))[:, :, None]

    def step(S, inp):
        q_, k_, v_, a_ = inp
        o_inter = jnp.einsum('bhtk,bhkv->bhtv', q_ * jnp.exp(a_), S)
        diff = a_[:, :, :, None, :] - a_[:, :, None, :, :]
        decay = jnp.exp(jnp.where(causal, diff, -jnp.inf))
        scores = jnp.einsum('bhtsk,bhsk->bhts', q_[:, :, :, None, :] * decay, k_)
        o = o_inter + jnp.einsum('bhts,bhsv->bhtv', scores, v_)
        a_last = a_[:, :, -1:, :]
        S = jnp.exp(a_last[:, :, 0, :])[..., None] * S + jnp.einsum(
            'bhsk,bhsv->bhkv', k_ * jnp.exp(a_last - a_), v_)
        return S, o

    S0 = jnp.zeros((B_, A_HEADS, A_KDIM, A_VDIM), f32)
    _, o = lax.scan(step, S0, (qc, kc, vc, ac))
    o = o.transpose(1, 0, 3, 2, 4).reshape(B_, n_chunks * CHUNK, A_HEADS, A_VDIM)[:, PAD:]
    o = o * lax.rsqrt(jnp.mean(o * o, axis=-1, keepdims=True) + EPS)
    o = o * head_g.astype(f32).reshape(A_HEADS, A_VDIM)
    o = o.reshape(B_, T, A_WIDTH) * jax.nn.silu(og.astype(f32))
    return o.astype(dt)

def pool_mixer(p, w_group, scale):
    dt = p.dtype
    B_, T, _ = p.shape
    pf = p.astype(jnp.float32).reshape(B_, T, B_GROUPS, B_GDIM)
    cs = jnp.cumsum(pf, axis=1)
    pos = jnp.arange(1, T + 1, dtype=jnp.float32)
    outs = []
    for gi, w in enumerate(POOL_WINDOWS):
        c = cs[:, :, gi]
        lag = jnp.pad(c[:, :-w], ((0, 0), (w, 0), (0, 0)))
        mean = (c - lag) / jnp.minimum(pos, float(w))[None, :, None]
        outs.append(mean - pf[:, :, gi])
    d = jnp.stack(outs, axis=2)
    y = jnp.einsum('btgc,gcd->btgd', d, w_group.astype(jnp.float32)).reshape(B_, T, B_WIDTH)
    return (y * scale.astype(jnp.float32)).astype(dt)

def causal_dwconv(u, w, b):
    C = u.shape[-1]
    up = jnp.pad(u, ((0, 0), (CONV_W - 1, 0), (0, 0)))
    y = lax.conv_general_dilated(up, w[:, None, :].astype(u.dtype), window_strides=(1,), padding='VALID',
                                 dimension_numbers=('NWC', 'WIO', 'NWC'), feature_group_count=C)
    return y + b

def first_inputs(seed: int = 0) -> dict:
    key = jax.random.key(seed)
    ks = jax.random.split(key, 20)
    f32 = jnp.float32
    nrm = lambda k, shape, s: jax.random.normal(k, shape, f32) * s
    L = DEPTH
    return {
        "x": nrm(ks[0], (BATCH, SEQ, D_MODEL), 1.0),
        "meta_tokens": nrm(ks[1], (N_META, D_MODEL), 1.0),
        "lb_logits": nrm(ks[2], (DEPTH + 1, A_FDIM), 1.0),
        "norm1_g": 1.0 + nrm(ks[3], (L, D_MODEL), 0.05),
        "w_in": nrm(ks[4], (L, D_MODEL, IN_COLS), D_MODEL ** -0.5),
        "b_f": nrm(ks[5], (L, A_FDIM), 0.1),
        "head_norm_g": 1.0 + nrm(ks[6], (L, A_WIDTH), 0.05),
        "w_pool": nrm(ks[7], (L, B_GROUPS, B_GDIM, B_GDIM), B_GDIM ** -0.5),
        "pool_scale": 1.0 + nrm(ks[8], (L, B_WIDTH), 0.1),
        "w_branch_a": nrm(ks[9], (L, A_WIDTH, D_MODEL), A_WIDTH ** -0.5),
        "w_branch_b": nrm(ks[10], (L, B_WIDTH, D_MODEL), B_WIDTH ** -0.5),
        "w_out": nrm(ks[11], (L, D_MODEL, D_MODEL), D_MODEL ** -0.5),
        "norm2_g": 1.0 + nrm(ks[12], (L, D_MODEL), 0.05),
        "w_up": nrm(ks[13], (L, D_MODEL, 2 * D_FF), D_MODEL ** -0.5),
        "conv_w": nrm(ks[14], (L, CONV_W, D_FF), CONV_W ** -0.5),
        "conv_b": nrm(ks[15], (L, D_FF), 0.01),
        "w_down": nrm(ks[16], (L, D_FF, D_MODEL), D_FF ** -0.5),
        "final_norm_g": 1.0 + nrm(ks[17], (D_MODEL,), 0.05),
    }

def first_block(x, meta_tokens, lb_logits, norm1_g, w_in, b_f, head_norm_g, w_pool, pool_scale,
              w_branch_a, w_branch_b, w_out, norm2_g, w_up, conv_w, conv_b, w_down, final_norm_g):
    B_ = x.shape[0]
    meta = jnp.broadcast_to(meta_tokens.astype(x.dtype)[None], (B_, N_META, D_MODEL))
    h = jnp.concatenate([meta, x], axis=1)
    lb_all = jnp.cumsum(jax.nn.softmax(lb_logits.astype(jnp.float32), axis=0), axis=0)
    for l in range(DEPTH):
        z = rmsnorm(h, norm1_g[l])
        proj = z @ w_in[l]
        q, fl, iv, og, pin, ga, gb = jnp.split(proj, SPLITS, axis=-1)
        o_a = hgrn2_mixer(q, fl + b_f[l], iv, og, lb_all[l], head_norm_g[l])
        o_b = pool_mixer(pin, w_pool[l], pool_scale[l])
        mix = jax.nn.sigmoid(ga) * (o_a @ w_branch_a[l]) + jax.nn.sigmoid(gb) * (o_b @ w_branch_b[l])
        h = h + mix @ w_out[l]
        z = rmsnorm(h, norm2_g[l])
        u, v = jnp.split(z @ w_up[l], 2, axis=-1)
        u = causal_dwconv(u, conv_w[l], conv_b[l])
        h = h + (jax.nn.silu(u) * v) @ w_down[l]
    h = rmsnorm(h, final_norm_g)
    return h[:, N_META:]


BLOCK_Q = 128
RMS_EPS = 1e-6

MLA_HEADS = 16
MLA_Q_RANK = 256
MLA_KV_RANK = 128
MLA_NOPE_DIM = 64
MLA_ROPE_DIM = 32
MLA_V_DIM = 64
MLA_WIDTH = MLA_HEADS * MLA_V_DIM
MLA_SCALE = 1.0 / math.sqrt(MLA_NOPE_DIM + MLA_ROPE_DIM)
ROPE_THETA = 10000.0

FOX_HEADS = 16
FOX_HEAD_DIM = 64
FOX_WIDTH = FOX_HEADS * FOX_HEAD_DIM
FOX_SCALE = 1.0 / math.sqrt(FOX_HEAD_DIM)

IN_SPLITS = (MLA_Q_RANK, MLA_KV_RANK, MLA_ROPE_DIM, MLA_WIDTH,
             FOX_WIDTH, FOX_WIDTH, FOX_WIDTH, FOX_HEADS, FOX_WIDTH,
             D_MODEL, D_MODEL)
IN_WIDTH = sum(IN_SPLITS)


def rmsnorm_2(x, g):
    xf = x.astype(jnp.float32)
    y = xf * lax.rsqrt(jnp.mean(xf * xf, axis=-1, keepdims=True) + RMS_EPS)
    return (y * g.astype(jnp.float32)).astype(x.dtype)

def rope(x, pos):
    half = x.shape[-1] // 2
    inv_freq = ROPE_THETA ** (-jnp.arange(half, dtype=jnp.float32) / half)
    ang = pos.astype(jnp.float32)[:, None] * inv_freq[None, :]
    cos, sin = jnp.cos(ang), jnp.sin(ang)
    x1 = x[..., :half].astype(jnp.float32)
    x2 = x[..., half:].astype(jnp.float32)
    return jnp.concatenate([x1 * cos - x2 * sin, x1 * sin + x2 * cos], axis=-1).astype(x.dtype)

def causal_block_attention(q, k, v, scale, cum=None):
    B, H, L, _ = q.shape
    n_real = L - N_META
    nb = n_real // BLOCK_Q
    key_pos = jnp.arange(L)

    def attend(qb, qpos, cq=None):
        s = jnp.einsum('bhqd,bhkd->bhqk', qb, k, preferred_element_type=jnp.float32) * scale
        if cq is not None:
            s = s + (cq[..., :, None] - cum[:, :, None, :])
        s = jnp.where(key_pos[None, :] <= qpos[:, None], s, -jnp.inf)
        p = jax.nn.softmax(s, axis=-1)
        return jnp.einsum('bhqk,bhkd->bhqd', p.astype(v.dtype), v)

    out_meta = attend(q[:, :, :N_META], key_pos[:N_META],
                      None if cum is None else cum[:, :, :N_META])

    def to_blocks(a):
        a = a[:, :, N_META:]
        a = a.reshape((B, H, nb, BLOCK_Q) + a.shape[3:])
        return jnp.moveaxis(a, 2, 0)

    xs = (to_blocks(q), key_pos[N_META:].reshape(nb, BLOCK_Q))
    if cum is not None:
        xs = xs + (to_blocks(cum),)
    out_real = lax.map(lambda args: attend(*args), xs)
    out_real = jnp.moveaxis(out_real, 0, 2).reshape(B, H, n_real, v.shape[-1])
    return jnp.concatenate([out_meta, out_real], axis=2)

def second_inputs(seed: int = 0) -> dict:
    key = jax.random.key(seed)
    ks = jax.random.split(key, 13)
    f32 = jnp.float32

    def gain(k, n):
        return 1.0 + 0.1 * jax.random.normal(k, (DEPTH, n), f32)

    def dense(k, fan_in, fan_out):
        return jax.random.normal(k, (DEPTH, fan_in, fan_out), f32) * fan_in ** -0.5

    return {
        'x': jax.random.normal(ks[0], (BATCH, SEQ, D_MODEL), f32),
        'meta_tokens': jax.random.normal(ks[1], (N_META, D_MODEL), f32),
        'pre_norm_g': gain(ks[2], D_MODEL),
        'w_in': dense(ks[3], D_MODEL, IN_WIDTH),
        'fox_forget_b': jax.random.uniform(ks[4], (DEPTH, FOX_HEADS), f32, 1.0, 4.0),
        'mla_q_norm_g': gain(ks[5], MLA_Q_RANK),
        'mla_kv_norm_g': gain(ks[6], MLA_KV_RANK),
        'w_uq': dense(ks[7], MLA_Q_RANK, MLA_HEADS * (MLA_NOPE_DIM + MLA_ROPE_DIM)),
        'w_ukv': dense(ks[8], MLA_KV_RANK, MLA_HEADS * (MLA_NOPE_DIM + MLA_V_DIM)),
        'w_br_mla': dense(ks[9], MLA_WIDTH, D_MODEL),
        'w_br_fox': dense(ks[10], FOX_WIDTH, D_MODEL),
        'w_out': dense(ks[11], D_MODEL, D_MODEL),
        'post_norm_g': gain(ks[12], D_MODEL),
    }

def second_block(x, meta_tokens, pre_norm_g, w_in, fox_forget_b, mla_q_norm_g, mla_kv_norm_g,
              w_uq, w_ukv, w_br_mla, w_br_fox, w_out, post_norm_g):
    B, S, D = x.shape
    L = S + N_META
    pos = jnp.arange(L)
    h = jnp.concatenate([jnp.broadcast_to(meta_tokens[None].astype(x.dtype), (B, N_META, D)), x], axis=1)
    split_idx = np.cumsum(IN_SPLITS)[:-1].tolist()

    def fox_heads(t):
        return t.reshape(B, L, FOX_HEADS, FOX_HEAD_DIM).transpose(0, 2, 1, 3)

    for l in range(DEPTH):
        u = rmsnorm_2(h, pre_norm_g[l])
        proj = u @ w_in[l]
        (cq, ckv, k_pe_raw, z_mla, fq, fk, fv, f_logit, z_fox, gate_a, gate_b) = jnp.split(proj, split_idx, axis=-1)

        q = (rmsnorm_2(cq, mla_q_norm_g[l]) @ w_uq[l]).reshape(B, L, MLA_HEADS, MLA_NOPE_DIM + MLA_ROPE_DIM).transpose(0, 2, 1, 3)
        kv = (rmsnorm_2(ckv, mla_kv_norm_g[l]) @ w_ukv[l]).reshape(B, L, MLA_HEADS, MLA_NOPE_DIM + MLA_V_DIM).transpose(0, 2, 1, 3)
        q_nope, q_pe = q[..., :MLA_NOPE_DIM], q[..., MLA_NOPE_DIM:]
        k_nope, v_mla = kv[..., :MLA_NOPE_DIM], kv[..., MLA_NOPE_DIM:]
        k_pe = rope(k_pe_raw, pos)[:, None]
        q_m = jnp.concatenate([q_nope, rope(q_pe, pos)], axis=-1)
        k_m = jnp.concatenate([k_nope, jnp.broadcast_to(k_pe, (B, MLA_HEADS, L, MLA_ROPE_DIM))], axis=-1)
        o_mla = causal_block_attention(q_m, k_m, v_mla, MLA_SCALE)
        o_mla = o_mla.transpose(0, 2, 1, 3).reshape(B, L, MLA_WIDTH)
        y_mla = (o_mla * jax.nn.silu(z_mla)) @ w_br_mla[l]

        log_f = jax.nn.log_sigmoid((f_logit + fox_forget_b[l]).astype(jnp.float32)).transpose(0, 2, 1)
        cum = jnp.cumsum(log_f, axis=-1)
        o_fox = causal_block_attention(fox_heads(fq), fox_heads(fk), fox_heads(fv), FOX_SCALE, cum)
        o_fox = o_fox.transpose(0, 2, 1, 3).reshape(B, L, FOX_WIDTH)
        y_fox = (o_fox * jax.nn.silu(z_fox)) @ w_br_fox[l]

        mixed = (jax.nn.sigmoid(gate_a) * y_mla + jax.nn.sigmoid(gate_b) * y_fox) @ w_out[l]
        h = h + rmsnorm_2(mixed, post_norm_g[l])

    return h[:, N_META:]


def setup_inputs(seed=0):
    out = dict(first_inputs(seed))
    for name, value in second_inputs(seed + 1).items():
        if name != "x":
            out[name + "_2"] = value
    return out


def reference(
    x, meta_tokens, lb_logits, norm1_g, w_in, b_f, head_norm_g, w_pool, pool_scale, w_branch_a,
    w_branch_b, w_out, norm2_g, w_up, conv_w, conv_b, w_down, final_norm_g, meta_tokens_2,
    pre_norm_g_2, w_in_2, fox_forget_b_2, mla_q_norm_g_2, mla_kv_norm_g_2, w_uq_2, w_ukv_2,
    w_br_mla_2, w_br_fox_2, w_out_2, post_norm_g_2,
):
    x = first_block(
        x, meta_tokens, lb_logits, norm1_g, w_in, b_f, head_norm_g, w_pool, pool_scale,
        w_branch_a, w_branch_b, w_out, norm2_g, w_up, conv_w, conv_b, w_down, final_norm_g,
    )
    return second_block(
        x, meta_tokens_2, pre_norm_g_2, w_in_2, fox_forget_b_2, mla_q_norm_g_2, mla_kv_norm_g_2,
        w_uq_2, w_ukv_2, w_br_mla_2, w_br_fox_2, w_out_2, post_norm_g_2,
    )


_drawn_inputs = setup_inputs


def setup_inputs(seed=0):
    import zlib

    import numpy as np

    out = dict(_drawn_inputs(seed))
    spreads = {}
    factors = {'b_f': 8.0, 'conv_b': 7.901}
    for name, (base, spread) in spreads.items():
        noise = np.random.default_rng([zlib.crc32(name.encode()), seed]).standard_normal(out[name].shape)
        drawn = base * np.exp(spread * noise) if base else spread * noise
        out[name] = __import__('jax').numpy.asarray(drawn.astype(out[name].dtype))
    for name, factor in factors.items():
        out[name] = (out[name] * factor).astype(out[name].dtype)
    return out
```

```python
from contextlib import ExitStack

import numpy as np

import concourse.bass as bass
from concourse import mybir

F32 = mybir.dt.float32
F32R = mybir.dt.float32r
BF16 = mybir.dt.bfloat16
U8 = mybir.dt.uint8
ALU = mybir.AluOpType
ACT = mybir.ActivationFunctionType
AX = mybir.AxisListType

P = 128
D = 1024
KT = D // P
NM = 16
SEQ = 512
T = NM + SEQ
HALF = T // 2
EPS = 1e-6

A_HEADS = 8
A_VDIM = 64
D_FF = 2816
FT = D_FF // P
POOL_WINDOWS = (2, 4, 8, 16)
PADC = 16
CH = 128
NCH = SEQ // CH
LEVELS = 7
MASKC = 64 * (LEVELS + 1)

HEADS = 16
ROPE = 32
NOPE = 64
QW = NOPE + ROPE
DV = 64
QB = SEQ // P
MLA_SCALE = 1.0 / float(np.sqrt(QW))
FOX_SCALE = 1.0 / 8.0
NEG = -1.0e30

A_Q, A_F, A_V, A_OG, B_IN, G_A, G_B = 0, 1024, 2048, 2560, 3072, 3584, 4608
M_CQ, M_CKV, M_KPE, M_Z, X_Q, X_K, X_V, X_F, X_Z, H_A, H_B = (
    0, 256, 384, 416, 1440, 2464, 3488, 4512, 4528, 5552, 6576)

ROWS = {}
for _name, _n in (("norm1", 8), ("lb0", 8), ("lb1", 8), ("bf", 8), ("head", 4), ("pscale", 4), ("norm2", 8),
                  ("final", 8), ("pre", 8), ("qn", 2), ("kvn", 1)):
    ROWS[_name] = (sum(n for _, n in ROWS.values()), _n)
NROW1 = sum(n for _, n in ROWS.values())
ROWS["convw"] = (P, 3 * FT)
ROWS["convb"] = (P + 3 * FT, FT)
NROW2 = 4 * FT


def host_constants():
    s = np.arange(P)[:, None]
    mask = np.zeros((P, MASKC), np.float32)
    for j in range(LEVELS):
        half = 1 << j
        n, b = np.divmod(np.arange(64), half)
        mask[:, 64 * j:64 * j + 64] = (s // (2 * half) == n[None]) & (s % (2 * half) < half)
    mask[:, 64 * LEVELS:] = s % 64 == np.arange(64)[None]
    pos = np.arange(T, dtype=np.float32)
    half = ROPE // 2
    freq = np.float32(10000.0) ** (-np.arange(half, dtype=np.float32) / np.float32(half))
    ang = (pos[None, :] * freq[:, None].astype(np.float32)).astype(np.float64)
    cos, sin = np.cos(ang).astype(np.float32), np.sin(ang).astype(np.float32)
    trig = np.ones((P, 3, T), np.float32)
    trig[64:96, 0] = np.concatenate([cos, cos])
    trig[96:128, 0] = np.concatenate([-sin, sin])
    trig[64:128, 1] = np.concatenate([cos, cos, cos, cos])
    trig[64:128, 2] = np.concatenate([-sin, sin, -sin, sin])
    inv = np.ones((P, PADC), np.float32)
    inv[:] = 1.0 / np.arange(1, PADC + 1, dtype=np.float32)
    causal = np.where(np.arange(P)[None] > np.arange(P)[:, None], np.float32(NEG), np.float32(0.0))
    e = np.zeros((P, HEADS), np.float32)
    for h in range(HEADS):
        e[h, h] = e[32 + h, h] = 1.0
    return {"c_level": mask, "c_trig": trig, "c_inv": inv, "c_causal": causal.astype(np.float32), "c_pick": e}


class Piece:

    def __init__(self, unit, col, kt, x, k0, mode, slot, first, last, name):
        self.unit, self.col, self.kt, self.x, self.k0 = unit, col, kt, x, k0
        self.mode, self.slot, self.first, self.last, self.name = mode, slot, first, last, name


class Plan:

    def __init__(self):
        self.units = []
        self.pieces = []
        self.tile = {}
        self.unit_end = []
        self.uses = [0, 0]

    def unit(self, parts, kt, cols):
        self.units.append((parts, kt, cols))
        self.unit_end.append(0)
        return len(self.units) - 1

    def piece(self, name, unit, col, kt, x, mode="full", slot=0, k0=0, first=True, last=True):
        if first:
            self.tile[name] = [slot, 0, self.uses[slot]]
            self.uses[slot] += 1
        self.pieces.append(Piece(unit, col, kt, x, k0, mode, slot, first, last, name))
        self.tile[name][1] = len(self.pieces)
        self.unit_end[unit] = len(self.pieces)


def make_plan():
    pl = Plan()
    n = 0

    def two(names, w, col0, x, kt=KT, mode="full"):
        nonlocal n
        u = pl.unit([(w, 0, col0, 256, 0)], kt, 256)
        for i, name in enumerate(names):
            pl.piece(name, u, 128 * i, kt, x, mode, slot=n % 2)
            n += 1

    for j in range(2):
        two([("v", 2 * j), ("v", 2 * j + 1)], "w_in", A_V + 256 * j, "z")
    for p in range(4):
        two([("q", 2 * p), ("q", 2 * p + 1)], "w_in", A_Q + 256 * p, "z")
        two([("f", 2 * p), ("f", 2 * p + 1)], "w_in", A_F + 256 * p, "z")
    for j in range(2):
        two([("og", 2 * j), ("og", 2 * j + 1)], "w_in", A_OG + 256 * j, "z")
    for j in range(2):
        two([("pin", 2 * j), ("pin", 2 * j + 1)], "w_in", B_IN + 256 * j, "z")
    pl.pool_unit = pl.unit([("w_pool", 0, 0, 512, 0)], 1, 512)
    for g in range(4):
        pl.piece(("pool", g), pl.pool_unit, 128 * g, 1, "pd", "full", slot=n % 2, k0=g)
        n += 1
    for b, (gc, w, x) in enumerate(((G_B, "w_branch_b", "ob"), (G_A, "w_branch_a", "oa"))):
        for j in range(4):
            two([("g", b, 2 * j), ("g", b, 2 * j + 1)], "w_in", gc + 256 * j, "z")
            two([("y", b, 2 * j), ("y", b, 2 * j + 1)], w, 256 * j, x, kt=4)
    for j in range(4):
        two([("out", 2 * j), ("out", 2 * j + 1)], "w_out", 256 * j, "z")
    for j in range(FT // 2):
        two([("u", 2 * j), ("u", 2 * j + 1)], "w_up", 256 * j, "z")
        two([("vv", 2 * j), ("vv", 2 * j + 1)], "w_up", D_FF + 256 * j, "z", mode="real")
    for j in range(4):
        for i, (k0, kt) in enumerate(((0, 8), (8, 8), (16, 6))):
            u = pl.unit([("w_down", k0 * P, 256 * j, 256, 0)], kt, 256)
            for m in range(2):
                pl.piece(("dn", 2 * j + m), u, 128 * m, kt, "g", "real", slot=m, k0=k0, first=i == 0, last=i == 2)
    n = 0
    two([("cq", 0), ("cq", 1)], "w_in_2", M_CQ, "z")
    u = pl.unit([("w_in_2", 0, M_CKV, 128, 0)], KT, 128)
    pl.piece(("ckv", 0), u, 0, KT, "z", "full", slot=n % 2)
    n += 1
    h = ROPE // 2
    parts = []
    for c in (0, 128):
        parts.append(("w_in_2", 0, X_F, 64, c))
    for c in (64, 96):
        parts.append(("w_in_2", 0, M_KPE, 32, c))
    for c in (192, 224):
        parts.append(("w_in_2", 0, M_KPE + h, h, c))
        parts.append(("w_in_2", 0, M_KPE, h, c + h))
    u = pl.unit(parts, KT, 256)
    for i in range(2):
        pl.piece(("kpe", i), u, 128 * i, KT, "z", "full", slot=n % 2)
        n += 1
    pl.uq = [pl.unit([("w_uq", 8 * i)], 2, 1024) for i in range(1)]
    pl.ukv = pl.unit([("w_ukv_2", 0, 0, 2048, 0)], 1, 2048)
    pl.uq.append(pl.unit([("w_uq", 8)], 2, 1024))
    for i in range(5):
        for j in range(2):
            pl.piece(("mv", i, j), pl.ukv, j, 1, "ckv", "values", slot=j, k0=i)
    for hd in range(HEADS):
        pl.piece(("mq", hd), pl.uq[hd // 8], 128 * (hd % 8), 2, "cq", "real", slot=0)
        pl.piece(("mk", hd), pl.ukv, 128 * hd, 1, "ckv", "full", slot=0)
    n = 0
    for j in range(4):
        two([("mz", 2 * j), ("mz", 2 * j + 1)], "w_in_2", M_Z + 256 * j, "z", mode="real")
    for j in range(4):
        two([("hg", 0, 2 * j), ("hg", 0, 2 * j + 1)], "w_in_2", H_A + 256 * j, "z", mode="real")
        two([("hy", 0, 2 * j), ("hy", 0, 2 * j + 1)], "w_br_mla_2", 256 * j, "y", mode="real512")
    for j in range(4):
        two([("xv", 2 * j), ("xv", 2 * j + 1)], "w_in_2", X_V + 256 * j, "z")
    for j in range(4):
        u1 = pl.unit([("w_in_2", 0, X_Q + 256 * j, 256, 0)], KT, 256)
        u2 = pl.unit([("w_in_2", 0, X_K + 256 * j, 256, 0)], KT, 256)
        for m in range(2):
            pl.piece(("xq", 2 * j + m), u1, 128 * m, KT, "z", "real", slot=0)
        for m in range(2):
            pl.piece(("xk", 2 * j + m), u2, 128 * m, KT, "z", "full", slot=0)
    n = 0
    for j in range(4):
        two([("xz", 2 * j), ("xz", 2 * j + 1)], "w_in_2", X_Z + 256 * j, "z", mode="real")
    for j in range(4):
        two([("hg", 1, 2 * j), ("hg", 1, 2 * j + 1)], "w_in_2", H_B + 256 * j, "z", mode="real")
        two([("hy", 1, 2 * j), ("hy", 1, 2 * j + 1)], "w_br_fox_2", 256 * j, "y", mode="real512")
    for j in range(4):
        u = pl.unit([("w_out_2", 0, 256 * j, 256, 0)], KT, 256)
        for i in range(QB):
            pl.piece(("fin", j, i), u, 0, KT, "mx", "tokens", slot=n % 2, k0=i)
            n += 1
    return pl


def build_program(nc: bass.Bass, a, out):
    pl = make_plan()
    NU = len(pl.units)
    ctx = ExitStack()
    with ctx:
        def at(name, shape, dt, offset):
            size = int(np.prod(shape[1:])) * {F32: 4, F32R: 4, BF16: 2, U8: 1}[dt]
            return nc.alloc_sbuf_tensor_at(name, shape, dt, offset=offset), offset + size

        def sem(name):
            return ctx.enter_context(nc.semaphore(name))

        o = 16512
        raw, hi, lo = [], [], []
        for i in range(2):
            t, o = at(f"raw{i}", [P, 2048], F32, o)
            raw.append(t)
        for i in range(2):
            t, o = at(f"whi{i}", [P, 2048], F32R, o)
            hi.append(t)
        for i in range(2):
            t, o = at(f"wlo{i}", [P, 2048], F32R, o)
            lo.append(t)
        prm, o = at("prm", [P, 256], F32, o)
        ident, o = at("ident", [P, P], F32, o)
        ones, o = at("ones", [P, P], F32, o)
        pair1, o = at("pair1", [P, P], F32, o)
        identb, o = at("identb", [P, P], BF16, o)
        causalb, o = at("causalb", [P, P], BF16, o)
        small, o = at("small", [P, 128], F32, o)
        inv_n, o = at("inv_n", [P, PADC], F32, o)
        pick, o = at("pick", [P, HEADS], F32R, o)
        lvl, o = at("lvl", [P, MASKC], U8, o)
        A = (o + 31) // 32 * 32
        B = A + KT * T * 4
        C = B + 2 * KT * T * 4

        hT, _ = at("hT", [P, KT, T], F32, A)
        mix, _ = at("mix", [P, KT, T], F32, A)
        omla, _ = at("omla", [P, KT, SEQ], F32, A)
        zhi, e = at("zhi", [P, KT, T], F32R, B)
        zlo, _ = at("zlo", [P, KT, T], F32R, e)
        xt, e = at("xt", [P, QB, D], F32, C)
        xm, e = at("xm", [NM, D], F32, e)
        prow, e = at("prow", [P, 2, P], F32, e)
        sq = [None, None]
        sq[0], e = at("sq0", [P, T], F32, e)
        sq[1], e = at("sq1", [P, T], F32, e)
        zt = [None, None]
        zt[0], e = at("zt0", [P, T], F32, e)
        zt[1], e = at("zt1", [P, T], F32, e)
        rb, e = at("rb", [P, T], F32, e)
        cstage, e = at("cstage", [P, P + HEADS + MASKC], F32, e)
        NORM_END = e
        vtok1, e = at("vtok1", [P, 5, 512], F32, C)
        qf = [at(f"qf{i}", [P, 2, T], F32, e + i * 2 * T * 4)[0] for i in range(2)]
        e += 4 * T * 4
        kf = [at(f"kf{i}", [P, 2, T], F32, e + i * 2 * T * 4)[0] for i in range(2)]
        e += 4 * T * 4
        av = [at(f"av{i}", [P, 2, T], F32, e + i * 2 * T * 4)[0] for i in range(2)]
        AVOFF = e
        e += 4 * T * 4
        E = [at(f"E{i}", [P, 2, T], F32, e + i * 2 * T * 4)[0] for i in range(2)]
        e += 4 * T * 4
        rmask, e = at("rmask", [P, T], F32, e)
        og, e = at("og", [P, 4, T], F32, e)
        pin, e = at("pin", [P, 4, T + PADC], F32, e)
        obhi, e = at("obhi", [P, 4, T], F32R, e)
        oblo, e = at("oblo", [P, 4, T], F32R, e)
        oT, e = at("oT", [P, 4, T], F32, e)
        Sc, e = at("Sc", [P, 2, 4, DV], F32, e)
        scT, e = at("scT", [P, 8, P], F32, e)
        sc0, e = at("sc0", [NM, 2, NM], F32, e)
        kdt, e = at("kdt", [P, 2, 4, P], F32, e)
        GOFF = e
        gbuf = [at(f"gbuf{i}", [P, T], F32, GOFF + i * T * 4)[0] for i in range(2)]
        tmp = [at(f"tmp{i}", [P, T], F32, GOFF + (2 + i) * T * 4)[0] for i in range(2)]
        pp = [at(f"pp{i}", [P, T + PADC], F32, GOFF + i * (T + PADC) * 4)[0] for i in range(2)]
        P1_END = GOFF + 4 * T * 4 + 256
        assert P1_END <= nc.sbuf_usable_end, (P1_END, nc.sbuf_usable_end)
        pdhi, _ = at("pdhi", [P, T], F32R, GOFF + 2 * (T + PADC) * 4)
        pdlo, _ = at("pdlo", [P, T], F32R, GOFF + (3 * T + 2 * PADC) * 4)
        assert GOFF + (4 * T + 2 * PADC) * 4 <= P1_END
        oahi, e2 = at("oahi", [P, 4, T], F32R, C + 10240)
        oalo, e2 = at("oalo", [P, 4, T], F32R, e2)
        hT2, _ = at("hT2", [P, KT, T], F32, AVOFF)
        ghi, e = at("ghi", [P, FT, SEQ], F32R, C)
        glo, e = at("glo", [P, FT, SEQ], F32R, e)
        ub = [at(f"ub{i}", [P, T], F32, e + i * T * 4)[0] for i in range(2)]
        e += 2 * T * 4
        cb = [at(f"cb{i}", [P, SEQ], F32, e + i * SEQ * 4)[0] for i in range(2)]
        e += 2 * SEQ * 4
        gt = [at(f"gt{i}", [P, SEQ], F32, e + i * SEQ * 4)[0] for i in range(2)]
        e += 2 * SEQ * 4
        assert e <= nc.sbuf_usable_end, e
        N0 = C + 97728
        nsq = [at(f"nsq{i}", [P, T], F32, N0 + i * T * 4)[0] for i in range(2)]
        nzt = [at(f"nzt{i}", [P, T], F32, N0 + (2 + i) * T * 4)[0] for i in range(2)]
        nrb, e = at("nrb", [P, T], F32, N0 + 4 * T * 4)
        assert e <= nc.sbuf_usable_end, e
        htok, e = at("htok", [P, QB, D], F32, C)
        vtok, e = at("vtok", [P, 5, D], F32, e)
        YOFF = e
        Pm = [at(f"Pm{i}", [P, 1344], F32, e + i * 1344 * 4)[0] for i in range(2)]
        e += 2 * 1344 * 4
        PT = [at(f"PT{i}", [P, 14 * P], F32, e + i * 14 * P * 4)[0] for i in range(2)]
        e += 2 * 14 * P * 4
        cqhi, e = at("cqhi", [P, 2, T], F32R, e)
        cqlo, e = at("cqlo", [P, 2, T], F32R, e)
        ckhi, e = at("ckhi", [P, T], F32R, e)
        cklo, e = at("cklo", [P, T], F32R, e)
        qh = [at(f"qh{i}", [P, SEQ], F32, e + i * SEQ * 4)[0] for i in range(2)]
        e += 2 * SEQ * 4
        kh = [at(f"kh{i}", [P, T], F32, e + i * T * 4)[0] for i in range(2)]
        e += 2 * T * 4
        trig, e = at("trig", [P, 3, T], F32, e)
        cqT, e = at("cqT", [P, 3, T], F32, e)
        nch, e = at("nch", [P, T], F32R, e)
        fgt, _ = at("fgt", [64, 2, T], F32, YOFF)
        assert e <= N0, (e, N0)
        yhi, e = at("yhi", [P, KT, SEQ], F32R, YOFF)
        ylo, e = at("ylo", [P, KT, SEQ], F32R, e)
        MIXOFF = e
        mix2, e = at("mix2", [P, KT, SEQ], F32, e)
        fq, e = at("fq", [P, 2, SEQ], F32, e)
        fk, e = at("fk", [P, 2, T], F32, e)
        assert e <= C + 95616, e - C
        mtok, _ = at("mtok", [P, QB, D], F32, C + 16384)
        fjunk, _ = at("fjunk", [P, D], F32, YOFF + 4 * D)
        gpost, _ = at("gpost", [P, D], F32, YOFF)

        PS = ctx.enter_context(nc.psum_tensor("PS", [P, 8, 512], F32))
        el = small[:, 0:8].rearrange("p (h c) -> p h c", h=2)
        lb, omlb, lbe, epst, fbias = small[:, 8:16], small[:, 16:24], small[:, 24:40], small[:, 40:41], small[:, 41:42]
        negmax, rowsum, rinv, ssum, lbt = small[:, 48:56], small[:, 56:64], small[:, 64:68], small[:, 72:76], small[:, 80:96]

        def col(name, k):
            r = ROWS[name][0]
            return prm[:, r + k:r + k + 1]

        w_landed = [sem(f"w_landed{i}") for i in range(2)]
        w_split = sem("w_split")
        pe_mark = sem("pe_mark")
        acc_free = [sem(f"acc_free{i}") for i in range(2)]
        act_step, dve_step = sem("act_step"), sem("dve_step")
        x_in, prm_in, const_in, late_in = sem("x_in"), sem("prm_in"), sem("const_in"), sem("late_in")
        const_ready, prm_turned, prm_ready = sem("const_ready"), sem("prm_turned"), sem("prm_ready")
        x_turned, h_copied = sem("x_turned"), sem("h_copied")
        lb_sub, lb_exp, lb_ready = sem("lb_sub"), sem("lb_exp"), sem("lb_ready")
        v_turned, v_copied = sem("v_turned"), sem("v_copied")
        f_ready, ln_ready, a_ready = sem("f_ready"), sem("ln_ready"), sem("a_ready")
        sub_ready, exp_ready, mul_ready = sem("sub_ready"), sem("exp_ready"), sem("mul_ready")
        qd_exp, qd_ready = sem("qd_exp"), sem("qd_ready")
        kd_turned, kdt_ready, upd_done, s_ready = sem("kd_turned"), sem("kdt_ready"), sem("upd_done"), sem("s_ready")
        sc_done, sc_copied, c0_copied = sem("sc_done"), sem("sc_copied"), sem("c0_copied")
        o_done, o_copied = sem("o_done"), sem("o_copied")
        pd_ready, obhi_ready = sem("pd_ready"), sem("obhi_ready")
        osq, ossd, orn, on_ready, oahi_ready, oa_ready = (sem("osq"), sem("ossd"), sem("orn"), sem("on_ready"),
                                                          sem("oahi_ready"), sem("oa_ready"))
        spilled, h_back = sem("spilled"), sem("h_back")
        mix_ready, mix2_ready = sem("mix_ready"), sem("mix2_ready")
        mixhi_ready, mixz_ready = sem("mixhi_ready"), sem("mixz_ready")
        c_ready, silu_ready, ghi_ready, g_ready = sem("c_ready"), sem("silu_ready"), sem("ghi_ready"), sem("g_ready")
        h1_ready, meta_turned, h1_meta = sem("h1_ready"), sem("meta_turned"), sem("h1_meta")
        ht_turned, ht_copied = sem("ht_turned"), sem("ht_copied")
        fl_ready, fl_abs, cum_ready, kr_ready = sem("fl_ready"), sem("fl_abs"), sem("cum_ready"), sem("kr_ready")
        xv_turned, xv_copied = sem("xv_turned"), sem("xv_copied")
        ysilu, ygt, yhi_r, y_ready = sem("ysilu"), sem("ygt"), sem("yhi_r"), sem("y_ready")
        fmixhi, fmix = sem("fmixhi"), sem("fmix")
        fin_rstd, fin_out, out_done = sem("fin_rstd"), sem("fin_out"), sem("out_done")

        class Norm:

            def __init__(self, name, src, K, n, width, sqb, ztb, rbb, gain, dst, lhs=None):
                self.src, self.K, self.n, self.width = src, K, n, width
                self.sqb, self.ztb, self.rbb, self.gain, self.dst = sqb, ztb, rbb, gain, dst
                self.lhs = lhs
                self.sq_ready, self.sq_used = sem(name + "_sq"), sem(name + "_sqd")
                self.rb_ready, self.zt_ready = sem(name + "_rb"), sem(name + "_zt")
                self.zhi_ready, self.z_ready = sem(name + "_zhi"), sem(name + "_z")

        zpair = lambda k: (zhi[:, k, :], zlo[:, k, :])
        h_src = lambda k: hT[:, k, :]
        norm1 = Norm("n1", h_src, KT, T, D, sq, zt, rb, "norm1", zpair)
        norm2 = Norm("n2", h_src, KT, T, D, nsq, nzt, nrb, "norm2", zpair)
        normf = Norm("nf", h_src, KT, T, D, nsq, nzt, nrb, "final", None)
        normp = Norm("np", h_src, KT, T, D, nsq, nzt, nrb, "pre", zpair)
        normq = Norm("nq", lambda k: cqT[:, k, :], 2, T, 256, nsq, nzt, nrb, "qn",
                     lambda k: (cqhi[:, k, :], cqlo[:, k, :]))
        normk = Norm("nk", lambda k: cqT[:, 2, :], 1, T, 128, nsq, nzt, nrb, "kvn", lambda k: (ckhi[:, :], cklo[:, :]))

        class Attn:
            def __init__(self, name):
                self.s_done, self.m_ready = sem(name + "s_done"), sem(name + "m_ready")
                self.p_exp, self.p_ready = sem(name + "p_exp"), sem(name + "p_ready")
                self.g_turned, self.pt_a, self.pt_v = sem(name + "g_turned"), sem(name + "pt_a"), sem(name + "pt_v")
                self.o_done, self.o_ready = sem(name + "o_done"), sem(name + "o_ready")

        mla, fox = Attn("mla_"), Attn("fox_")
        hspill = nc.dram_tensor("hspill", [P, KT * T], F32, kind="Internal").ap()

        def acc_full(name, rows=slice(0, P)):
            s = 2 * pl.tile[name][0]
            return PS[rows, s:s + 2, 0:HALF]

        def acc_real(name, rows=slice(0, P), n=SEQ):
            return PS[rows, 2 * pl.tile[name][0], 0:n]

        def halves(t):
            return t.rearrange("p (a b) -> p a b", a=2)

        def tile_done(eng, name):
            eng.wait_ge(pe_mark, pl.tile[name][1])

        def tile_free(ins, name):
            ins.then_inc(acc_free[pl.tile[name][0]], 1)

        def tile_freed(eng, name):
            slot, _, uses = pl.tile[name]
            eng.wait_ge(acc_free[slot], uses + 1)

        def chunk(c):
            return (0, NM) if c == 0 else (NM + CH * (c - 1), CH)

        STEPS = {0: (0, 1), 1: (2, 3, 4), 2: (5, 6), 3: (7, 8, 9)}
        order = [(("v", j), []) for j in range(4)]
        names = [("q", 0), ("q", 1), ("f", 0), ("f", 1)]
        order += [(n, []) for n in names]
        for p in range(1, 4):
            for i, n in enumerate((("q", 2 * p), ("q", 2 * p + 1), ("f", 2 * p), ("f", 2 * p + 1))):
                order.append((n, [(p - 1, s) for s in STEPS[i]]))
        for i in range(4):
            order.append((("og", i), [(3, s) for s in STEPS[i]]))
        order += [(("pin", j), []) for j in range(4)]

        ROW_LOADS = (("norm1_g", 0, "norm1"), ("lb_logits", 0, "lb0"), ("b_f", 0, "bf"), ("head_norm_g", 0, "head"),
                     ("pool_scale", 0, "pscale"), ("norm2_g", 0, "norm2"), ("final_norm_g", 0, "final"),
                     ("pre_norm_g_2", 0, "pre"), ("mla_q_norm_g_2", 0, "qn"), ("mla_kv_norm_g_2", 0, "kvn"),
                     ("conv_w", 1, "convw"), ("conv_b", 1, "convb"))
        PRM_DMAS = 16 * len(ROW_LOADS)

        def level_views(t, j):
            half, blk = 1 << j, 2 << j
            if blk <= NM:
                v = t.rearrange("p h (n b) -> p (h n) b", b=blk)
                return v[:, :, 0:half], v[:, :, half:blk], v[:, :, half - 1:half], [P, 2 * T // blk, half]
            v = t[:, :, NM:T].rearrange("p h (n b) -> p h n b", b=blk)
            return v[:, :, :, 0:half], v[:, :, :, half:blk], v[:, :, :, half - 1:half], [P, 2, SEQ // blk, half]

        ATT_OFF = [0, 144, 416, 816]
        ATT_N = [144, 272, 400, 528]
        GROUPS = [[(0, i) for i in range(4)], [(1, i) for i in range(4)], [(2, 1), (2, 2), (2, 3)],
                  [(3, 2), (3, 3), (4, 3)]]
        G_COL = [0, 512, 1024, 1408]

        def s_view(i):
            if i == 3:
                return PS[:, 5:7, 0:264]
            return PS[:, 4 if i % 2 == 0 else 5, 0:ATT_N[i]]

        block = ctx.enter_context(nc.Block())

        @block.sync
        def _(sp):
            for i in range(QB):
                sp.dma_start(xt[:, i, :], a["x"][0, P * i:P * (i + 1), :]).then_inc(x_in, 16)
            sp.dma_start(xm[:, :], a["meta_tokens"]).then_inc(x_in, 16)
            landed = [0, 0]

            def dram(name):
                t = a[name]
                return t if len(t.shape) == 2 else t.rearrange("l k n -> (l k) n")

            def load(u):
                parts, kt, cols = pl.units[u]
                s = u % 2
                if u >= 2:
                    sp.wait_ge(w_split, 2 * (u - 1))
                for part in parts:
                    if part[0] == "w_uq":
                        src = a["w_uq_2"][0].rearrange("(k p) (h c) -> p k h c", p=P, c=QW)
                        dst = raw[s][:, :].rearrange("p (k h c) -> p k h c", k=2, h=8)
                        hs = slice(part[1], part[1] + 8)
                        for k in range(2):
                            for d0, s0, n in ((0, 0, QW), (96, NOPE + 16, 16), (112, NOPE, 16)):
                                sp.dma_start(dst[:, k, :, d0:d0 + n], src[:, k, hs, s0:s0 + n])\
                                  .then_inc(w_landed[s], 16)
                                landed[s] += 16
                        continue
                    name, row0, col0, n, d0 = part
                    if name == "w_pool":
                        src = a["w_pool"][0].rearrange("g c d -> c g d")
                        dst = raw[s][:, 0:512].rearrange("p (g d) -> p g d", g=4)
                    else:
                        src = dram(name)[row0:row0 + kt * P, col0:col0 + n].rearrange("(k p) c -> p k c", p=P)
                        dst = raw[s][:, 0:kt * cols].rearrange("p (k c) -> p k c", k=kt)[:, :, d0:d0 + n]
                    sp.dma_start(dst, src).then_inc(w_landed[s], 16)
                    landed[s] += 16

            spill_at = 3
            back_at = next(p.unit for p in pl.pieces if p.name == ("g", 1, 4))
            meta_at = next(p.unit for p in pl.pieces if p.name == ("dn", 6)) + 2
            trig_at = meta_at + 1
            for u in range(NU):
                load(u)
                if u == spill_at:
                    sp.wait_ge(norm1.z_ready, KT)
                    sp.dma_start(hspill, hT[:, :, :].rearrange("p k t -> p (k t)")).then_inc(spilled, 16)
                if u == back_at:
                    sp.wait_ge(oa_ready, 4)
                    sp.wait_ge(spilled, 16)
                    sp.dma_start(hT2[:, :, :].rearrange("p k t -> p (k t)"), hspill).then_inc(h_back, 16)
                if u == meta_at:
                    sp.wait_ge(pe_mark, pl.tile[("dn", 7)][1])
                    sp.dma_start(mtok[0:NM, 0, :], a["meta_tokens_2"]).then_inc(late_in, 16)
                    sp.dma_start(trig[:, :, :], a["c_trig"]).then_inc(late_in, 16)
            sp.wait_ge(pe_mark, pl.tile[("hy", 1, 7)][1])
            sp.dma_start(gpost[:, :], a["post_norm_g_2"].broadcast_to([P, D])).then_inc(late_in, 16)
            for i in range(QB):
                sp.wait_ge(fin_out, i + 1)
                sp.dma_start(out[0, P * i:P * (i + 1), :], mtok[:, i, :]).then_inc(out_done, 16)
            sp.wait_ge(out_done, 16 * QB)

        @block.gpsimd
        def _(pool):
            nc.gpsimd.memset(ident[:, :], 0.0).then_inc(const_ready, 1)
            nc.gpsimd.memset(ones[:, :], 1.0).then_inc(const_ready, 1)
            nc.gpsimd.memset(pair1[:, :], 0.0).then_inc(const_ready, 1)
            pool.wait_ge(const_ready, 3)
            nc.gpsimd.affine_select(out=ident[:, :], in_=ident[:, :], compare_op=ALU.not_equal, fill=1.0,
                                    base=0, pattern=[[-1, P]], channel_multiplier=1).then_inc(const_ready, 1)
            pool.wait_ge(const_ready, 4)
            nc.gpsimd.memset(pair1[0:64, 0:64], 1.0).then_inc(const_ready, 1)
            pool.wait_ge(const_ready, 5)
            nc.gpsimd.memset(pair1[64:P, 64:P], 1.0).then_inc(const_ready, 1)
            pool.wait_ge(const_ready, 6)
            landed = [0, 0]
            for u in range(NU):
                parts, kt, cols = pl.units[u]
                s, n = u % 2, kt * cols
                landed[s] += 16 * sum(6 if p[0] == "w_uq" else 1 for p in parts)
                pool.wait_ge(w_landed[s], landed[s])
                if u >= 2:
                    pool.wait_ge(pe_mark, pl.unit_end[u - 2])
                nc.gpsimd.tensor_scalar(hi[s][:, 0:n], raw[s][:, 0:n], 1.0, 1.0, ALU.mult, ALU.mult)\
                  .then_inc(w_split, 1)
                pool.wait_ge(w_split, 2 * u + 1)
                nc.gpsimd.tensor_tensor(lo[s][:, 0:n], raw[s][:, 0:n], hi[s][:, 0:n].bitcast(F32), ALU.subtract)\
                  .then_inc(w_split, 1)

        @block.tensor
        def _(pe):
            mm, tr = nc.tensor.matmul, nc.tensor.transpose
            X = {"z": (zhi, zlo), "ob": (obhi, oblo), "oa": (oahi, oalo), "g": (ghi, glo), "cq": (cqhi, cqlo),
                 "y": (yhi, ylo), "mx": (zhi, zlo)}
            at_piece = [0]

            def gemm(name, x_wait=None):
                p = pl.pieces[at_piece[0]]
                assert p.name == name, (p.name, name)
                at_piece[0] += 1
                parts, kt, cols = pl.units[p.unit]
                s = p.unit % 2
                pe.wait_ge(w_split, 2 * p.unit + 2)
                slot, _, uses = pl.tile[name]
                if p.first and uses:
                    pe.wait_ge(acc_free[slot], uses)
                W = [t[s][:, 0:kt * cols].rearrange("p (k c) -> p k c", k=kt) for t in (hi, lo)]
                for k in range(p.kt):
                    if x_wait is not None:
                        pe.wait_ge(x_wait, p.k0 + k + 1)
                    for w, x in ((0, 0), (0, 1), (1, 0)):
                        first = p.first and k == 0 and w == 0 and x == 0
                        last = p.last and k == p.kt - 1 and w == 1
                        if p.mode == "values":
                            t0, _ = chunk(p.k0)
                            lhs = (ckhi, cklo)[x][:, t0:t0 + P]
                            rhs = (hi, lo)[w][s][:, :].rearrange("p (h two c) -> p h two c", two=2, c=64)[
                                :, 8 * p.col:8 * p.col + 8, 1, :]
                            outs = [(PS[:, 2 * slot, :], lhs, rhs)]
                        elif p.mode == "tokens":
                            lhs = X["mx"][x][:, k, P * p.k0:P * p.k0 + P]
                            outs = [(PS[:, 2 * slot, 0:256], lhs, W[w][:, k, :])]
                        else:
                            lhs = W[w][:, k, p.col:p.col + P]
                            if p.x == "pd":
                                xs = (pdhi, pdlo)[x][:, :]
                            elif p.x == "ckv":
                                xs = (ckhi, cklo)[x][:, :]
                            else:
                                xs = X[p.x][x][:, p.k0 + k, :]
                            if p.mode == "full":
                                outs = [(PS[:, 2 * slot + b, 0:HALF], lhs, xs[:, HALF * b:HALF * (b + 1)])
                                        for b in range(2)]
                            else:
                                t0 = NM if p.mode == "real" and p.x != "g" else 0
                                outs = [(PS[:, 2 * slot, :], lhs, xs[:, t0:t0 + SEQ])]
                        for o_, l_, r_ in outs:
                            ins = mm(o_, l_, r_, start=first, stop=last)
                ins.then_inc(pe_mark, 1)

            def stats(n, lhs):
                for k in range(n.K):
                    pe.wait_ge(n.sq_ready, k + 1)
                    for b in range(2):
                        ins = mm(PS[:, 6 + b, 0:HALF], lhs[:, :], n.sqb[k % 2][:, HALF * b:HALF * (b + 1)],
                                 start=k == 0, stop=k == n.K - 1)
                    ins.then_inc(n.sq_used, 1)

            pe.wait_ge(const_ready, 6)
            pe.wait_ge(prm_in, PRM_DMAS)
            tr(PS[:, 4, 0:NROW1], prow[0:NROW1, 0, :], ident[0:NROW1, 0:NROW1])
            tr(PS[:, 4, P:P + NROW2], prow[0:NROW2, 1, :], ident[0:NROW2, 0:NROW2]).then_inc(prm_turned, 1)
            pe.wait_ge(x_in, 16 * (QB + 1))
            for k in range(KT):
                ins = tr(PS[:, 5, NM * k:NM * (k + 1)], xm[:, P * k:P * (k + 1)], ident[0:NM, 0:NM])
            ins.then_inc(x_turned, 1)
            for k in range(KT):
                if k >= 4:
                    pe.wait_ge(h_copied, k - 4 + 2)
                for i in range(QB):
                    ins = tr(PS[:, k % 4, P * i:P * (i + 1)], xt[:, i, P * k:P * (k + 1)], ident[:, :])
                ins.then_inc(x_turned, 1)
            stats(norm1, ones)
            pe.wait_ge(h_copied, KT + 1)

            def turn_values(src, j, turned, copied, tile_name):
                tile_freed(pe, tile_name)
                if j:
                    pe.wait_ge(copied, 2 * j)
                tr(PS[0:NM, 5, 0:P], src[:, 0:NM], ident[:, :])
                for c in range(1, 5):
                    t0, n = chunk(c)
                    ins = tr(PS[:, 4, P * (c - 1):P * c], src[:, t0:t0 + n], ident[:, :])
                ins.then_inc(turned, 1)

            def rec_step(p, i):
                b = 9 * p
                if i == 0:
                    pe.wait_ge(mul_ready, 8 * p + 1)
                    e = E[b % 2]
                    for hh in range(2):
                        bank = 7 - hh
                        if p:
                            if hh == 0:
                                pe.wait_ge(s_ready, 4 * p)
                            pe.wait_ge(o_copied, 5 * p)
                        else:
                            pe.wait_ge(norm1.rb_ready, 1)
                        for c in range(4):
                            t0, n = chunk(c)
                            ins = tr(PS[0:n, bank, P * c:P * (c + 1)], e[:, hh, t0:t0 + n], ident[:, :])
                        ins.then_inc(kd_turned, 1)
                    return
                if 1 <= i <= 7:
                    j = i - 1
                    half, blk = 1 << j, 2 << j
                    e = E[(b + i) % 2]
                    use = 8 * p + j
                    bank = 4 + use % 2
                    pe.wait_ge(mul_ready, 8 * p + i + 1)
                    if use >= 2:
                        pe.wait_ge(sc_copied, use - 1)
                    elif use == 0:
                        pe.wait_ge(v_copied, 8)
                    if blk <= NM:
                        if j == 0:
                            pe.wait_ge(kdt_ready, 2 * p + 2)
                        for hh in range(2):
                            rhs = e[:, hh, 0:NM].rearrange("p (n b) -> p n b", b=blk)[:, :, half:blk]
                            mm(PS[0:NM, 6, 16 * j + 8 * hh:16 * j + 8 * hh + 8].rearrange("p (n b) -> p n b", b=half),
                               e[:, hh, 0:NM], rhs, start=True, stop=True)
                    for hh in range(2):
                        for c in range(1, 5):
                            t0, n = chunk(c)
                            it = 4 * hh + c - 1
                            m = 64 if j == 6 else P
                            rhs = e[:, hh, t0:t0 + n].rearrange("p (n b) -> p n b", b=blk)[:, :, half:blk]
                            ins = mm(PS[0:m, bank, 64 * it:64 * it + 64].rearrange("p (n b) -> p n b", b=half),
                                     e[:, hh, t0:t0 + m], rhs, start=True, stop=True)
                    ins.then_inc(sc_done, 1)
                    if i <= 4:
                        c = i - 1
                        t0, n = chunk(c)
                        if c == 0:
                            pe.wait_ge(kdt_ready, 2 * p + 2)
                        else:
                            pe.wait_ge(s_ready, 4 * p + c)
                        for hh in range(2):
                            h = 2 * p + hh
                            ins = mm(PS[:, 7, 64 * hh:64 * hh + 64], kdt[0:n, hh, c, :],
                                     vtok1[0:n, c, 64 * h:64 * h + 64], start=True, stop=True)
                        ins.then_inc(upd_done, 1)
                    return
                if i == 8:
                    use = 8 * p + 7
                    pe.wait_ge(sc_copied, use - 1)
                    q, k = qf[p % 2], kf[p % 2]
                    for hh in range(2):
                        mm(PS[0:NM, 6, 64 + 16 * hh:80 + 16 * hh], k[:, hh, 0:NM], q[:, hh, 0:NM], start=True, stop=True)
                        for c in range(1, 5):
                            t0, n = chunk(c)
                            it = 4 * hh + c - 1
                            for r in range(2):
                                ins = mm(PS[64 * r:64 * r + 64, 4 + use % 2, 64 * it:64 * it + 64],
                                         k[:, hh, t0 + 64 * r:t0 + 64 * r + 64],
                                         q[:, hh, t0 + 64 * r:t0 + 64 * r + 64], start=True, stop=True)
                    ins.then_inc(sc_done, 1)
                    return
                pe.wait_ge(qd_ready, p + 1)
                e = E[(b + 8) % 2]
                for c in range(5):
                    t0, n = chunk(c)
                    bank = 6 + c % 2
                    if c == 0:
                        pe.wait_ge(c0_copied, p + 1)
                    elif c == 1:
                        pe.wait_ge(s_ready, 4 * p + 4)
                        pe.wait_ge(sc_copied, 8 * p + 8)
                    else:
                        pe.wait_ge(o_copied, 5 * p + c - 1)
                    for hh in range(2):
                        h = 2 * p + hh
                        sc = sc0[:, hh, :] if c == 0 else scT[:, 4 * hh + c - 1, :]
                        dst = PS[64 * hh:64 * hh + 64, bank, 0:n]
                        ins = mm(dst, vtok1[0:n, c, 64 * h:64 * h + 64], sc, start=True, stop=c == 0)
                        if c:
                            ins = mm(dst, Sc[:, hh, c - 1, :], e[:, hh, t0:t0 + n], start=False, stop=True)
                    ins.then_inc(o_done, 1)

            pending = None
            for n, steps in order:
                gemm(n, norm1.z_ready if n == ("v", 0) else None)
                if pending is not None:
                    j = pending
                    turn_values(E[j % 2][:, 0, :], j, v_turned, v_copied, ("v", j))
                    pending = None
                if n[0] == "v":
                    pending = n[1]
                for p, i in steps:
                    rec_step(p, i)
            for g in range(4):
                pe.wait_ge(pd_ready, g + 1)
                gemm(("pool", g))
            for b in range(2):
                for j in range(4):
                    for m in range(2):
                        gemm(("g", b, 2 * j + m))
                    if b == 0 and j == 0:
                        tile_freed(pe, ("pool", 3))
                    if b == 1 and j == 0:
                        for t in range(4):
                            pe.wait_ge(osq, t + 1)
                            if t:
                                pe.wait_ge(orn, t)
                            for r in range(2):
                                ins = mm(PS[:, 6 + r, 0:HALF], pair1[:, :], E[0][:, t % 2, HALF * r:HALF * (r + 1)],
                                         start=True, stop=True)
                            ins.then_inc(ossd, 1)
                        pe.wait_ge(oa_ready, 4)
                    for m in range(2):
                        gemm(("y", b, 2 * j + m))
            for k in range(KT):
                gemm(("out", k), mixz_ready if k == 0 else None)
            stats(norm2, ones)
            for j in range(FT // 2):
                for m in range(2):
                    gemm(("u", 2 * j + m), norm2.z_ready if j + m == 0 else None)
                for m in range(2):
                    gemm(("vv", 2 * j + m))
            pe.wait_ge(g_ready, FT)
            for j in range(4):
                for i in range(3):
                    for m in range(2):
                        gemm(("dn", 2 * j + m))
            stats(normf, ones)
            pe.wait_ge(late_in, 32)
            pe.wait_ge(h1_ready, KT)
            for k in range(KT):
                ins = tr(PS[:, 5, NM * k:NM * (k + 1)], mtok[0:NM, 0, P * k:P * (k + 1)], ident[0:NM, 0:NM])
            ins.then_inc(meta_turned, 1)
            stats(normp, ones)
            tile_freed(pe, ("dn", 6))
            tile_freed(pe, ("dn", 7))
            for i in range(QB):
                for q in range(2):
                    r = 2 * i + q
                    if r >= 4:
                        pe.wait_ge(ht_copied, r - 3)
                    for k in range(4):
                        ins = tr(PS[:, r % 4, P * k:P * (k + 1)], hT[:, 4 * q + k, NM + P * i:NM + P * (i + 1)], ident[:, :])
                    ins.then_inc(ht_turned, 1)
            pe.wait_ge(ht_copied, 8)
            gemm(("cq", 0), normp.z_ready)
            gemm(("cq", 1))
            gemm(("ckv", 0))
            gemm(("kpe", 0))
            gemm(("kpe", 1))
            stats(normq, ones)
            pe.wait_ge(normq.rb_ready, 1)
            stats(normk, ones)
            for i in range(5):
                for j in range(2):
                    gemm(("mv", i, j), normk.z_ready if i + j == 0 else None)

            def scores(A, h, i):
                if 4 * h + i >= 2:
                    pe.wait_ge(A.p_exp, 4 * h + i - 1)
                if i == 0:
                    tile_freed(pe, ("mk", h) if A is mla else ("xk", h // 4 * 2 + 1))
                t0, n = P * i, ATT_N[i]
                if i == 3:
                    cuts, tail = [(PS[:, 5, 0:264], 0), (PS[:, 6, 0:136], 264)], PS[:, 6, 136:264]
                else:
                    bank = 4 if i % 2 == 0 else 5
                    cuts, tail = [(PS[:, bank, 0:n - P], 0)], PS[:, bank, n - P:n]
                for dst, c0 in cuts + [(tail, n - P)]:
                    last = dst is tail
                    c1 = c0 + dst.shape[-1]
                    if A is mla:
                        ins = mm(dst, qh[h % 2][:, t0:t0 + P], kh[h % 2][:, c0:c1], start=True, stop=not last)
                    else:
                        r, m = 64 * (h % 2), (h // 2) % 2
                        mm(dst, fq[r:r + 64, m, t0:t0 + P], fk[r:r + 64, m, c0:c1], start=True, stop=False)
                        ins = mm(dst, pick[:, h:h + 1].broadcast_to([P, P]), nch[:, c0:c1], start=False,
                                 stop=not last)
                    if last:
                        ins = mm(dst, identb[:, :], causalb[:, :], start=False, stop=True)
                ins.then_inc(A.s_done, 1)

            def turn(A, h, g):
                if g == 0:
                    pe.wait_ge(A.p_ready, h + 1)
                done = A.pt_a if g % 2 == 0 else A.pt_v
                if 2 * h + g // 2:
                    pe.wait_ge(done, 2 * h + g // 2)
                for x, (j, i) in enumerate(GROUPS[g]):
                    o_ = ATT_OFF[i] + (0 if j == 0 else NM + P * (j - 1))
                    n = NM if j == 0 else P
                    ins = tr(PS[0:n, 2 + g % 2, P * x:P * (x + 1)], Pm[h % 2][:, o_:o_ + n], ident[:, :])
                ins.then_inc(A.g_turned, 1)

            def weigh(A, h):
                pe.wait_ge(A.pt_a, 2 * h + 2)
                pe.wait_ge(A.pt_v, 2 * h + 2)
                if h:
                    pe.wait_ge(A.o_ready, h)
                r = 64 * (h % 2)
                for j, (c0, q0, n) in enumerate(((0, 0, 512), (512, 0, 512), (1024, 128, 384), (1408, 256, 256),
                                                 (1664, 384, 128))):
                    rows = NM if j == 0 else P
                    ins = mm(PS[r:r + 64, 7, q0:q0 + n], vtok[0:rows, j, 64 * h:64 * h + 64],
                             PT[h % 2][0:rows, c0:c0 + n], start=j == 0, stop=j == 4, skip_group_check=True)
                ins.then_inc(A.o_done, 1)

            def attention(A, project):
                for h in range(HEADS + 2):
                    project(h)
                    if h >= 2:
                        weigh(A, h - 2)
                    for i in range(4):
                        if h < HEADS:
                            scores(A, h, i)
                        if 1 <= h <= HEADS:
                            turn(A, h - 1, i)

            def mla_project(h):
                for x in ([0, 1] if h == 0 else [h + 1]):
                    if x < HEADS:
                        gemm(("mq", x), normq.z_ready if x == 0 else None)
                        gemm(("mk", x))

            pe.wait_ge(kr_ready, 1)
            for i, j in ((4, 0), (4, 1)):
                tile_freed(pe, ("mv", i, j))
            attention(mla, mla_project)
            pe.wait_ge(mla.pt_a, 2 * HEADS)
            pe.wait_ge(mla.pt_v, 2 * HEADS)
            for k in range(KT):
                gemm(("mz", k))

            def gates(b):
                for j in range(4):
                    for m in range(2):
                        gemm(("hg", b, 2 * j + m))
                    if j == 0:
                        pe.wait_ge(y_ready, KT * (b + 1))
                    for m in range(2):
                        gemm(("hy", b, 2 * j + m))

            gates(0)
            for k in range(KT):
                gemm(("xv", k))
                if k:
                    turn_values(nzt[(k - 1) % 2][:, :], k - 1, xv_turned, xv_copied, ("xv", k - 1))
            turn_values(nzt[(KT - 1) % 2][:, :], KT - 1, xv_turned, xv_copied, ("xv", KT - 1))
            pe.wait_ge(xv_copied, 2 * KT)

            pe.wait_ge(cum_ready, 1)

            def fox_project(h):
                if h % 4 == 0 and h < HEADS:
                    for x in ("xq", "xk"):
                        for m in range(2):
                            gemm((x, h // 2 + m))

            pe.wait_ge(acc_free[1], pl.tile[("xv", KT - 1)][2] + 1)
            attention(fox, fox_project)
            pe.wait_ge(fox.pt_a, 2 * HEADS)
            pe.wait_ge(fox.pt_v, 2 * HEADS)
            for k in range(KT):
                gemm(("xz", k))
            gates(1)
            for j in range(4):
                for i in range(QB):
                    gemm(("fin", j, i), fmix if i + j == 0 else None)
            assert at_piece[0] == len(pl.pieces)

        @block.scalar
        def _(act):
            A_ = nc.scalar.activation
            steps = [0]

            def tick(ins):
                steps[0] += 1
                ins.then_inc(act_step, 1)

            def settle():
                act.wait_ge(act_step, steps[0])

            for name, half, dst in ROW_LOADS:
                src = a[name]
                flat = {1: "(t p) -> t p", 2: "l (t p) -> (l t) p", 3: "l w (t p) -> (l w t) p"}[len(src.shape)]
                r0, n = ROWS[dst]
                n = 16 if name == "lb_logits" else n
                r0 -= P * half
                act.dma_start(prow[r0:r0 + n, half, :], src.rearrange(flat, p=P)).then_inc(prm_in, 16)
            act.dma_start(cstage[:, 0:P], a["c_causal"]).then_inc(const_in, 16)
            act.dma_start(cstage[:, P:P + HEADS], a["c_pick"]).then_inc(const_in, 16)
            act.dma_start(cstage[:, P + HEADS:], a["c_level"]).then_inc(const_in, 16)
            act.dma_start(inv_n[:, :], a["c_inv"]).then_inc(const_in, 16)
            with nc.allow_non_contiguous_dma(reason="sixteen biases, one for each of sixteen partitions"):
                act.dma_start(fbias[0:HEADS, :], a["fox_forget_b_2"].rearrange("l (h o) -> (l h) o", o=1))\
                   .then_inc(const_in, 16)

            act.wait_ge(lb_sub, 1)
            A_(lbe, lbt, ACT.Exp).then_inc(lb_exp, 1)

            def norm_sq(n, k):
                if k >= 2:
                    act.wait_ge(n.sq_used, k - 1)
                A_(n.sqb[k % 2][:, :], n.src(k), ACT.Square).then_inc(n.sq_ready, 1)

            def norm_rb(n):
                act.wait_ge(n.sq_used, n.K)
                tick(A_(halves(n.rbb[:, :]), PS[:, 6:8, 0:HALF], ACT.Ln, scale=1.0 / n.width, bias=epst))
                settle()
                A_(n.rbb[:, :], n.rbb[:, :], ACT.Exp, scale=-0.5).then_inc(n.rb_ready, 1)

            def norm_hi(n, k):
                act.wait_ge(n.zt_ready, k + 1)
                A_(n.dst(k)[0], n.ztb[k % 2][:, :], ACT.Copy).then_inc(n.zhi_ready, 1)

            for k in range(KT):
                act.wait_ge(h_copied, k + 2)
                norm_sq(norm1, k)
            norm_rb(norm1)
            for k in range(KT):
                norm_hi(norm1, k)

            def rec_step(p, i):
                b = 9 * p

                def level_exp(x):
                    act.wait_ge(sub_ready, 8 * p + x + 1)
                    t = E[(b + x) % 2]
                    v = t[:, :, 0:400] if x == 0 else t[:, :, NM:T] if x - 1 >= 4 else t[:, :, :]
                    A_(v, v, ACT.Exp).then_inc(exp_ready, 1)

                if i == 0:
                    act.wait_ge(a_ready, 2 * p + 2)
                    if p:
                        act.wait_ge(s_ready, 4 * p)
                    tick(A_(el, av[p % 2][:, :, NM - 1:400:P], ACT.Exp))
                    level_exp(0)
                    level_exp(1)
                    for hh in range(2):
                        act.wait_ge(kd_turned, 2 * p + hh + 1)
                        tick(A_(kdt[0:NM, hh, 0, :], PS[0:NM, 7 - hh, 0:P], ACT.Copy))
                        A_(kdt[:, hh, 1:4, :], PS[:, 7 - hh, P:4 * P].rearrange("p (c k) -> p c k", c=3), ACT.Copy)\
                            .then_inc(kdt_ready, 1)
                elif i <= 6:
                    level_exp(i + 1)
                elif i == 7:
                    act.wait_ge(sc_done, 8 * p + 6)
                    A_(E[(b + 8) % 2][:, :, :], av[p % 2][:, :, :], ACT.Exp).then_inc(qd_exp, 1)
                elif i == 9:
                    for c in range(5):
                        t0, n = chunk(c)
                        act.wait_ge(o_done, 5 * p + c + 1)
                        A_(oT[:, p, t0:t0 + n], PS[:, 6 + c % 2, 0:n], ACT.Copy).then_inc(o_copied, 1)

            for name, hooks in order:
                kind, h = name
                p, hh = h // 2, h % 2
                tile_done(act, name)
                src = acc_full(name)
                if kind == "v":
                    if h >= 2:
                        act.wait_ge(v_turned, h - 1)
                    tile_free(A_(halves(E[h % 2][:, 0, :]), src, ACT.Copy), name)
                elif kind == "q":
                    if p >= 2:
                        act.wait_ge(o_done, 5 * (p - 1))
                    tile_free(A_(halves(qf[p % 2][:, hh, :]), src, ACT.Silu), name)
                elif kind == "f":
                    if p >= 2:
                        act.wait_ge(o_done, 5 * (p - 1))
                    tile_free(A_(halves(kf[p % 2][:, hh, :]), src, ACT.Sigmoid, bias=col("bf", h)), name)
                    act.wait_ge(f_ready, h + 1)
                    t = av[p % 2][:, hh, :]
                    A_(t, t, ACT.Ln).then_inc(ln_ready, 1)
                elif kind == "og":
                    tile_free(A_(halves(og[:, h, :]), src, ACT.Silu), name)
                else:
                    tile_free(A_(halves(pin[:, h, PADC:]), src, ACT.Copy), name)
                for step in hooks:
                    rec_step(*step)

            for g in range(4):
                tile_done(act, ("pool", g))
                A_(halves(obhi[:, g, :]), acc_full(("pool", g)), ACT.Copy, scale=col("pscale", g)).then_inc(obhi_ready, 1)

            for b in range(2):
                if b == 1:
                    act.wait_ge(o_copied, 20)
                    tile_freed(act, ("y", 0, 7))
                    for t in range(4):
                        if t >= 2:
                            act.wait_ge(ossd, t - 1)
                        A_(E[0][:, t % 2, :], oT[:, t, :], ACT.Square).then_inc(osq, 1)
                        act.wait_ge(ossd, t + 1)
                        if t >= 2:
                            act.wait_ge(on_ready, t - 1)
                        tick(A_(halves(E[1][:, t % 2, :]), PS[:, 6:8, 0:HALF], ACT.Ln, scale=1.0 / A_VDIM, bias=epst))
                        settle()
                        A_(E[1][:, t % 2, :], E[1][:, t % 2, :], ACT.Exp, scale=-0.5).then_inc(orn, 1)
                        act.wait_ge(on_ready, t + 1)
                        A_(oahi[:, t, :], oT[:, t, :], ACT.Copy).then_inc(oahi_ready, 1)
                for k in range(KT):
                    if k >= 2:
                        tile_freed(act, ("y", b, k - 2))
                    elif b == 0:
                        tile_freed(act, ("pool", 3))
                    else:
                        tile_freed(act, ("y", 0, 6 + k))
                    tile_done(act, ("g", b, k))
                    tile_free(A_(halves(gbuf[k % 2][:, :]), acc_full(("g", b, k)), ACT.Sigmoid), ("g", b, k))

            for k in range(KT):
                act.wait_ge(mix_ready, k + 1)
                A_(zhi[:, k, :], mix[:, k, :], ACT.Copy).then_inc(mixhi_ready, 1)
            for k in range(KT):
                tile_freed(act, ("out", k))
                norm_sq(norm2, k)
            norm_rb(norm2)
            for k in range(KT):
                norm_hi(norm2, k)

            for j in range(FT // 2):
                for k in (2 * j, 2 * j + 1):
                    tile_done(act, ("u", k))
                    if k >= 2:
                        act.wait_ge(c_ready, k - 1)
                    tile_free(A_(halves(ub[k % 2][:, :]), acc_full(("u", k)), ACT.Copy), ("u", k))
                for k in (2 * j, 2 * j + 1):
                    act.wait_ge(c_ready, k + 1)
                    A_(cb[k % 2][:, :], cb[k % 2][:, :], ACT.Silu).then_inc(silu_ready, 1)
                for k in (2 * j, 2 * j + 1):
                    tile_freed(act, ("vv", k))
                    A_(ghi[:, k, :], gt[k % 2][:, :], ACT.Copy).then_inc(ghi_ready, 1)

            for k in range(KT):
                tile_freed(act, ("dn", k))
                norm_sq(normf, k)
            norm_rb(normf)
            act.wait_ge(h1_meta, 1)
            for k in range(KT):
                act.wait_ge(h1_ready, k + 1)
                norm_sq(normp, k)
            norm_rb(normp)
            for k in range(KT):
                norm_hi(normp, k)
                act.wait_ge(ht_turned, k + 1)
                A_(htok[:, k // 2, SEQ * (k % 2):SEQ * (k % 2 + 1)], PS[:, k % 4, :], ACT.Copy).then_inc(ht_copied, 1)

            for k, name in enumerate((("cq", 0), ("cq", 1), ("ckv", 0))):
                tile_done(act, name)
                tile_free(A_(halves(cqT[:, k, :]), acc_full(name), ACT.Copy), name)
            tile_done(act, ("kpe", 0))
            f0, f1 = fgt[0:HEADS, 0, :], fgt[0:HEADS, 1, :]
            A_(halves(f0), acc_full(("kpe", 0), slice(0, HEADS)), ACT.Identity, bias=fbias[0:HEADS, :])\
                .then_inc(fl_ready, 1)
            act.wait_ge(fl_ready, 1)
            tick(A_(f1, f0, ACT.Abs))
            settle()
            tick(A_(f1, f1, ACT.Exp, scale=-1.0))
            settle()
            A_(f1, f1, ACT.Ln, bias=ones[0:HEADS, 0:1]).then_inc(fl_abs, 1)
            for n in (normq, normk):
                for k in range(n.K):
                    tile_freed(act, ("cq", k) if n is normq else ("ckv", 0))
                    norm_sq(n, k)
                norm_rb(n)
                for k in range(n.K):
                    norm_hi(n, k)

            def k_out(x):
                tile_done(act, ("mk", x))
                if x >= 2:
                    act.wait_ge(mla.s_done, 4 * (x - 1))
                tile_free(A_(halves(kh[x % 2][0:NOPE, :]), acc_full(("mk", x), slice(0, NOPE)), ACT.Copy), ("mk", x))

            def attention(A, project):
                for h in range(HEADS + 2):
                    project(h)
                    if h >= 2:
                        x, r = h - 2, 64 * (h % 2)
                        act.wait_ge(A.o_done, x + 1)
                        A_(omla[r:r + 64, x // 2, :], PS[r:r + 64, 7, :], ACT.Copy).then_inc(A.o_ready, 1)
                    for i in range(4):
                        if h < HEADS:
                            if h >= 2 and i == 0:
                                act.wait_ge(A.g_turned, 4 * (h - 1))
                            act.wait_ge(A.m_ready, 4 * h + i + 1)
                            s = 4 * (h % 2) + i
                            dst = Pm[h % 2][:, ATT_OFF[i]:ATT_OFF[i] + ATT_N[i]]
                            dst = halves(dst) if i == 3 else dst
                            A_(dst, s_view(i), ACT.Exp, bias=negmax[:, s:s + 1],
                               accum_out=rowsum[:, s:s + 1]).then_inc(A.p_exp, 1)
                        if 1 <= h <= HEADS and i % 2 == 0:
                            x = h - 1
                            act.wait_ge(A.g_turned, 4 * x + i + 1)
                            if x >= 2:
                                act.wait_ge(A.o_done, x - 1)
                            rows, n = (NM, 512) if i == 0 else (P, 384)
                            A_(PT[x % 2][0:rows, G_COL[i]:G_COL[i] + n], PS[0:rows, 2, 0:n], ACT.Copy)\
                                .then_inc(A.pt_a, 1)

            def mla_project(h):
                for x in ([0, 1] if h == 0 else [h + 1]):
                    if x < HEADS:
                        k_out(x)

            attention(mla, mla_project)

            def gated(kind, A, b):
                act.wait_ge(A.o_ready, HEADS)
                for k in range(KT):
                    tile_done(act, (kind, k))
                    if k >= 2:
                        act.wait_ge(ygt, KT * b + k - 1)
                    tile_free(A_(nsq[k % 2][:, 0:SEQ], acc_real((kind, k)), ACT.Silu), (kind, k))
                    act.wait_ge(ygt, KT * b + k + 1)
                    A_(yhi[:, k, :], nzt[k % 2][:, 0:SEQ], ACT.Copy).then_inc(yhi_r, 1)

            def gates(b):
                act.wait_ge(y_ready, KT * (b + 1))
                for k in range(KT):
                    if k >= 2:
                        tile_freed(act, ("hy", b, k - 2))
                    tile_done(act, ("hg", b, k))
                    tile_free(A_(nsq[k % 2][:, 0:SEQ], acc_real(("hg", b, k)), ACT.Sigmoid), ("hg", b, k))

            gated("mz", mla, 0)
            gates(0)
            for k in range(KT):
                tile_done(act, ("xv", k))
                if k >= 2:
                    act.wait_ge(xv_turned, k - 1)
                tile_free(A_(halves(nzt[k % 2][:, :]), acc_full(("xv", k)), ACT.Copy), ("xv", k))

            def fox_project(h):
                if h % 4 == 0 and h < HEADS:
                    for m in range(2):
                        n = ("xq", h // 2 + m)
                        tile_done(act, n)
                        tile_free(A_(fq[:, m, :], acc_real(n), ACT.Copy, scale=FOX_SCALE), n)
                    for m in range(2):
                        n = ("xk", h // 2 + m)
                        tile_done(act, n)
                        tile_free(A_(halves(fk[:, m, :]), acc_full(n), ACT.Copy), n)

            attention(fox, fox_project)
            gated("xz", fox, 1)
            gates(1)
            tile_done(act, ("hg", 1, 7))
            for k in range(KT):
                act.wait_ge(mix2_ready, k + 1)
                A_(zhi[:, k, 0:SEQ], mix2[:, k, :], ACT.Copy).then_inc(fmixhi, 1)
            for i in range(QB):
                tile_freed(act, ("fin", 3, i))
                s = ssum[:, i:i + 1]
                tick(A_(fjunk[:, :], mtok[:, i, :], ACT.Square, accum_out=s))
                settle()
                tick(A_(s, s, ACT.Ln, scale=1.0 / D, bias=epst))
                settle()
                A_(s, s, ACT.Exp, scale=-0.5).then_inc(fin_rstd, 1)

        @block.vector
        def _(dve):
            V = nc.vector
            steps = [0]

            def tick(ins):
                steps[0] += 1
                ins.then_inc(dve_step, 1)

            def settle():
                dve.wait_ge(dve_step, steps[0])

            tick(V.memset(epst, EPS))
            tick(V.memset(rmask[:, :], 1.0))
            tick(V.memset(pin[:, :, 0:PADC], 0.0))
            tick(V.memset(scT[:, :, :], 0.0))
            tick(V.memset(sc0[:, :, :], 0.0))
            settle()
            for c in range(5):
                tick(V.memset(rmask[:, chunk(c)[0]:chunk(c)[0] + 1], 0.0))
            dve.wait_ge(prm_turned, 1)
            tick(V.tensor_copy(prm[:, 0:NROW1], PS[:, 4, 0:NROW1]))
            tick(V.tensor_copy(prm[:, P:P + NROW2], PS[:, 4, P:P + NROW2]))
            settle()
            l0, l1 = prm[:, 8:16], prm[:, 16:24]
            tick(V.tensor_tensor(lb, l0, l1, ALU.max))
            settle()
            tick(V.tensor_tensor(lbt[:, 0:8], l0, lb, ALU.subtract))
            V.tensor_tensor(lbt[:, 8:16], l1, lb, ALU.subtract).then_inc(lb_sub, 1)
            dve.wait_ge(x_turned, 1)
            V.tensor_copy(hT[:, :, 0:NM], PS[:, 5, 0:P].rearrange("p (k t) -> p k t", k=KT)).then_inc(h_copied, 1)
            for k in range(KT):
                dve.wait_ge(x_turned, k + 2)
                V.tensor_copy(hT[:, k, NM:T], PS[:, k % 4, :]).then_inc(h_copied, 1)
            dve.wait_ge(lb_exp, 1)
            tick(V.tensor_tensor(omlb, lbe[:, 0:8], lbe[:, 8:16], ALU.add))
            settle()
            tick(V.reciprocal(omlb, omlb))
            settle()
            tick(V.tensor_tensor(lb, lbe[:, 0:8], omlb, ALU.mult))
            settle()
            tick(V.tensor_scalar(lb, lb, 2.0 ** -63, None, ALU.max))
            settle()
            tick(V.tensor_scalar(omlb, lb, -1.0, 1.0, ALU.mult, ALU.add))
            dve.wait_ge(const_in, 16 * 5)
            dve.wait_ge(const_ready, 6)
            tick(V.tensor_copy(causalb[:, :], cstage[:, 0:P]))
            tick(V.tensor_copy(identb[:, :], ident[:, :]))
            tick(V.tensor_copy(pick[:, :], cstage[:, P:P + HEADS]))
            tick(V.tensor_copy(lvl[:, :], cstage[:, P + HEADS:]))
            settle()

            def norm_zt(n, k):
                if k == 0:
                    dve.wait_ge(n.rb_ready, 1)
                V.scalar_tensor_tensor(out=n.ztb[k % 2][:, :], in0=n.src(k), scalar=col(n.gain, k),
                                       in1=n.rbb[:, :], op0=ALU.mult, op1=ALU.mult).then_inc(n.zt_ready, 1)

            def norm_lo(n, k):
                dve.wait_ge(n.zhi_ready, k + 1)
                h_, l_ = n.dst(k)
                V.tensor_tensor(l_, n.ztb[k % 2][:, :], h_.bitcast(F32), ALU.subtract).then_inc(n.z_ready, 1)

            def norm_split(n):
                for k in range(n.K + 1):
                    if k < n.K:
                        if k >= 2:
                            dve.wait_ge(n.z_ready, k - 1)
                        norm_zt(n, k)
                    if k >= 1:
                        norm_lo(n, k - 1)

            norm_split(norm1)

            def values_out(j, turned, copied, dst):
                dve.wait_ge(turned, j + 1)
                V.tensor_copy(dst[0:NM, 0, P * j:P * (j + 1)], PS[0:NM, 5, 0:P]).then_inc(copied, 1)
                V.tensor_copy(dst[:, 1:5, P * j:P * (j + 1)], PS[:, 4, :].rearrange("p (c f) -> p c f", c=4))\
                 .then_inc(copied, 1)

            def rec_step(p, i):
                b = 9 * p
                q, kk, ac = qf[p % 2], kf[p % 2], av[p % 2]

                def free(x):
                    if x == 0:
                        if p:
                            dve.wait_ge(sc_done, 8 * p - 1)
                        else:
                            dve.wait_ge(v_turned, 4)
                    elif x == 1:
                        if p:
                            dve.wait_ge(o_done, 5 * p)
                    elif x == 2:
                        dve.wait_ge(kd_turned, 2 * p + 2)
                    else:
                        dve.wait_ge(sc_done, 8 * p + x - 2)

                def sub(x):
                    free(x)
                    t = E[(b + x) % 2]
                    if x == 0:
                        dve.wait_ge(a_ready, 2 * p + 2)
                        tick(V.tensor_tensor(t[:, :, 0:NM], ac[:, :, NM - 1:NM].broadcast_to([P, 2, NM]),
                                             ac[:, :, 0:NM], ALU.subtract))
                        sv = lambda z: z[:, :, NM:400].rearrange("p h (c t) -> p h c t", t=CH)
                        V.tensor_tensor(sv(t), sv(ac)[:, :, :, CH - 1:CH].broadcast_to([P, 2, 3, CH]), sv(ac),
                                        ALU.subtract).then_inc(sub_ready, 1)
                        return
                    tl, tr_, _, shape = level_views(t, x - 1)
                    al, ar, mid, _ = level_views(ac, x - 1)
                    tick(V.tensor_tensor(tl, mid.broadcast_to(shape), al, ALU.subtract))
                    V.tensor_tensor(tr_, ar, mid.broadcast_to(shape), ALU.subtract).then_inc(sub_ready, 1)

                def mul(x):
                    dve.wait_ge(exp_ready, 8 * p + x + 1)
                    t = E[(b + x) % 2]
                    if x == 0:
                        V.tensor_tensor(t[:, :, 0:400], t[:, :, 0:400], kk[:, :, 0:400], ALU.mult).then_inc(mul_ready, 1)
                        return
                    tl, tr_, _, _ = level_views(t, x - 1)
                    ql = level_views(q, x - 1)[1]
                    kl = level_views(kk, x - 1)[0]
                    tick(V.tensor_tensor(tr_, tr_, ql, ALU.mult))
                    V.tensor_tensor(tl, tl, kl, ALU.mult).then_inc(mul_ready, 1)

                def evac(j):
                    use = 8 * p + j
                    bank = 4 + use % 2
                    dve.wait_ge(sc_done, use + 1)
                    if use:
                        dve.wait_ge(sc_copied, use)
                    if j == 0 and p:
                        dve.wait_ge(o_done, 5 * p)
                    if j == 6:
                        V.tensor_copy(scT[0:64, :, 64:P], PS[0:64, bank, :].rearrange("p (i t) -> p i t", i=8))\
                         .then_inc(sc_copied, 1)
                        return
                    if j == 7:
                        for r in range(2):
                            rows = slice(64 * r, 64 * r + 64)
                            ins = V.copy_predicated(scT[rows, :, 64 * r:64 * r + 64],
                                                    lvl[rows, 448:512].unsqueeze(1).broadcast_to([64, 8, 64]),
                                                    PS[rows, bank, :].rearrange("p (i t) -> p i t", i=8))
                            if r == 0:
                                tick(ins)
                        ins.then_inc(sc_copied, 1)
                        return
                    half, blk = 1 << j, 2 << j
                    n = P // blk
                    m = lvl[:, 64 * j:64 * j + 64].rearrange("p (n b) -> p n b", b=half).unsqueeze(1)
                    V.copy_predicated(scT[:, :, :].rearrange("p i (n b) -> p i n b", b=blk)[:, :, :, half:blk],
                                      m.broadcast_to([P, 8, n, half]),
                                      PS[:, bank, :].rearrange("p (i n b) -> p i n b", i=8, b=half)).then_inc(sc_copied, 1)

                def state(c):
                    dve.wait_ge(upd_done, 4 * p + c + 1)
                    if c == 0:
                        V.tensor_copy(Sc[:, :, 0, :], PS[:, 7, 0:P].rearrange("p (h v) -> p h v", h=2)).then_inc(s_ready, 1)
                        return
                    dve.wait_ge(s_ready, 4 * p + c)
                    for hh in range(2):
                        ins = V.scalar_tensor_tensor(out=Sc[:, hh, c, :], in0=Sc[:, hh, c - 1, :], scalar=el[:, hh, c:c + 1],
                                                     in1=PS[:, 7, 64 * hh:64 * hh + 64], op0=ALU.mult, op1=ALU.add)
                        if hh == 0:
                            tick(ins)
                    ins.then_inc(s_ready, 1)

                if i == 0:
                    for hh in range(2):
                        tile_freed(dve, ("q", 2 * p + hh))
                    sub(0)
                    sub(1)
                    mul(0)
                elif i <= 7:
                    if 2 <= i <= 5:
                        state(i - 2)
                    if i <= 6:
                        sub(i + 1)
                    mul(i)
                    if i >= 2:
                        evac(i - 2)
                elif i == 8:
                    evac(6)
                    dve.wait_ge(qd_exp, p + 1)
                    t = E[(b + 8) % 2]
                    V.tensor_tensor(t[:, :, :], t[:, :, :], q[:, :, :], ALU.mult).then_inc(qd_ready, 1)
                else:
                    evac(7)
                    for j in range(4):
                        half, blk = 1 << j, 2 << j
                        n = NM // blk
                        m = lvl[0:NM, 64 * j:64 * j + 8].rearrange("p (n b) -> p n b", b=half).unsqueeze(1)
                        tick(V.copy_predicated(
                            sc0[:, :, :].rearrange("p i (n b) -> p i n b", b=blk)[:, :, :, half:blk],
                            m.broadcast_to([NM, 2, n, half]),
                            PS[0:NM, 6, 16 * j:16 * j + 16].rearrange("p (i n b) -> p i n b", i=2, b=half)))
                        settle()
                    V.copy_predicated(sc0[:, :, :], lvl[0:NM, 448:464].unsqueeze(1).broadcast_to([NM, 2, NM]),
                                      PS[0:NM, 6, 64:96].rearrange("p (i t) -> p i t", i=2)).then_inc(c0_copied, 1)

            for idx, (name, hooks) in enumerate(order):
                kind, h = name
                p, hh = h // 2, h % 2
                if 1 <= idx <= 4:
                    values_out(idx - 1, v_turned, v_copied, vtok1)
                if kind == "f":
                    tile_freed(dve, name)
                    if p >= 2:
                        dve.wait_ge(o_done, 5 * (p - 1))
                    f, k_ = av[p % 2][:, hh, :], kf[p % 2][:, hh, :]
                    tick(V.tensor_scalar(f, k_, omlb[:, h:h + 1], lb[:, h:h + 1], ALU.mult, ALU.add))
                    settle()
                    V.tensor_scalar(k_, f, -1.0, 1.0, ALU.mult, ALU.add).then_inc(f_ready, 1)
                    dve.wait_ge(ln_ready, h + 1)
                    V.tensor_tensor_scan(f, rmask[:, :], f, 0.0, ALU.mult, ALU.add).then_inc(a_ready, 1)
                for step in hooks:
                    rec_step(*step)

            def pool_out(g):
                n = ("pool", g)
                dve.wait_ge(obhi_ready, g + 1)
                tile_free(V.scalar_tensor_tensor(out=halves(oblo[:, g, :]), in0=acc_full(n), scalar=col("pscale", g),
                                                 in1=halves(obhi[:, g, :].bitcast(F32)), op0=ALU.mult,
                                                 op1=ALU.subtract), n)

            W_ = T + PADC
            for g in range(4):
                w = POOL_WINDOWS[g]
                tile_freed(dve, ("pin", g))
                src = pin[:, g, :]
                cur = src
                for s in range(g + 1):
                    d = 1 << s
                    dst = pp[s % 2]
                    tick(V.tensor_tensor(dst[:, 2 * d - 1:W_], cur[:, 2 * d - 1:W_], cur[:, d - 1:W_ - d], ALU.add))
                    settle()
                    cur = dst
                dst = pp[(g + 1) % 2]
                c0 = PADC + w - 1
                tick(V.scalar_tensor_tensor(out=dst[:, c0:W_], in0=cur[:, c0:W_], scalar=1.0 / w, in1=src[:, c0:W_],
                                            op0=ALU.mult, op1=ALU.subtract))
                tick(V.tensor_tensor(dst[:, PADC:c0], cur[:, PADC:c0], inv_n[:, 0:w - 1], ALU.mult))
                settle()
                tick(V.tensor_tensor(dst[:, PADC:c0], dst[:, PADC:c0], src[:, PADC:c0], ALU.subtract))
                settle()
                if g:
                    tile_done(dve, ("pool", g - 1))
                tick(V.tensor_copy(pdhi[:, :], dst[:, PADC:W_]))
                settle()
                V.tensor_tensor(pdlo[:, :], dst[:, PADC:W_], pdhi[:, :].bitcast(F32), ALU.subtract).then_inc(pd_ready, 1)
                dve.wait_ge(pd_ready, g + 1)
                if g:
                    pool_out(g - 1)
            pool_out(3)

            dve.wait_ge(spilled, 16)
            for b in range(2):
                if b == 1:
                    for t in range(4):
                        tile_freed(dve, ("og", t))
                        dve.wait_ge(orn, t + 1)
                        tick(V.scalar_tensor_tensor(out=oT[:, t, :], in0=oT[:, t, :], scalar=col("head", t),
                                                    in1=E[1][:, t % 2, :], op0=ALU.mult, op1=ALU.mult))
                        settle()
                        V.tensor_tensor(oT[:, t, :], oT[:, t, :], og[:, t, :], ALU.mult).then_inc(on_ready, 1)
                        dve.wait_ge(oahi_ready, t + 1)
                        V.tensor_tensor(oalo[:, t, :], oT[:, t, :], oahi[:, t, :].bitcast(F32), ALU.subtract)\
                         .then_inc(oa_ready, 1)
                for k in range(KT):
                    n = ("y", b, k)
                    tile_done(dve, n)
                    tile_freed(dve, ("g", b, k))
                    dst = mix[:, k, :] if b == 0 else tmp[k % 2][:, :]
                    if b and k >= 2:
                        dve.wait_ge(mix_ready, k - 1)
                    tile_free(V.tensor_tensor(halves(dst), acc_full(n), halves(gbuf[k % 2][:, :]), ALU.mult), n)
                    if b:
                        tile_freed(dve, n)
                        V.tensor_tensor(mix[:, k, :], mix[:, k, :], tmp[k % 2][:, :], ALU.add).then_inc(mix_ready, 1)
            for k in range(KT):
                dve.wait_ge(mixhi_ready, k + 1)
                dve.wait_ge(mix_ready, k + 1)
                V.tensor_tensor(zlo[:, k, :], mix[:, k, :], zhi[:, k, :].bitcast(F32), ALU.subtract)\
                 .then_inc(mixz_ready, 1)
            dve.wait_ge(h_back, 16)
            dve.wait_ge(mixz_ready, KT)
            for k in range(KT):
                n = ("out", k)
                tile_done(dve, n)
                tile_free(V.tensor_tensor(halves(hT[:, k, :]), acc_full(n), halves(hT2[:, k, :]), ALU.add), n)
            for k in (6, 7):
                tile_freed(dve, ("out", k))
            norm_split(norm2)

            for j in range(FT // 2):
                for k in (2 * j, 2 * j + 1):
                    tile_freed(dve, ("u", k))
                    u, c = ub[k % 2], cb[k % 2][:, :]
                    if k >= 2:
                        tile_freed(dve, ("vv", k - 2))
                    tick(V.tensor_scalar(c, u[:, NM:T], col("convw", 2 * FT + k), col("convb", k), ALU.mult, ALU.add))
                    settle()
                    tick(V.scalar_tensor_tensor(out=c, in0=u[:, NM - 1:T - 1], scalar=col("convw", FT + k), in1=c,
                                                op0=ALU.mult, op1=ALU.add))
                    settle()
                    V.scalar_tensor_tensor(out=c, in0=u[:, NM - 2:T - 2], scalar=col("convw", k), in1=c,
                                           op0=ALU.mult, op1=ALU.add).then_inc(c_ready, 1)
                for k in (2 * j, 2 * j + 1):
                    n = ("vv", k)
                    tile_done(dve, n)
                    dve.wait_ge(silu_ready, k + 1)
                    if k >= 2:
                        dve.wait_ge(g_ready, k - 1)
                    tile_free(V.tensor_tensor(gt[k % 2][:, :], acc_real(n), cb[k % 2][:, :], ALU.mult), n)
                for k in (2 * j, 2 * j + 1):
                    dve.wait_ge(ghi_ready, k + 1)
                    V.tensor_tensor(glo[:, k, :], gt[k % 2][:, :], ghi[:, k, :].bitcast(F32), ALU.subtract)\
                     .then_inc(g_ready, 1)
            for k in range(KT):
                n = ("dn", k)
                tile_done(dve, n)
                tile_free(V.tensor_tensor(hT[:, k, NM:T], acc_real(n), hT[:, k, NM:T], ALU.add), n)
            for k in (6, 7):
                tile_freed(dve, ("dn", k))
            dve.wait_ge(normf.rb_ready, 1)
            for k in range(KT):
                V.scalar_tensor_tensor(out=hT[:, k, :], in0=hT[:, k, :], scalar=col("final", k), in1=nrb[:, :],
                                       op0=ALU.mult, op1=ALU.mult).then_inc(h1_ready, 1)
            dve.wait_ge(h1_ready, KT)
            dve.wait_ge(meta_turned, 1)
            V.tensor_copy(hT[:, :, 0:NM], PS[:, 5, 0:P].rearrange("p (k t) -> p k t", k=KT)).then_inc(h1_meta, 1)
            dve.wait_ge(h1_meta, 1)
            norm_split(normp)

            dve.wait_ge(late_in, 32)
            r_ = slice(64, P)
            t1, t2 = PT[0][r_, 0:T], PT[0][r_, T:2 * T]
            dve.wait_ge(fl_ready, 1)
            tile_done(dve, ("kpe", 1))
            tile_free(V.tensor_tensor(halves(t1), acc_full(("kpe", 0), r_), halves(trig[r_, 1, :]), ALU.mult), ("kpe", 0))
            tile_free(V.tensor_tensor(halves(t2), acc_full(("kpe", 1), r_), halves(trig[r_, 2, :]), ALU.mult), ("kpe", 1))
            tile_freed(dve, ("kpe", 0))
            tile_freed(dve, ("kpe", 1))
            tick(V.tensor_tensor(kh[0][r_, :], t1, t2, ALU.add))
            V.tensor_tensor(kh[1][r_, :], t1, t2, ALU.add).then_inc(kr_ready, 1)
            f0, f1 = fgt[0:HEADS, 0, :], fgt[0:HEADS, 1, :]
            dve.wait_ge(fl_abs, 1)
            tick(V.memset(nch[:, :].bitcast(F32), 0.0))
            tick(V.tensor_scalar(f0, f0, 0.0, None, ALU.min))
            settle()
            tick(V.tensor_tensor(f0, f0, f1, ALU.subtract))
            settle()
            tick(V.tensor_tensor_scan(f1, trig[0:HEADS, 0, :], f0, 0.0, ALU.mult, ALU.add))
            settle()
            tick(V.tensor_scalar(f0, f1, -1.0, None, ALU.mult))
            settle()
            tick(V.tensor_copy(nch[0:HEADS, :], f0))
            settle()
            V.tensor_tensor(nch[32:32 + HEADS, :], f0, nch[0:HEADS, :].bitcast(F32), ALU.subtract).then_inc(cum_ready, 1)
            norm_split(normq)
            dve.wait_ge(normq.z_ready, 2)
            norm_split(normk)
            for i in range(5):
                for j in range(2):
                    n = ("mv", i, j)
                    rows = NM if i == 0 else P
                    tile_done(dve, n)
                    tile_free(V.tensor_copy(vtok[0:rows, i, SEQ * j:SEQ * (j + 1)], acc_real(n, slice(0, rows))), n)

            def attention(A, project):
                for h in range(HEADS + 2):
                    project(h)
                    for i in range(4):
                        if h < HEADS:
                            dve.wait_ge(A.s_done, 4 * h + i + 1)
                            s = 4 * (h % 2) + i
                            V.tensor_reduce(negmax[:, s:s + 1], s_view(i), AX.XY if i == 3 else AX.X, ALU.max,
                                            negate=True).then_inc(A.m_ready, 1)
                        if 1 <= h <= HEADS and i % 2 == 1:
                            x = h - 1
                            dve.wait_ge(A.g_turned, 4 * x + i + 1)
                            if x >= 2:
                                dve.wait_ge(A.o_done, x - 1)
                            n = 512 if i == 1 else 384
                            V.tensor_copy(PT[x % 2][:, G_COL[i]:G_COL[i] + n], PS[:, 3, 0:n]).then_inc(A.pt_v, 1)
                    if h < HEADS:
                        dve.wait_ge(A.p_exp, 4 * h + 4)
                        s = 4 * (h % 2)
                        tick(V.reciprocal(rinv, rowsum[:, s:s + 4]))
                        settle()
                        for i in range(4):
                            t = Pm[h % 2][:, ATT_OFF[i]:ATT_OFF[i] + ATT_N[i]]
                            ins = V.tensor_scalar(t, t, rinv[:, i:i + 1], None, ALU.mult)
                            if i < 3:
                                tick(ins)
                        ins.then_inc(A.p_ready, 1)

            def mla_project(h):
                for x in ([0, 1] if h == 0 else [h + 1]):
                    if x < HEADS:
                        n = ("mq", x)
                        tile_done(dve, n)
                        if x >= 2:
                            dve.wait_ge(mla.s_done, 4 * (x - 1))
                        tile_free(V.scalar_tensor_tensor(out=qh[x % 2][:, :], in0=acc_real(n), scalar=MLA_SCALE,
                                                         in1=trig[:, 0, NM:T], op0=ALU.mult, op1=ALU.mult), n)

            attention(mla, mla_project)

            def gated(kind, A, b):
                dve.wait_ge(A.o_ready, HEADS)
                for k in range(KT):
                    tile_freed(dve, (kind, k))
                    if k >= 2:
                        dve.wait_ge(y_ready, KT * b + k - 1)
                    V.tensor_tensor(nzt[k % 2][:, 0:SEQ], omla[:, k, :], nsq[k % 2][:, 0:SEQ], ALU.mult).then_inc(ygt, 1)
                    dve.wait_ge(yhi_r, KT * b + k + 1)
                    V.tensor_tensor(ylo[:, k, :], nzt[k % 2][:, 0:SEQ], yhi[:, k, :].bitcast(F32), ALU.subtract)\
                     .then_inc(y_ready, 1)

            def gates(b):
                for k in range(KT):
                    n = ("hy", b, k)
                    tile_done(dve, n)
                    tile_freed(dve, ("hg", b, k))
                    dst = mix2[:, k, :] if b == 0 else nzt[k % 2][:, 0:SEQ]
                    if b and k >= 2:
                        dve.wait_ge(mix2_ready, k - 1)
                    tile_free(V.tensor_tensor(dst, acc_real(n), nsq[k % 2][:, 0:SEQ], ALU.mult), n)
                    if b:
                        tile_freed(dve, n)
                        V.tensor_tensor(mix2[:, k, :], mix2[:, k, :], nzt[k % 2][:, 0:SEQ], ALU.add)\
                         .then_inc(mix2_ready, 1)

            gated("mz", mla, 0)
            gates(0)
            for k in range(KT):
                values_out(k, xv_turned, xv_copied, vtok)
            attention(fox, lambda h: None)
            gated("xz", fox, 1)
            dve.wait_ge(y_ready, 2 * KT)
            gates(1)
            for k in range(KT):
                dve.wait_ge(fmixhi, k + 1)
                dve.wait_ge(mix2_ready, k + 1)
                V.tensor_tensor(zlo[:, k, 0:SEQ], mix2[:, k, :], zhi[:, k, 0:SEQ].bitcast(F32), ALU.subtract)\
                 .then_inc(fmix, 1)
            for j in range(4):
                for i in range(QB):
                    n = ("fin", j, i)
                    tile_done(dve, n)
                    tile_free(V.tensor_copy(mtok[:, i, 256 * j:256 * (j + 1)], acc_real(n, n=256)), n)
            dve.wait_ge(late_in, 48)
            for i in range(2, QB):
                tile_freed(dve, ("fin", 3, i))
            for i in range(QB):
                dve.wait_ge(fin_rstd, i + 1)
                tick(V.scalar_tensor_tensor(out=mtok[:, i, :], in0=mtok[:, i, :], scalar=ssum[:, i:i + 1],
                                            in1=gpost[:, :], op0=ALU.mult, op1=ALU.mult))
                settle()
                V.tensor_tensor(mtok[:, i, :], mtok[:, i, :], htok[:, i, :], ALU.add).then_inc(fin_out, 1)


_OUTS = [((1, SEQ, D), "float32")]


def kernel(**inputs):
    import concourse.bacc as _bacc
    from concourse.bass_utils import run_bass_kernel_spmd as _run

    nc = _bacc.Bacc("TRN2", target_bir_lowering=False, num_devices=1)
    arrays, args = {}, {}
    every = {k: np.asarray(v) for k, v in inputs.items()}
    every.update(host_constants())
    for name, value in every.items():
        value = np.ascontiguousarray(value)
        arrays[f"in_{name}"] = value
        args[name] = nc.dram_tensor(f"in_{name}", value.shape, mybir.dt.from_np(value.dtype), kind="ExternalInput").ap()
    out = nc.dram_tensor("out_0", _OUTS[0][0], F32, kind="ExternalOutput").ap()
    build_program(nc, args, out)
    r = _run(nc, [arrays], core_ids=[0])
    return r.results[0]["out_0"]
```

```python
from contextlib import ExitStack

import numpy as np

import concourse.bass as bass
from concourse import mybir

F32 = mybir.dt.float32
F32R = mybir.dt.float32r
BF16 = mybir.dt.bfloat16
U8 = mybir.dt.uint8
ALU = mybir.AluOpType
ACT = mybir.ActivationFunctionType
AX = mybir.AxisListType

P = 128
D = 1024
KT = D // P
NM = 16
SEQ = 512
T = NM + SEQ
HALF = T // 2
EPS = 1e-6

A_HEADS = 8
A_VDIM = 64
D_FF = 2816
FT = D_FF // P
POOL_WINDOWS = (2, 4, 8, 16)
PADC = 16
CH = 128
NCH = SEQ // CH
LEVELS = 7
MASKC = 64 * (LEVELS + 1)

HEADS = 16
ROPE = 32
NOPE = 64
QW = NOPE + ROPE
DV = 64
QB = SEQ // P
MLA_SCALE = 1.0 / float(np.sqrt(QW))
FOX_SCALE = 1.0 / 8.0
NEG = -1.0e30

A_Q, A_F, A_V, A_OG, B_IN, G_A, G_B = 0, 1024, 2048, 2560, 3072, 3584, 4608
M_CQ, M_CKV, M_KPE, M_Z, X_Q, X_K, X_V, X_F, X_Z, H_A, H_B = (
    0, 256, 384, 416, 1440, 2464, 3488, 4512, 4528, 5552, 6576)

ROWS = {}
for _name, _n in (("norm1", 8), ("lb0", 8), ("lb1", 8), ("bf", 8), ("head", 4), ("pscale", 4), ("norm2", 8),
                  ("final", 8), ("pre", 8), ("qn", 2), ("kvn", 1)):
    ROWS[_name] = (sum(n for _, n in ROWS.values()), _n)
NROW1 = sum(n for _, n in ROWS.values())
ROWS["convw"] = (P, 3 * FT)
ROWS["convb"] = (P + 3 * FT, FT)
NROW2 = 4 * FT


def host_constants():
    s = np.arange(P)[:, None]
    mask = np.zeros((P, MASKC), np.float32)
    for j in range(LEVELS):
        half = 1 << j
        n, b = np.divmod(np.arange(64), half)
        mask[:, 64 * j:64 * j + 64] = (s // (2 * half) == n[None]) & (s % (2 * half) < half)
    mask[:, 64 * LEVELS:] = s % 64 == np.arange(64)[None]
    pos = np.arange(T, dtype=np.float32)
    half = ROPE // 2
    freq = np.float32(10000.0) ** (-np.arange(half, dtype=np.float32) / np.float32(half))
    ang = (pos[None, :] * freq[:, None].astype(np.float32)).astype(np.float64)
    cos, sin = np.cos(ang).astype(np.float32), np.sin(ang).astype(np.float32)
    trig = np.ones((P, 3, T), np.float32)
    trig[64:96, 0] = np.concatenate([cos, cos])
    trig[96:128, 0] = np.concatenate([-sin, sin])
    trig[64:128, 1] = np.concatenate([cos, cos, cos, cos])
    trig[64:128, 2] = np.concatenate([-sin, sin, -sin, sin])
    inv = np.ones((P, PADC), np.float32)
    inv[:] = 1.0 / np.arange(1, PADC + 1, dtype=np.float32)
    causal = np.where(np.arange(P)[None] > np.arange(P)[:, None], np.float32(NEG), np.float32(0.0))
    e = np.zeros((P, HEADS), np.float32)
    for h in range(HEADS):
        e[h, h] = e[32 + h, h] = 1.0
    return {"c_level": mask, "c_trig": trig, "c_inv": inv, "c_causal": causal.astype(np.float32), "c_pick": e}


class Piece:

    def __init__(self, unit, col, kt, x, k0, mode, slot, first, last, name):
        self.unit, self.col, self.kt, self.x, self.k0 = unit, col, kt, x, k0
        self.mode, self.slot, self.first, self.last, self.name = mode, slot, first, last, name


class Plan:

    def __init__(self):
        self.units = []
        self.pieces = []
        self.tile = {}
        self.unit_end = []
        self.uses = [0, 0]
        self.slot, self.before = [], []
        self.last, self.next_slot = {}, 0

    def unit(self, parts, kt, cols, own_place=False):
        self.units.append((parts, kt, cols))
        self.unit_end.append(0)
        self.before.append(self.last.get(self.next_slot))
        self.slot.append(self.next_slot)
        if own_place:
            self.before[-1] = None
        else:
            self.last[self.next_slot] = len(self.units) - 1
            self.next_slot = 1 - self.next_slot
        return len(self.units) - 1

    def piece(self, name, unit, col, kt, x, mode="full", slot=0, k0=0, first=True, last=True):
        if first:
            self.tile[name] = [slot, 0, self.uses[slot]]
            self.uses[slot] += 1
        self.pieces.append(Piece(unit, col, kt, x, k0, mode, slot, first, last, name))
        self.tile[name][1] = len(self.pieces)
        self.unit_end[unit] = len(self.pieces)


def make_plan():
    pl = Plan()
    n = 0

    def two(names, w, col0, x, kt=KT, mode="full"):
        nonlocal n
        u = pl.unit([(w, 0, col0, 256, 0)], kt, 256)
        for i, name in enumerate(names):
            pl.piece(name, u, 128 * i, kt, x, mode, slot=n % 2)
            n += 1

    def pair(kind, col0, j):
        two([(kind, 2 * j), (kind, 2 * j + 1)], "w_in", col0 + 256 * j, "z")

    def gate(b, j):
        two([("g", b, 2 * j), ("g", b, 2 * j + 1)], "w_in", (G_B, G_A)[b] + 256 * j, "z")

    def branch(b, j):
        two([("y", b, 2 * j), ("y", b, 2 * j + 1)], ("w_branch_b", "w_branch_a")[b], 256 * j, ("ob", "oa")[b], kt=4)

    for j in range(2):
        pair("v", A_V, j)
    for p in range(2):
        pair("q", A_Q, p)
        pair("f", A_F, p)
    for j in range(2):
        pair("pin", B_IN, j)
    pair("q", A_Q, 2)
    pair("f", A_F, 2)
    pl.pool_unit = pl.unit([("w_pool", 0, 0, 512, 0)], 1, 512, own_place=True)
    for j in range(2):
        u = pl.unit([("w_in", 0, A_OG + 256 * j, 256, 0)], KT, 256)
        for m in range(2):
            g = 2 * j + m
            pl.piece(("og", g), u, 128 * m, KT, "z", slot=n % 2)
            pl.piece(("pool", g), pl.pool_unit, 128 * g, 1, "pd", slot=(n + 1) % 2, k0=g)
            n += 1
    pair("q", A_Q, 3)
    pair("f", A_F, 3)
    for j in range(4):
        gate(0, j)
    for j in range(2):
        gate(1, j)
    for j in range(4):
        branch(0, j)
    for j in range(2, 4):
        gate(1, j)
    for j in range(4):
        branch(1, j)
    for j in range(4):
        two([("out", 2 * j), ("out", 2 * j + 1)], "w_out", 256 * j, "z")
    for j in range(FT // 2):
        two([("u", 2 * j), ("u", 2 * j + 1)], "w_up", 256 * j, "z")
        two([("vv", 2 * j), ("vv", 2 * j + 1)], "w_up", D_FF + 256 * j, "z", mode="real")
    for j in range(4):
        for i, (k0, kt) in enumerate(((0, 8), (8, 8), (16, 6))):
            u = pl.unit([("w_down", k0 * P, 256 * j, 256, 0)], kt, 256)
            for m in range(2):
                pl.piece(("dn", 2 * j + m), u, 128 * m, kt, "g", "real", slot=m, k0=k0, first=i == 0, last=i == 2)
    n = 0
    two([("cq", 0), ("cq", 1)], "w_in_2", M_CQ, "z")
    u = pl.unit([("w_in_2", 0, M_CKV, 128, 0)], KT, 128)
    pl.piece(("ckv", 0), u, 0, KT, "z", "full", slot=n % 2)
    n += 1
    h = ROPE // 2
    parts = []
    for c in (0, 128):
        parts.append(("w_in_2", 0, X_F, 64, c))
    for c in (64, 96):
        parts.append(("w_in_2", 0, M_KPE, 32, c))
    for c in (192, 224):
        parts.append(("w_in_2", 0, M_KPE + h, h, c))
        parts.append(("w_in_2", 0, M_KPE, h, c + h))
    u = pl.unit(parts, KT, 256)
    for i in range(2):
        pl.piece(("kpe", i), u, 128 * i, KT, "z", "full", slot=n % 2)
        n += 1
    pl.ukv = pl.unit([("w_ukv_2", 0, 0, 2048, 0)], 1, 2048)
    pl.uq = [pl.unit([("w_uq", 0)], 2, 1024)]
    pl.next_slot = 1 - pl.next_slot
    pl.uq.append(pl.unit([("w_uq", 8)], 2, 1024))
    for i in range(5):
        for j in range(2):
            pl.piece(("mv", i, j), pl.ukv, j, 1, "ckv", "values", slot=j, k0=i)
    for hd in range(HEADS):
        pl.piece(("mq", hd), pl.uq[hd // 8], 128 * (hd % 8), 2, "cq", "real", slot=0)
        pl.piece(("mk", hd), pl.ukv, 128 * hd, 1, "ckv", "full", slot=0)
    n = 0
    for j in range(4):
        two([("mz", 2 * j), ("mz", 2 * j + 1)], "w_in_2", M_Z + 256 * j, "z", mode="real")
    for j in range(4):
        two([("hg", 0, 2 * j), ("hg", 0, 2 * j + 1)], "w_in_2", H_A + 256 * j, "z", mode="real")
        two([("hy", 0, 2 * j), ("hy", 0, 2 * j + 1)], "w_br_mla_2", 256 * j, "y", mode="real512")
    for j in range(4):
        two([("xv", 2 * j), ("xv", 2 * j + 1)], "w_in_2", X_V + 256 * j, "z")
    for j in range(4):
        u1 = pl.unit([("w_in_2", 0, X_Q + 256 * j, 256, 0)], KT, 256)
        u2 = pl.unit([("w_in_2", 0, X_K + 256 * j, 256, 0)], KT, 256)
        for m in range(2):
            pl.piece(("xq", 2 * j + m), u1, 128 * m, KT, "z", "real", slot=0)
            pl.piece(("xk", 2 * j + m), u2, 128 * m, KT, "z", "full", slot=0)
    n = 0
    for j in range(4):
        two([("xz", 2 * j), ("xz", 2 * j + 1)], "w_in_2", X_Z + 256 * j, "z", mode="real")
    for j in range(4):
        two([("hg", 1, 2 * j), ("hg", 1, 2 * j + 1)], "w_in_2", H_B + 256 * j, "z", mode="real")
        two([("hy", 1, 2 * j), ("hy", 1, 2 * j + 1)], "w_br_fox_2", 256 * j, "y", mode="real512")
    for j in range(4):
        u = pl.unit([("w_out_2", 0, 256 * j, 256, 0)], KT, 256)
        for i in range(QB):
            pl.piece(("fin", j, i), u, 0, KT, "mx", "tokens", slot=n % 2, k0=i)
            n += 1
    return pl


def build_program(nc: bass.Bass, a, out):
    pl = make_plan()
    NU = len(pl.units)
    ctx = ExitStack()
    with ctx:
        def at(name, shape, dt, offset):
            size = int(np.prod(shape[1:])) * {F32: 4, F32R: 4, BF16: 2, U8: 1}[dt]
            return nc.alloc_sbuf_tensor_at(name, shape, dt, offset=offset), offset + size

        def sem(name):
            return ctx.enter_context(nc.semaphore(name))

        o = 16512
        raw, hi, lo = [], [], []
        for i in range(2):
            t, o = at(f"raw{i}", [P, 2048], F32, o)
            raw.append(t)
        for i in range(2):
            t, o = at(f"whi{i}", [P, 2048], F32R, o)
            hi.append(t)
        for i in range(2):
            t, o = at(f"wlo{i}", [P, 2048], F32R, o)
            lo.append(t)
        prm, o = at("prm", [P, 256], F32, o)
        ident, o = at("ident", [P, P], F32, o)
        ones, o = at("ones", [P, P], F32, o)
        pair1, o = at("pair1", [P, P], F32, o)
        identb, o = at("identb", [P, P], BF16, o)
        causalb, o = at("causalb", [P, P], BF16, o)
        small, o = at("small", [P, 128], F32, o)
        inv_n, o = at("inv_n", [P, PADC], F32, o)
        pick, o = at("pick", [P, HEADS], F32R, o)
        lvl, o = at("lvl", [P, MASKC], U8, o)
        A = (o + 31) // 32 * 32
        B = A + KT * T * 4
        C = B + 2 * KT * T * 4

        hT, _ = at("hT", [P, KT, T], F32, A)
        mix, _ = at("mix", [P, KT, T], F32, A)
        omla, _ = at("omla", [P, KT, SEQ], F32, A)
        zhi, e = at("zhi", [P, KT, T], F32R, B)
        zlo, _ = at("zlo", [P, KT, T], F32R, e)
        xt, e = at("xt", [P, QB, D], F32, C)
        xm, e = at("xm", [NM, D], F32, e)
        prow, e = at("prow", [P, 2, P], F32, e)
        sq = [None, None]
        sq[0], e = at("sq0", [P, T], F32, e)
        sq[1], e = at("sq1", [P, T], F32, e)
        zt = [None, None]
        zt[0], e = at("zt0", [P, T], F32, e)
        zt[1], e = at("zt1", [P, T], F32, e)
        rb, e = at("rb", [P, T], F32, e)
        cstage, e = at("cstage", [P, P + HEADS + MASKC], F32, e)
        NORM_END = e
        vtok1, e = at("vtok1", [P, 5, 512], F32, C)
        qf = [at(f"qf{i}", [P, 2, T], F32, e + i * 2 * T * 4)[0] for i in range(2)]
        e += 4 * T * 4
        kf = [at(f"kf{i}", [P, 2, T], F32, e + i * 2 * T * 4)[0] for i in range(2)]
        e += 4 * T * 4
        av = [at(f"av{i}", [P, 2, T], F32, e + i * 2 * T * 4)[0] for i in range(2)]
        AVOFF = e
        e += 4 * T * 4
        E = [at(f"E{i}", [P, 2, T], F32, e + i * 2 * T * 4)[0] for i in range(2)]
        e += 4 * T * 4
        rmask, e = at("rmask", [P, T], F32, e)
        og, e = at("og", [P, 4, T], F32, e)
        pin, e = at("pin", [P, 4, T + PADC], F32, e)
        obhi, e = at("obhi", [P, 4, T], F32R, e)
        oblo, e = at("oblo", [P, 4, T], F32R, e)
        oT, e = at("oT", [P, 4, T], F32, e)
        Sc, e = at("Sc", [P, 2, 4, DV], F32, e)
        scT, e = at("scT", [P, 8, P], F32, e)
        sc0, e = at("sc0", [NM, 2, NM], F32, e)
        kdt, e = at("kdt", [P, 2, 4, P], F32, e)
        GOFF = e
        tmp = [at(f"tmp{i}", [P, T], F32, GOFF + (2 + i) * T * 4)[0] for i in range(2)]
        pp = [at(f"pp{i}", [P, T + PADC], F32, GOFF + i * (T + PADC) * 4)[0] for i in range(2)]
        P1_END = GOFF + 4 * T * 4 + 256
        assert P1_END <= nc.sbuf_usable_end, (P1_END, nc.sbuf_usable_end)
        wphi, e2 = at("wphi", [P, 512], F32R, A)
        wplo, e2 = at("wplo", [P, 512], F32R, e2)
        pdhi = [at(f"pdhi{i}", [P, T], F32R, e2 + i * T * 4)[0] for i in range(2)]
        pdlo = [at(f"pdlo{i}", [P, T], F32R, e2 + (2 + i) * T * 4)[0] for i in range(2)]
        assert e2 + 4 * T * 4 <= B
        ga2, _ = at("ga2", [P, 4, T], F32, C)
        ga = lambda k: pin[:, k, 0:T] if k < 4 else ga2[:, k - 4, :]
        oahi, e2 = at("oahi", [P, 4, T], F32R, C + 10240)
        oalo, e2 = at("oalo", [P, 4, T], F32R, e2)
        hT2, _ = at("hT2", [P, KT, T], F32, AVOFF)
        ghi, e = at("ghi", [P, FT, SEQ], F32R, C)
        glo, e = at("glo", [P, FT, SEQ], F32R, e)
        ub = [at(f"ub{i}", [P, T], F32, e + i * T * 4)[0] for i in range(2)]
        e += 2 * T * 4
        cb = [at(f"cb{i}", [P, SEQ], F32, e + i * SEQ * 4)[0] for i in range(2)]
        e += 2 * SEQ * 4
        gt = [at(f"gt{i}", [P, SEQ], F32, e + i * SEQ * 4)[0] for i in range(2)]
        e += 2 * SEQ * 4
        assert e <= nc.sbuf_usable_end, e
        N0 = C + 97728
        nsq = [at(f"nsq{i}", [P, T], F32, N0 + i * T * 4)[0] for i in range(2)]
        nzt = [at(f"nzt{i}", [P, T], F32, N0 + (2 + i) * T * 4)[0] for i in range(2)]
        nrb, e = at("nrb", [P, T], F32, N0 + 4 * T * 4)
        assert e <= nc.sbuf_usable_end, e
        htok, e = at("htok", [P, QB, D], F32, C)
        vtok, e = at("vtok", [P, 5, D], F32, e)
        YOFF = e
        Pm = [at(f"Pm{i}", [P, 1344], F32, e + i * 1344 * 4)[0] for i in range(2)]
        e += 2 * 1344 * 4
        PT = [at(f"PT{i}", [P, 14 * P], F32, e + i * 14 * P * 4)[0] for i in range(2)]
        e += 2 * 14 * P * 4
        cqhi, e = at("cqhi", [P, 2, T], F32R, e)
        cqlo, e = at("cqlo", [P, 2, T], F32R, e)
        ckhi, e = at("ckhi", [P, T], F32R, e)
        cklo, e = at("cklo", [P, T], F32R, e)
        qh = [at(f"qh{i}", [P, SEQ], F32, e + i * SEQ * 4)[0] for i in range(2)]
        e += 2 * SEQ * 4
        kh = [at(f"kh{i}", [P, T], F32, e + i * T * 4)[0] for i in range(2)]
        e += 2 * T * 4
        trig, e = at("trig", [P, 3, T], F32, e)
        cqT, e = at("cqT", [P, 3, T], F32, e)
        nch, e = at("nch", [P, T], F32R, e)
        fgt, _ = at("fgt", [64, 2, T], F32, YOFF)
        assert e <= N0, (e, N0)
        yhi, e = at("yhi", [P, KT, SEQ], F32R, YOFF)
        ylo, e = at("ylo", [P, KT, SEQ], F32R, e)
        MIXOFF = e
        mix2, e = at("mix2", [P, KT, SEQ], F32, e)
        fq, e = at("fq", [P, 2, SEQ], F32, e)
        fk, e = at("fk", [P, 2, T], F32, e)
        assert e <= C + 95616, e - C
        mtok, _ = at("mtok", [P, QB, D], F32, C + 16384)
        fjunk, _ = at("fjunk", [P, 4, QB, 256], F32, YOFF)
        gpost, _ = at("gpost", [P, D], F32, C + 32768)

        PS = ctx.enter_context(nc.psum_tensor("PS", [P, 8, 512], F32))
        el = small[:, 0:8].rearrange("p (h c) -> p h c", h=2)
        lb, omlb, lbe, epst, fbias = small[:, 8:16], small[:, 16:24], small[:, 24:40], small[:, 40:41], small[:, 41:42]
        negmax, rowsum, rinv, ssum, lbt = small[:, 48:56], small[:, 56:64], small[:, 64:68], small[:, 72:76], small[:, 80:96]
        fsum = small[:, 96:112]

        def col(name, k):
            r = ROWS[name][0]
            return prm[:, r + k:r + k + 1]

        w_landed = [sem(f"w_landed{i}") for i in range(2)]
        w_split = sem("w_split")
        pe_mark = sem("pe_mark")
        acc_free = [sem(f"acc_free{i}") for i in range(2)]
        act_step, dve_step = sem("act_step"), sem("dve_step")
        x_in, prm_in, const_in, late_in = sem("x_in"), sem("prm_in"), sem("const_in"), sem("late_in")
        const_ready, prm_turned, prm_ready = sem("const_ready"), sem("prm_turned"), sem("prm_ready")
        x_turned, h_copied = sem("x_turned"), sem("h_copied")
        lb_sub, lb_exp, lb_ready = sem("lb_sub"), sem("lb_exp"), sem("lb_ready")
        v_turned, v_copied = sem("v_turned"), sem("v_copied")
        f_ready, ln_ready, a_ready = sem("f_ready"), sem("ln_ready"), sem("a_ready")
        sub_ready, exp_ready, mul_ready = sem("sub_ready"), sem("exp_ready"), sem("mul_ready")
        qd_exp, qd_ready = sem("qd_exp"), sem("qd_ready")
        kd_turned, kdt_ready, upd_done, s_ready = sem("kd_turned"), sem("kdt_ready"), sem("upd_done"), sem("s_ready")
        sc_done, sc_copied, c0_copied = sem("sc_done"), sem("sc_copied"), sem("c0_copied")
        o_done, o_copied = sem("o_done"), sem("o_copied")
        pd_ready, obhi_ready = sem("pd_ready"), sem("obhi_ready")
        osq, ossd, orn, on_ready, oahi_ready, oa_ready = (sem("osq"), sem("ossd"), sem("orn"), sem("on_ready"),
                                                          sem("oahi_ready"), sem("oa_ready"))
        spilled, h_back = sem("spilled"), sem("h_back")
        mix_ready, mix2_ready = sem("mix_ready"), sem("mix2_ready")
        mixhi_ready, mixz_ready = sem("mixhi_ready"), sem("mixz_ready")
        c_ready, silu_ready, ghi_ready, g_ready = sem("c_ready"), sem("silu_ready"), sem("ghi_ready"), sem("g_ready")
        h1_ready, meta_turned, h1_meta = sem("h1_ready"), sem("meta_turned"), sem("h1_meta")
        ht_turned, ht_copied = sem("ht_turned"), sem("ht_copied")
        fl_ready, fl_abs, cum_ready, kr_ready = sem("fl_ready"), sem("fl_abs"), sem("cum_ready"), sem("kr_ready")
        xv_turned, xv_copied = sem("xv_turned"), sem("xv_copied")
        ysilu, ygt, yhi_r, y_ready = sem("ysilu"), sem("ygt"), sem("yhi_r"), sem("y_ready")
        fmixhi, fmix = sem("fmixhi"), sem("fmix")
        fin_sq, fin_sum, fin_rstd, fin_out, out_done = sem("fin_sq"), sem("fin_sum"), sem("fin_rstd"), sem("fin_out"), sem("out_done")

        class Norm:

            def __init__(self, name, src, K, n, width, sqb, ztb, rbb, gain, dst, lhs=None):
                self.src, self.K, self.n, self.width = src, K, n, width
                self.sqb, self.ztb, self.rbb, self.gain, self.dst = sqb, ztb, rbb, gain, dst
                self.lhs = lhs
                self.sq_ready, self.sq_used = sem(name + "_sq"), sem(name + "_sqd")
                self.rb_ready, self.zt_ready = sem(name + "_rb"), sem(name + "_zt")
                self.zhi_ready, self.z_ready = sem(name + "_zhi"), sem(name + "_z")

        zpair = lambda k: (zhi[:, k, :], zlo[:, k, :])
        h_src = lambda k: hT[:, k, :]
        norm1 = Norm("n1", h_src, KT, T, D, sq, zt, rb, "norm1", zpair)
        norm2 = Norm("n2", h_src, KT, T, D, nsq, nzt, nrb, "norm2", zpair)
        normf = Norm("nf", h_src, KT, T, D, nsq, nzt, nrb, "final", None)
        normp = Norm("np", h_src, KT, T, D, nsq, nzt, nrb, "pre", zpair)
        normq = Norm("nq", lambda k: cqT[:, k, :], 2, T, 256, nsq, nzt, nrb, "qn",
                     lambda k: (cqhi[:, k, :], cqlo[:, k, :]))
        normk = Norm("nk", lambda k: cqT[:, 2, :], 1, T, 128, nsq, nzt, nrb, "kvn", lambda k: (ckhi[:, :], cklo[:, :]))

        class Attn:
            def __init__(self, name):
                self.s_done, self.m_ready = sem(name + "s_done"), sem(name + "m_ready")
                self.p_exp, self.p_ready = sem(name + "p_exp"), sem(name + "p_ready")
                self.g_turned, self.pt_a, self.pt_v = sem(name + "g_turned"), sem(name + "pt_a"), sem(name + "pt_v")
                self.o_done, self.o_ready = sem(name + "o_done"), sem(name + "o_ready")

        mla, fox = Attn("mla_"), Attn("fox_")
        hspill = nc.dram_tensor("hspill", [P, KT * T], F32, kind="Internal").ap()

        def acc_full(name, rows=slice(0, P)):
            s = 2 * pl.tile[name][0]
            return PS[rows, s:s + 2, 0:HALF]

        def acc_real(name, rows=slice(0, P), n=SEQ):
            return PS[rows, 2 * pl.tile[name][0], 0:n]

        def halves(t):
            return t.rearrange("p (a b) -> p a b", a=2)

        def tile_done(eng, name):
            eng.wait_ge(pe_mark, pl.tile[name][1])

        def tile_free(ins, name):
            ins.then_inc(acc_free[pl.tile[name][0]], 1)

        def tile_freed(eng, name):
            slot, _, uses = pl.tile[name]
            eng.wait_ge(acc_free[slot], uses + 1)

        def chunk(c):
            return (0, NM) if c == 0 else (NM + CH * (c - 1), CH)

        order = [(("v", j), []) for j in range(4)] + [(n, []) for n in (("q", 0), ("q", 1), ("f", 0), ("f", 1))]
        qf_tiles = [[("q", 2 * p), ("q", 2 * p + 1), ("f", 2 * p), ("f", 2 * p + 1)] for p in range(4)]
        beside = (qf_tiles[1] + [("pin", g) for g in range(4)], qf_tiles[2] + [("og", g) for g in range(4)],
                  qf_tiles[3] + [("g", 0, k) for k in range(4)],
                  [("g", 0, k) for k in range(4, 8)] + [("g", 1, k) for k in range(4)])
        for p, tiles in enumerate(beside):
            for i, n in enumerate(tiles):
                steps = [(p, i)]
                if i == 0 and p:
                    steps = [(p - 1, 9), (p, 0)]
                elif i == 7:
                    steps = [(p, 7), (p, 8)]
                order.append((n, steps))
                if n[0] == "og":
                    order.append((("pool", n[1]), []))
        order.append((("y", 0, 0), [(3, 9)]))

        ROW_LOADS = (("norm1_g", 0, "norm1"), ("lb_logits", 0, "lb0"), ("b_f", 0, "bf"), ("head_norm_g", 0, "head"),
                     ("pool_scale", 0, "pscale"), ("norm2_g", 0, "norm2"), ("final_norm_g", 0, "final"),
                     ("pre_norm_g_2", 0, "pre"), ("mla_q_norm_g_2", 0, "qn"), ("mla_kv_norm_g_2", 0, "kvn"),
                     ("conv_w", 1, "convw"), ("conv_b", 1, "convb"))
        PRM_DMAS = 16 * len(ROW_LOADS)

        def level_views(t, j):
            half, blk = 1 << j, 2 << j
            if blk <= NM:
                v = t.rearrange("p h (n b) -> p (h n) b", b=blk)
                return v[:, :, 0:half], v[:, :, half:blk], v[:, :, half - 1:half], [P, 2 * T // blk, half]
            v = t[:, :, NM:T].rearrange("p h (n b) -> p h n b", b=blk)
            return v[:, :, :, 0:half], v[:, :, :, half:blk], v[:, :, :, half - 1:half], [P, 2, SEQ // blk, half]

        ATT_OFF = [0, 144, 416, 816]
        ATT_N = [144, 272, 400, 528]
        GROUPS = [[(0, i) for i in range(4)], [(1, i) for i in range(4)], [(2, 1), (2, 2), (2, 3)],
                  [(3, 2), (3, 3), (4, 3)]]
        G_COL = [0, 512, 1024, 1408]

        def s_view(i):
            if i == 3:
                return PS[:, 5:7, 0:264]
            return PS[:, 4 if i % 2 == 0 else 5, 0:ATT_N[i]]

        block = ctx.enter_context(nc.Block())

        @block.sync
        def _(sp):
            for i in range(QB):
                sp.dma_start(xt[:, i, :], a["x"][0, P * i:P * (i + 1), :]).then_inc(x_in, 16)
            sp.dma_start(xm[:, :], a["meta_tokens"]).then_inc(x_in, 16)
            landed = [0, 0]

            def dram(name):
                t = a[name]
                return t if len(t.shape) == 2 else t.rearrange("l k n -> (l k) n")

            def load(u):
                parts, kt, cols = pl.units[u]
                s = u % 2
                if u >= 2:
                    sp.wait_ge(w_split, 2 * (u - 1))
                for part in parts:
                    if part[0] == "w_uq":
                        src = a["w_uq_2"][0].rearrange("(k p) (h c) -> p k h c", p=P, c=QW)
                        dst = raw[s][:, :].rearrange("p (k h c) -> p k h c", k=2, h=8)
                        hs = slice(part[1], part[1] + 8)
                        for k in range(2):
                            for d0, s0, n in ((0, 0, QW), (96, NOPE + 16, 16), (112, NOPE, 16)):
                                sp.dma_start(dst[:, k, :, d0:d0 + n], src[:, k, hs, s0:s0 + n])\
                                  .then_inc(w_landed[s], 16)
                                landed[s] += 16
                        continue
                    name, row0, col0, n, d0 = part
                    if name == "w_pool":
                        src = a["w_pool"][0].rearrange("g c d -> c g d")
                        dst = raw[s][:, 0:512].rearrange("p (g d) -> p g d", g=4)
                    else:
                        src = dram(name)[row0:row0 + kt * P, col0:col0 + n].rearrange("(k p) c -> p k c", p=P)
                        dst = raw[s][:, 0:kt * cols].rearrange("p (k c) -> p k c", k=kt)[:, :, d0:d0 + n]
                    sp.dma_start(dst, src).then_inc(w_landed[s], 16)
                    landed[s] += 16

            spill_at = 3
            back_at = next(p.unit for p in pl.pieces if p.name == ("y", 1, 0))
            meta_at = next(p.unit for p in pl.pieces if p.name == ("dn", 6)) + 2
            gpost_at = next(p.unit for p in pl.pieces if p.name == ("hy", 1, 6))
            for u in range(NU):
                load(u)
                if u == spill_at:
                    sp.wait_ge(norm1.z_ready, KT)
                    sp.dma_start(hspill, hT[:, :, :].rearrange("p k t -> p (k t)")).then_inc(spilled, 16)
                if u == back_at:
                    sp.wait_ge(oa_ready, 4)
                    sp.wait_ge(spilled, 16)
                    sp.dma_start(hT2[:, :, :].rearrange("p k t -> p (k t)"), hspill).then_inc(h_back, 16)
                if u == gpost_at:
                    sp.wait_ge(fox.o_done, HEADS)
                    sp.dma_start(gpost[:, :], a["post_norm_g_2"].broadcast_to([P, D])).then_inc(late_in, 16)
                if u == meta_at:
                    sp.wait_ge(pe_mark, pl.tile[("dn", 7)][1])
                    sp.dma_start(mtok[0:NM, 0, :], a["meta_tokens_2"]).then_inc(late_in, 16)
                    sp.dma_start(trig[:, :, :], a["c_trig"]).then_inc(late_in, 16)
            for i in range(QB):
                sp.wait_ge(fin_out, i + 1)
                sp.dma_start(out[0, P * i:P * (i + 1), :], mtok[:, i, :]).then_inc(out_done, 16)
            sp.wait_ge(out_done, 16 * QB)

        @block.gpsimd
        def _(pool):
            nc.gpsimd.memset(ident[:, :], 0.0).then_inc(const_ready, 1)
            nc.gpsimd.memset(ones[:, :], 1.0).then_inc(const_ready, 1)
            nc.gpsimd.memset(pair1[:, :], 0.0).then_inc(const_ready, 1)
            pool.wait_ge(const_ready, 3)
            nc.gpsimd.affine_select(out=ident[:, :], in_=ident[:, :], compare_op=ALU.not_equal, fill=1.0,
                                    base=0, pattern=[[-1, P]], channel_multiplier=1).then_inc(const_ready, 1)
            pool.wait_ge(const_ready, 4)
            nc.gpsimd.memset(pair1[0:64, 0:64], 1.0).then_inc(const_ready, 1)
            pool.wait_ge(const_ready, 5)
            nc.gpsimd.memset(pair1[64:P, 64:P], 1.0).then_inc(const_ready, 1)
            pool.wait_ge(const_ready, 6)
            landed = [0, 0]
            for u in range(NU):
                parts, kt, cols = pl.units[u]
                s, n = u % 2, kt * cols
                landed[s] += 16 * sum(6 if p[0] == "w_uq" else 1 for p in parts)
                pool.wait_ge(w_landed[s], landed[s])
                if pl.before[u] is not None:
                    pool.wait_ge(pe_mark, pl.unit_end[pl.before[u]])
                hi_, lo_ = hi[pl.slot[u]], lo[pl.slot[u]]
                if u == pl.pool_unit:
                    pool.wait_ge(spilled, 16)
                    hi_, lo_ = wphi, wplo
                nc.gpsimd.tensor_scalar(hi_[:, 0:n], raw[s][:, 0:n], 1.0, 1.0, ALU.mult, ALU.mult)\
                  .then_inc(w_split, 1)
                pool.wait_ge(w_split, 2 * u + 1)
                nc.gpsimd.tensor_tensor(lo_[:, 0:n], raw[s][:, 0:n], hi_[:, 0:n].bitcast(F32), ALU.subtract)\
                  .then_inc(w_split, 1)

        @block.tensor
        def _(pe):
            mm, tr = nc.tensor.matmul, nc.tensor.transpose
            X = {"z": (zhi, zlo), "ob": (obhi, oblo), "oa": (oahi, oalo), "g": (ghi, glo), "cq": (cqhi, cqlo),
                 "y": (yhi, ylo), "mx": (zhi, zlo)}
            at_piece = [0]

            def gemm_pair(names, x_wait):
                parts = [gemm_steps(name) for name in names]
                for k in range(KT):
                    pe.wait_ge(x_wait, k + 1)
                    ends = [step(k) for step in parts]
                for ins in ends:
                    ins.then_inc(pe_mark, 1)

            def gemm(name, x_wait=None):
                step = gemm_steps(name)
                p = pl.pieces[at_piece[0] - 1]
                for k in range(p.kt):
                    if x_wait is not None:
                        pe.wait_ge(x_wait, p.k0 + k + 1)
                    ins = step(k)
                ins.then_inc(pe_mark, 1)

            def gemm_steps(name):
                p = pl.pieces[at_piece[0]]
                assert p.name == name, (p.name, name)
                at_piece[0] += 1
                parts, kt, cols = pl.units[p.unit]
                s = pl.slot[p.unit]
                pe.wait_ge(w_split, 2 * p.unit + 2)
                slot, _, uses = pl.tile[name]
                if p.first and uses:
                    pe.wait_ge(acc_free[slot], uses)
                W = [t[:, 0:kt * cols].rearrange("p (k c) -> p k c", k=kt)
                     for t in ((wphi, wplo) if p.x == "pd" else (hi[s], lo[s]))]

                def step(k):
                    for w, x in ((0, 0), (0, 1), (1, 0)):
                        first = p.first and k == 0 and w == 0 and x == 0
                        last = p.last and k == p.kt - 1 and w == 1
                        if p.mode == "values":
                            t0, _ = chunk(p.k0)
                            lhs = (ckhi, cklo)[x][:, t0:t0 + P]
                            rhs = (hi, lo)[w][s][:, :].rearrange("p (h two c) -> p h two c", two=2, c=64)[
                                :, 8 * p.col:8 * p.col + 8, 1, :]
                            outs = [(PS[:, 2 * slot, :], lhs, rhs)]
                        elif p.mode == "tokens":
                            lhs = X["mx"][x][:, k, P * p.k0:P * p.k0 + P]
                            outs = [(PS[:, 2 * slot, 0:256], lhs, W[w][:, k, :])]
                        else:
                            lhs = W[w][:, k, p.col:p.col + P]
                            if p.x == "pd":
                                xs = (pdhi, pdlo)[x][p.k0 % 2][:, :]
                            elif p.x == "ckv":
                                xs = (ckhi, cklo)[x][:, :]
                            else:
                                xs = X[p.x][x][:, p.k0 + k, :]
                            if p.mode == "full":
                                outs = [(PS[:, 2 * slot + b, 0:HALF], lhs, xs[:, HALF * b:HALF * (b + 1)])
                                        for b in range(2)]
                            else:
                                t0 = NM if p.mode == "real" and p.x != "g" else 0
                                outs = [(PS[:, 2 * slot, :], lhs, xs[:, t0:t0 + SEQ])]
                        for o_, l_, r_ in outs:
                            ins = mm(o_, l_, r_, start=first, stop=last)
                    return ins

                return step

            def stats(n, lhs):
                for k in range(n.K):
                    pe.wait_ge(n.sq_ready, k + 1)
                    for b in range(2):
                        ins = mm(PS[:, 6 + b, 0:HALF], lhs[:, :], n.sqb[k % 2][:, HALF * b:HALF * (b + 1)],
                                 start=k == 0, stop=k == n.K - 1)
                    ins.then_inc(n.sq_used, 1)

            pe.wait_ge(const_ready, 6)
            pe.wait_ge(x_in, 16 * (QB + 1))
            for k in range(KT):
                ins = tr(PS[:, 5, NM * k:NM * (k + 1)], xm[:, P * k:P * (k + 1)], ident[0:NM, 0:NM])
            ins.then_inc(x_turned, 1)
            for k in range(KT):
                if k >= 4:
                    pe.wait_ge(h_copied, k - 4 + 2)
                for i in range(QB):
                    ins = tr(PS[:, k % 4, P * i:P * (i + 1)], xt[:, i, P * k:P * (k + 1)], ident[:, :])
                ins.then_inc(x_turned, 1)
            pe.wait_ge(prm_in, PRM_DMAS)
            tr(PS[:, 4, 0:NROW1], prow[0:NROW1, 0, :], ident[0:NROW1, 0:NROW1])
            tr(PS[:, 4, P:P + NROW2], prow[0:NROW2, 1, :], ident[0:NROW2, 0:NROW2]).then_inc(prm_turned, 1)
            stats(norm1, ones)
            pe.wait_ge(h_copied, KT + 1)

            def turn_values(src, j, turned, copied, tile_name):
                tile_freed(pe, tile_name)
                if j:
                    pe.wait_ge(copied, 2 * j)
                tr(PS[0:NM, 5, 0:P], src[:, 0:NM], ident[:, :])
                for c in range(1, 5):
                    t0, n = chunk(c)
                    ins = tr(PS[:, 4, P * (c - 1):P * c], src[:, t0:t0 + n], ident[:, :])
                ins.then_inc(turned, 1)

            def rec_step(p, i):
                b = 9 * p
                if i == 0:
                    pe.wait_ge(mul_ready, 8 * p + 1)
                    e = E[b % 2]
                    for hh in range(2):
                        bank = 7 - hh
                        if p:
                            if hh == 0:
                                pe.wait_ge(s_ready, 4 * p)
                            pe.wait_ge(o_copied, 5 * p)
                        else:
                            pe.wait_ge(norm1.rb_ready, 1)
                        for c in range(4):
                            t0, n = chunk(c)
                            ins = tr(PS[0:n, bank, P * c:P * (c + 1)], e[:, hh, t0:t0 + n], ident[:, :])
                        ins.then_inc(kd_turned, 1)
                    return
                if 1 <= i <= 7:
                    j = i - 1
                    half, blk = 1 << j, 2 << j
                    e = E[(b + i) % 2]
                    use = 8 * p + j
                    bank = 4 + use % 2
                    pe.wait_ge(mul_ready, 8 * p + i + 1)
                    if use >= 2:
                        pe.wait_ge(sc_copied, use - 1)
                    elif use == 0:
                        pe.wait_ge(v_copied, 8)
                    if blk <= NM:
                        if j == 0:
                            pe.wait_ge(kdt_ready, 2 * p + 2)
                        for hh in range(2):
                            rhs = e[:, hh, 0:NM].rearrange("p (n b) -> p n b", b=blk)[:, :, half:blk]
                            mm(PS[0:NM, 6, 16 * j + 8 * hh:16 * j + 8 * hh + 8].rearrange("p (n b) -> p n b", b=half),
                               e[:, hh, 0:NM], rhs, start=True, stop=True)
                    for hh in range(2):
                        for c in range(1, 5):
                            t0, n = chunk(c)
                            it = 4 * hh + c - 1
                            m = 64 if j == 6 else P
                            rhs = e[:, hh, t0:t0 + n].rearrange("p (n b) -> p n b", b=blk)[:, :, half:blk]
                            ins = mm(PS[0:m, bank, 64 * it:64 * it + 64].rearrange("p (n b) -> p n b", b=half),
                                     e[:, hh, t0:t0 + m], rhs, start=True, stop=True)
                    ins.then_inc(sc_done, 1)
                    if i <= 4:
                        c = i - 1
                        t0, n = chunk(c)
                        if c == 0:
                            pe.wait_ge(kdt_ready, 2 * p + 2)
                        else:
                            pe.wait_ge(s_ready, 4 * p + c)
                        for hh in range(2):
                            h = 2 * p + hh
                            ins = mm(PS[:, 7, 64 * hh:64 * hh + 64], kdt[0:n, hh, c, :],
                                     vtok1[0:n, c, 64 * h:64 * h + 64], start=True, stop=True)
                        ins.then_inc(upd_done, 1)
                    return
                if i == 8:
                    use = 8 * p + 7
                    pe.wait_ge(sc_copied, use - 1)
                    q, k = qf[p % 2], kf[p % 2]
                    for hh in range(2):
                        mm(PS[0:NM, 6, 64 + 16 * hh:80 + 16 * hh], k[:, hh, 0:NM], q[:, hh, 0:NM], start=True, stop=True)
                        for c in range(1, 5):
                            t0, n = chunk(c)
                            it = 4 * hh + c - 1
                            for r in range(2):
                                ins = mm(PS[64 * r:64 * r + 64, 4 + use % 2, 64 * it:64 * it + 64],
                                         k[:, hh, t0 + 64 * r:t0 + 64 * r + 64],
                                         q[:, hh, t0 + 64 * r:t0 + 64 * r + 64], start=True, stop=True)
                    ins.then_inc(sc_done, 1)
                    return
                pe.wait_ge(qd_ready, p + 1)
                e = E[(b + 8) % 2]
                for c in range(5):
                    t0, n = chunk(c)
                    bank = 6 + c % 2
                    if c == 0:
                        pe.wait_ge(c0_copied, p + 1)
                    elif c == 1:
                        pe.wait_ge(s_ready, 4 * p + 4)
                        pe.wait_ge(sc_copied, 8 * p + 8)
                    else:
                        pe.wait_ge(o_copied, 5 * p + c - 1)
                    for hh in range(2):
                        h = 2 * p + hh
                        sc = sc0[:, hh, :] if c == 0 else scT[:, 4 * hh + c - 1, :]
                        dst = PS[64 * hh:64 * hh + 64, bank, 0:n]
                        ins = mm(dst, vtok1[0:n, c, 64 * h:64 * h + 64], sc, start=True, stop=c == 0)
                        if c:
                            ins = mm(dst, Sc[:, hh, c - 1, :], e[:, hh, t0:t0 + n], start=False, stop=True)
                    ins.then_inc(o_done, 1)

            pending = None
            for n, steps in order:
                if n[0] == "pool":
                    pe.wait_ge(pd_ready, n[1] + 1)
                if n == ("v", 0):
                    gemm_pair([("v", 0), ("v", 1)], norm1.z_ready)
                elif n != ("v", 1):
                    gemm(n)
                if pending is not None:
                    j = pending
                    turn_values(E[j % 2][:, 0, :], j, v_turned, v_copied, ("v", j))
                    pending = None
                if n[0] == "v":
                    pending = n[1]
                for p, i in steps:
                    rec_step(p, i)
            for t in range(4):
                for m in range(2):
                    if t + m:
                        gemm(("y", 0, 2 * t + m))
                pe.wait_ge(osq, t + 1)
                if t:
                    pe.wait_ge(orn, t)
                for r in range(2):
                    ins = mm(PS[:, 6 + r, 0:HALF], pair1[:, :], E[0][:, t % 2, HALF * r:HALF * (r + 1)],
                             start=True, stop=True)
                ins.then_inc(ossd, 1)
            for k in range(4, KT):
                gemm(("g", 1, k))
            pe.wait_ge(oa_ready, 4)
            for k in range(KT):
                gemm(("y", 1, k))
            gemm_pair([("out", 0), ("out", 1)], mixz_ready)
            for k in range(2, KT):
                gemm(("out", k))
            stats(norm2, ones)
            for j in range(FT // 2):
                if j == 0:
                    gemm_pair([("u", 0), ("u", 1)], norm2.z_ready)
                else:
                    for m in range(2):
                        gemm(("u", 2 * j + m))
                for m in range(2):
                    gemm(("vv", 2 * j + m))
            pe.wait_ge(g_ready, FT)
            for j in range(4):
                for i in range(3):
                    for m in range(2):
                        gemm(("dn", 2 * j + m))
            stats(normf, ones)
            pe.wait_ge(late_in, 32)
            pe.wait_ge(h1_ready, KT)
            for k in range(KT):
                ins = tr(PS[:, 5, NM * k:NM * (k + 1)], mtok[0:NM, 0, P * k:P * (k + 1)], ident[0:NM, 0:NM])
            ins.then_inc(meta_turned, 1)
            stats(normp, ones)
            def turn_h(*rs):
                for r in rs:
                    if r >= 2:
                        pe.wait_ge(ht_copied, r - 1)
                    for k in range(4):
                        ins = tr(PS[:, 4 + r % 2, P * k:P * (k + 1)],
                                 hT[:, 4 * (r % 2) + k, NM + P * (r // 2):NM + P * (r // 2 + 1)], ident[:, :])
                    ins.then_inc(ht_turned, 1)

            gemm_pair([("cq", 0), ("cq", 1)], normp.z_ready)
            pe.wait_ge(h1_meta, 1)
            turn_h(0, 1)
            turn_h(2, 3)
            gemm(("ckv", 0))
            stats(normq, ones)
            gemm(("kpe", 0))
            pe.wait_ge(normq.rb_ready, 1)
            stats(normk, ones)
            turn_h(4, 5)
            gemm(("kpe", 1))
            turn_h(6, 7)
            pe.wait_ge(ht_copied, 8)
            for i in range(5):
                for j in range(2):
                    gemm(("mv", i, j), normk.z_ready if i + j == 0 else None)

            def scores(A, h, i):
                if 4 * h + i >= 2:
                    pe.wait_ge(A.p_exp, 4 * h + i - 1)
                if i == 0:
                    tile_freed(pe, ("mk", h) if A is mla else ("xk", h // 2))
                t0, n = P * i, ATT_N[i]
                if i == 3:
                    cuts, tail = [(PS[:, 5, 0:264], 0), (PS[:, 6, 0:136], 264)], PS[:, 6, 136:264]
                else:
                    bank = 4 if i % 2 == 0 else 5
                    cuts, tail = [(PS[:, bank, 0:n - P], 0)], PS[:, bank, n - P:n]
                for dst, c0 in cuts + [(tail, n - P)]:
                    last = dst is tail
                    c1 = c0 + dst.shape[-1]
                    if A is mla:
                        ins = mm(dst, qh[h % 2][:, t0:t0 + P], kh[h % 2][:, c0:c1], start=True, stop=not last)
                    else:
                        r, m = 64 * (h % 2), (h // 2) % 2
                        mm(dst, fq[r:r + 64, m, t0:t0 + P], fk[r:r + 64, m, c0:c1], start=True, stop=False)
                        ins = mm(dst, pick[:, h:h + 1].broadcast_to([P, P]), nch[:, c0:c1], start=False,
                                 stop=not last)
                    if last:
                        ins = mm(dst, identb[:, :], causalb[:, :], start=False, stop=True)
                ins.then_inc(A.s_done, 1)

            def turn(A, h, g):
                if g == 0:
                    pe.wait_ge(A.p_ready, h + 1)
                done = A.pt_a if g % 2 == 0 else A.pt_v
                if 2 * h + g // 2:
                    pe.wait_ge(done, 2 * h + g // 2)
                for x, (j, i) in enumerate(GROUPS[g]):
                    o_ = ATT_OFF[i] + (0 if j == 0 else NM + P * (j - 1))
                    n = NM if j == 0 else P
                    ins = tr(PS[0:n, 2 + g % 2, P * x:P * (x + 1)], Pm[h % 2][:, o_:o_ + n], ident[:, :])
                ins.then_inc(A.g_turned, 1)

            def weigh(A, h):
                pe.wait_ge(A.pt_a, 2 * h + 2)
                pe.wait_ge(A.pt_v, 2 * h + 2)
                if h:
                    pe.wait_ge(A.o_ready, h)
                r = 64 * (h % 2)
                for j, (c0, q0, n) in enumerate(((0, 0, 512), (512, 0, 512), (1024, 128, 384), (1408, 256, 256),
                                                 (1664, 384, 128))):
                    rows = NM if j == 0 else P
                    ins = mm(PS[r:r + 64, 7, q0:q0 + n], vtok[0:rows, j, 64 * h:64 * h + 64],
                             PT[h % 2][0:rows, c0:c0 + n], start=j == 0, stop=j == 4, skip_group_check=True)
                ins.then_inc(A.o_done, 1)

            def attention(A, project, between):
                for h in range(HEADS + 2):
                    project(h)
                    if h < HEADS:
                        scores(A, h, 0)
                    if h >= 2:
                        weigh(A, h - 2)
                    if h < HEADS:
                        scores(A, h, 1)
                    if 1 <= h <= HEADS:
                        turn(A, h - 1, 0)
                    between(h)
                    for i in range(1, 4):
                        if 1 <= h <= HEADS:
                            turn(A, h - 1, i)
                        if h < HEADS and i < 3:
                            scores(A, h, i + 1)

            def mla_project(h):
                for x in ([0, 1] if h == 0 else [h + 1]):
                    if x < HEADS:
                        gemm(("mq", x), normq.z_ready if x == 0 else None)
                        if h == 0:
                            gemm(("mk", x))

            def mla_between(h):
                if 1 <= h < HEADS - 1:
                    gemm(("mk", h + 1))

            pe.wait_ge(kr_ready, 1)
            for i, j in ((4, 0), (4, 1)):
                tile_freed(pe, ("mv", i, j))
            attention(mla, mla_project, mla_between)
            pe.wait_ge(mla.pt_a, 2 * HEADS)
            pe.wait_ge(mla.pt_v, 2 * HEADS)
            for k in range(KT):
                gemm(("mz", k))

            def gates(b):
                for j in range(4):
                    for m in range(2):
                        gemm(("hg", b, 2 * j + m))
                    if j == 0:
                        pe.wait_ge(y_ready, KT * (b + 1))
                    for m in range(2):
                        gemm(("hy", b, 2 * j + m))

            gates(0)
            for k in range(KT):
                gemm(("xv", k))
                if k:
                    turn_values(nzt[(k - 1) % 2][:, :], k - 1, xv_turned, xv_copied, ("xv", k - 1))
            turn_values(nzt[(KT - 1) % 2][:, :], KT - 1, xv_turned, xv_copied, ("xv", KT - 1))
            pe.wait_ge(xv_copied, 2 * KT)

            pe.wait_ge(cum_ready, 1)

            def fox_project(h):
                if h == 0:
                    gemm(("xq", 0))
                    gemm(("xk", 0))

            def fox_between(h):
                if h < HEADS - 2:
                    gemm((("xq", "xk")[h % 2], h // 2 + 1))

            pe.wait_ge(acc_free[1], pl.tile[("xv", KT - 1)][2] + 1)
            attention(fox, fox_project, fox_between)
            pe.wait_ge(fox.pt_a, 2 * HEADS)
            pe.wait_ge(fox.pt_v, 2 * HEADS)
            for k in range(KT):
                gemm(("xz", k))
            gates(1)
            gemm_pair([("fin", 0, 0), ("fin", 0, 1)], fmix)
            for j in range(4):
                for i in range(QB):
                    if j or i >= 2:
                        gemm(("fin", j, i))
            assert at_piece[0] == len(pl.pieces)

        @block.scalar
        def _(act):
            A_ = nc.scalar.activation
            steps = [0]

            def tick(ins):
                steps[0] += 1
                ins.then_inc(act_step, 1)

            def settle():
                act.wait_ge(act_step, steps[0])

            for name, half, dst in ROW_LOADS:
                src = a[name]
                flat = {1: "(t p) -> t p", 2: "l (t p) -> (l t) p", 3: "l w (t p) -> (l w t) p"}[len(src.shape)]
                r0, n = ROWS[dst]
                n = 16 if name == "lb_logits" else n
                r0 -= P * half
                act.dma_start(prow[r0:r0 + n, half, :], src.rearrange(flat, p=P)).then_inc(prm_in, 16)
            act.dma_start(cstage[:, 0:P], a["c_causal"]).then_inc(const_in, 16)
            act.dma_start(cstage[:, P:P + HEADS], a["c_pick"]).then_inc(const_in, 16)
            act.dma_start(cstage[:, P + HEADS:], a["c_level"]).then_inc(const_in, 16)
            act.dma_start(inv_n[:, :], a["c_inv"]).then_inc(const_in, 16)
            with nc.allow_non_contiguous_dma(reason="sixteen biases, one for each of sixteen partitions"):
                act.dma_start(fbias[0:HEADS, :], a["fox_forget_b_2"].rearrange("l (h o) -> (l h) o", o=1))\
                   .then_inc(const_in, 16)

            def norm_sq(n, k):
                if k >= 2:
                    act.wait_ge(n.sq_used, k - 1)
                A_(n.sqb[k % 2][:, :], n.src(k), ACT.Square).then_inc(n.sq_ready, 1)

            def norm_rb(n):
                act.wait_ge(n.sq_used, n.K)
                tick(A_(halves(n.rbb[:, :]), PS[:, 6:8, 0:HALF], ACT.Ln, scale=1.0 / n.width, bias=epst))
                settle()
                A_(n.rbb[:, :], n.rbb[:, :], ACT.Exp, scale=-0.5).then_inc(n.rb_ready, 1)

            def norm_hi(n, k):
                act.wait_ge(n.zt_ready, k + 1)
                A_(n.dst(k)[0], n.ztb[k % 2][:, :], ACT.Copy).then_inc(n.zhi_ready, 1)

            for k in range(KT):
                act.wait_ge(h_copied, k + 2)
                norm_sq(norm1, k)
            act.wait_ge(lb_sub, 1)
            A_(lbe, lbt, ACT.Exp).then_inc(lb_exp, 1)
            norm_rb(norm1)
            for k in range(KT):
                norm_hi(norm1, k)

            def rec_step(p, i):
                b = 9 * p

                def level_exp(x):
                    act.wait_ge(sub_ready, 8 * p + x + 1)
                    t = E[(b + x) % 2]
                    v = t[:, :, 0:400] if x == 0 else t[:, :, NM:T] if x - 1 >= 4 else t[:, :, :]
                    A_(v, v, ACT.Exp).then_inc(exp_ready, 1)

                if i == 0:
                    act.wait_ge(a_ready, 2 * p + 2)
                    if p:
                        act.wait_ge(s_ready, 4 * p)
                    tick(A_(el, av[p % 2][:, :, NM - 1:400:P], ACT.Exp))
                    level_exp(0)
                elif i <= 6:
                    level_exp(i + 1)
                elif i == 7:
                    act.wait_ge(sc_done, 8 * p + 6)
                    A_(E[(b + 8) % 2][:, :, :], av[p % 2][:, :, :], ACT.Exp).then_inc(qd_exp, 1)
                elif i == 9:
                    for c in range(5):
                        t0, n = chunk(c)
                        act.wait_ge(o_done, 5 * p + c + 1)
                        A_(oT[:, p, t0:t0 + n], PS[:, 6 + c % 2, 0:n], ACT.Copy).then_inc(o_copied, 1)

            def rec_after(p):
                act.wait_ge(sub_ready, 8 * p + 2)
                t = E[(9 * p + 1) % 2][:, :, :]
                A_(t, t, ACT.Exp).then_inc(exp_ready, 1)
                for hh in range(2):
                    act.wait_ge(kd_turned, 2 * p + hh + 1)
                    tick(A_(kdt[0:NM, hh, 0, :], PS[0:NM, 7 - hh, 0:P], ACT.Copy))
                    A_(kdt[:, hh, 1:4, :], PS[:, 7 - hh, P:4 * P].rearrange("p (c k) -> p c k", c=3), ACT.Copy)\
                        .then_inc(kdt_ready, 1)

            for name, hooks in order:
                kind, h = name[0:2]
                p, hh = h // 2, h % 2
                for step in sorted(hooks, reverse=True):
                    rec_step(*step)
                if kind == "y":
                    continue
                tile_done(act, name)
                src = acc_full(name)
                if kind == "v":
                    if h >= 2:
                        act.wait_ge(v_turned, h - 1)
                    tile_free(A_(halves(E[h % 2][:, 0, :]), src, ACT.Copy), name)
                elif kind == "q":
                    if p >= 2:
                        act.wait_ge(o_done, 5 * (p - 1))
                    tile_free(A_(halves(qf[p % 2][:, hh, :]), src, ACT.Silu), name)
                elif kind == "f":
                    if p >= 2:
                        act.wait_ge(o_done, 5 * (p - 1))
                    tile_free(A_(halves(kf[p % 2][:, hh, :]), src, ACT.Sigmoid, bias=col("bf", h)), name)
                    act.wait_ge(f_ready, h + 1)
                    t = av[p % 2][:, hh, :]
                    A_(t, t, ACT.Ln).then_inc(ln_ready, 1)
                elif kind == "og":
                    tile_free(A_(halves(og[:, h, :]), src, ACT.Silu), name)
                elif kind == "pool":
                    A_(halves(obhi[:, h, :]), src, ACT.Copy, scale=col("pscale", h)).then_inc(obhi_ready, 1)
                elif kind == "g":
                    if name == ("g", 0, 0):
                        tile_done(act, ("pool", 3))
                    if name == ("g", 1, 0):
                        act.wait_ge(pd_ready, 4)
                    dst = mix[:, name[2], :] if h == 0 else ga(name[2])
                    tile_free(A_(halves(dst), src, ACT.Sigmoid), name)
                else:
                    tile_free(A_(halves(pin[:, h, PADC:]), src, ACT.Copy), name)
                if hooks and hooks[-1][1] == 0:
                    rec_after(hooks[-1][0])

            act.wait_ge(o_copied, 20)
            for t in range(2):
                A_(E[0][:, t, :], oT[:, t, :], ACT.Square).then_inc(osq, 1)
            for t in range(4):
                act.wait_ge(ossd, t + 1)
                if t >= 2:
                    act.wait_ge(on_ready, t - 1)
                tick(A_(halves(E[1][:, t % 2, :]), PS[:, 6:8, 0:HALF], ACT.Ln, scale=1.0 / A_VDIM, bias=epst))
                settle()
                A_(E[1][:, t % 2, :], E[1][:, t % 2, :], ACT.Exp, scale=-0.5).then_inc(orn, 1)
                act.wait_ge(on_ready, t + 1)
                A_(oahi[:, t, :], oT[:, t, :], ACT.Copy).then_inc(oahi_ready, 1)
                if t < 2:
                    A_(E[0][:, t, :], oT[:, t + 2, :], ACT.Square).then_inc(osq, 1)
            for k in range(4, KT):
                tile_done(act, ("g", 1, k))
                tile_free(A_(halves(ga(k)), acc_full(("g", 1, k)), ACT.Sigmoid), ("g", 1, k))

            for k in range(KT):
                act.wait_ge(mix_ready, k + 1)
                A_(zhi[:, k, :], mix[:, k, :], ACT.Copy).then_inc(mixhi_ready, 1)
            for k in range(KT):
                tile_freed(act, ("out", k))
                norm_sq(norm2, k)
            norm_rb(norm2)
            for k in range(KT):
                norm_hi(norm2, k)

            for j in range(FT // 2):
                for k in (2 * j, 2 * j + 1):
                    tile_done(act, ("u", k))
                    if k >= 2:
                        act.wait_ge(c_ready, k - 1)
                    tile_free(A_(halves(ub[k % 2][:, :]), acc_full(("u", k)), ACT.Copy), ("u", k))
                for k in (2 * j, 2 * j + 1):
                    act.wait_ge(c_ready, k + 1)
                    A_(cb[k % 2][:, :], cb[k % 2][:, :], ACT.Silu).then_inc(silu_ready, 1)
                for k in (2 * j, 2 * j + 1):
                    tile_freed(act, ("vv", k))
                    A_(ghi[:, k, :], gt[k % 2][:, :], ACT.Copy).then_inc(ghi_ready, 1)

            for k in range(KT):
                tile_freed(act, ("dn", k))
                norm_sq(normf, k)
            norm_rb(normf)
            act.wait_ge(h1_meta, 1)
            for k in range(KT):
                act.wait_ge(h1_ready, k + 1)
                norm_sq(normp, k)
            norm_rb(normp)
            for k in range(KT):
                norm_hi(normp, k)

            def h_out(*rs):
                for r in rs:
                    act.wait_ge(ht_turned, r + 1)
                    A_(htok[:, r // 2, SEQ * (r % 2):SEQ * (r % 2 + 1)], PS[:, 4 + r % 2, :], ACT.Copy)\
                        .then_inc(ht_copied, 1)

            def compressed(k, name):
                tile_done(act, name)
                tile_free(A_(halves(cqT[:, k, :]), acc_full(name), ACT.Copy), name)
                tile_freed(act, name)

            for k in range(2):
                compressed(k, ("cq", k))
                norm_sq(normq, k)
                h_out(2 * k, 2 * k + 1)
            compressed(2, ("ckv", 0))
            norm_rb(normq)
            norm_sq(normk, 0)
            act.wait_ge(normq.zt_ready, 2)
            norm_rb(normk)
            for k in range(2):
                norm_hi(normq, k)
            norm_hi(normk, 0)
            h_out(4, 5)
            tile_done(act, ("kpe", 0))
            f0, f1 = fgt[0:HEADS, 0, :], fgt[0:HEADS, 1, :]
            A_(halves(f0), acc_full(("kpe", 0), slice(0, HEADS)), ACT.Identity, bias=fbias[0:HEADS, :])\
                .then_inc(fl_ready, 1)
            act.wait_ge(fl_ready, 1)
            tick(A_(f1, f0, ACT.Abs))
            settle()
            tick(A_(f1, f1, ACT.Exp, scale=-1.0))
            settle()
            A_(f1, f1, ACT.Ln, bias=ones[0:HEADS, 0:1]).then_inc(fl_abs, 1)
            h_out(6, 7)

            def k_out(x):
                tile_done(act, ("mk", x))
                if x >= 2:
                    act.wait_ge(mla.s_done, 4 * (x - 1))
                tile_free(A_(halves(kh[x % 2][0:NOPE, :]), acc_full(("mk", x), slice(0, NOPE)), ACT.Copy), ("mk", x))

            def attention(A, project, between):
                for h in range(HEADS + 2):
                    project(h)
                    for i in range(4):
                        if h < HEADS:
                            if h >= 2 and i == 0:
                                act.wait_ge(A.g_turned, 4 * (h - 1))
                            act.wait_ge(A.m_ready, 4 * h + i + 1)
                            s = 4 * (h % 2) + i
                            dst = Pm[h % 2][:, ATT_OFF[i]:ATT_OFF[i] + ATT_N[i]]
                            dst = halves(dst) if i == 3 else dst
                            A_(dst, s_view(i), ACT.Exp, bias=negmax[:, s:s + 1],
                               accum_out=rowsum[:, s:s + 1]).then_inc(A.p_exp, 1)
                        if h >= 2 and i == 0:
                            x, r = h - 2, 64 * (h % 2)
                            act.wait_ge(A.o_done, x + 1)
                            A_(omla[r:r + 64, x // 2, :], PS[r:r + 64, 7, :], ACT.Copy).then_inc(A.o_ready, 1)
                        if 1 <= h <= HEADS and i in (1, 2):
                            x, g = h - 1, 2 * i - 2
                            act.wait_ge(A.g_turned, 4 * x + g + 1)
                            if x >= 2:
                                act.wait_ge(A.o_done, x - 1)
                            rows, n = (NM, 512) if g == 0 else (P, 384)
                            A_(PT[x % 2][0:rows, G_COL[g]:G_COL[g] + n], PS[0:rows, 2, 0:n], ACT.Copy)\
                                .then_inc(A.pt_a, 1)
                        if i == 1:
                            between(h)

            def mla_project(h):
                if h == 0:
                    k_out(0)
                    k_out(1)

            def mla_between(h):
                if 1 <= h < HEADS - 1:
                    k_out(h + 1)

            attention(mla, mla_project, mla_between)

            def gated(kind, A, b):
                act.wait_ge(A.o_ready, HEADS)
                for k in range(KT):
                    tile_done(act, (kind, k))
                    if k >= 2:
                        act.wait_ge(ygt, KT * b + k - 1)
                    tile_free(A_(nsq[k % 2][:, 0:SEQ], acc_real((kind, k)), ACT.Silu), (kind, k))
                    act.wait_ge(ygt, KT * b + k + 1)
                    A_(yhi[:, k, :], nzt[k % 2][:, 0:SEQ], ACT.Copy).then_inc(yhi_r, 1)

            def gates(b):
                act.wait_ge(y_ready, KT * (b + 1))
                for k in range(KT):
                    if k >= 2:
                        tile_freed(act, ("hy", b, k - 2))
                    tile_done(act, ("hg", b, k))
                    tile_free(A_(nsq[k % 2][:, 0:SEQ], acc_real(("hg", b, k)), ACT.Sigmoid), ("hg", b, k))

            gated("mz", mla, 0)
            gates(0)
            for k in range(KT):
                tile_done(act, ("xv", k))
                if k >= 2:
                    act.wait_ge(xv_turned, k - 1)
                tile_free(A_(halves(nzt[k % 2][:, :]), acc_full(("xv", k)), ACT.Copy), ("xv", k))

            def fq_out(x):
                tile_done(act, ("xq", x))
                if x >= 2:
                    act.wait_ge(fox.s_done, 4 * (2 * x - 2))
                tile_free(A_(fq[:, x % 2, :], acc_real(("xq", x)), ACT.Copy, scale=FOX_SCALE), ("xq", x))

            def fk_out(x):
                tile_done(act, ("xk", x))
                tile_free(A_(halves(fk[:, x % 2, :]), acc_full(("xk", x)), ACT.Copy), ("xk", x))

            def fox_project(h):
                if h == 0:
                    fq_out(0)
                    fk_out(0)

            def fox_between(h):
                if h < HEADS - 2:
                    (fq_out, fk_out)[h % 2](h // 2 + 1)

            attention(fox, fox_project, fox_between)
            gated("xz", fox, 1)
            gates(1)
            tile_done(act, ("hg", 1, 7))
            for k in range(KT):
                act.wait_ge(mix2_ready, k + 1)
                A_(zhi[:, k, 0:SEQ], mix2[:, k, :], ACT.Copy).then_inc(fmixhi, 1)
            for j in range(4):
                for i in range(QB):
                    n = ("fin", j, i)
                    tile_done(act, n)
                    A_(fjunk[:, j, i, :], acc_real(n, n=256), ACT.Square, accum_out=fsum[:, 4 * i + j:4 * i + j + 1])\
                        .then_inc(fin_sq, 1)
            act.wait_ge(fin_sum, 1)
            tick(A_(ssum, ssum, ACT.Ln, scale=1.0 / D, bias=epst))
            settle()
            A_(ssum, ssum, ACT.Exp, scale=-0.5).then_inc(fin_rstd, 1)

        @block.vector
        def _(dve):
            V = nc.vector
            steps = [0]

            def tick(ins):
                steps[0] += 1
                ins.then_inc(dve_step, 1)

            def settle():
                dve.wait_ge(dve_step, steps[0])

            tick(V.memset(epst, EPS))
            tick(V.memset(rmask[:, :], 1.0))
            tick(V.memset(pin[:, :, 0:PADC], 0.0))
            tick(V.memset(scT[:, :, :], 0.0))
            tick(V.memset(sc0[:, :, :], 0.0))
            settle()
            for c in range(5):
                tick(V.memset(rmask[:, chunk(c)[0]:chunk(c)[0] + 1], 0.0))
            dve.wait_ge(x_turned, 1)
            V.tensor_copy(hT[:, :, 0:NM], PS[:, 5, 0:P].rearrange("p (k t) -> p k t", k=KT)).then_inc(h_copied, 1)
            for k in range(KT):
                dve.wait_ge(x_turned, k + 2)
                V.tensor_copy(hT[:, k, NM:T], PS[:, k % 4, :]).then_inc(h_copied, 1)
            dve.wait_ge(prm_turned, 1)
            tick(V.tensor_copy(prm[:, 0:NROW1], PS[:, 4, 0:NROW1]))
            tick(V.tensor_copy(prm[:, P:P + NROW2], PS[:, 4, P:P + NROW2]))
            settle()
            l0, l1 = prm[:, 8:16], prm[:, 16:24]
            tick(V.tensor_tensor(lb, l0, l1, ALU.max))
            settle()
            tick(V.tensor_tensor(lbt[:, 0:8], l0, lb, ALU.subtract))
            V.tensor_tensor(lbt[:, 8:16], l1, lb, ALU.subtract).then_inc(lb_sub, 1)
            dve.wait_ge(lb_exp, 1)
            tick(V.tensor_tensor(omlb, lbe[:, 0:8], lbe[:, 8:16], ALU.add))
            settle()
            tick(V.reciprocal(omlb, omlb))
            settle()
            tick(V.tensor_tensor(lb, lbe[:, 0:8], omlb, ALU.mult))
            settle()
            tick(V.tensor_scalar(lb, lb, 2.0 ** -63, None, ALU.max))
            settle()
            tick(V.tensor_scalar(omlb, lb, -1.0, 1.0, ALU.mult, ALU.add))
            dve.wait_ge(const_in, 16 * 5)
            dve.wait_ge(const_ready, 6)
            tick(V.tensor_copy(causalb[:, :], cstage[:, 0:P]))
            tick(V.tensor_copy(identb[:, :], ident[:, :]))
            tick(V.tensor_copy(pick[:, :], cstage[:, P:P + HEADS]))
            tick(V.tensor_copy(lvl[:, :], cstage[:, P + HEADS:]))
            settle()

            def norm_zt(n, k):
                if k == 0:
                    dve.wait_ge(n.rb_ready, 1)
                V.scalar_tensor_tensor(out=n.ztb[k % 2][:, :], in0=n.src(k), scalar=col(n.gain, k),
                                       in1=n.rbb[:, :], op0=ALU.mult, op1=ALU.mult).then_inc(n.zt_ready, 1)

            def norm_lo(n, k):
                dve.wait_ge(n.zhi_ready, k + 1)
                h_, l_ = n.dst(k)
                V.tensor_tensor(l_, n.ztb[k % 2][:, :], h_.bitcast(F32), ALU.subtract).then_inc(n.z_ready, 1)

            def norm_split(n):
                for k in range(n.K + 1):
                    if k < n.K:
                        if k >= 2:
                            dve.wait_ge(n.z_ready, k - 1)
                        norm_zt(n, k)
                    if k >= 1:
                        norm_lo(n, k - 1)

            norm_split(norm1)

            def values_out(j, turned, copied, dst):
                dve.wait_ge(turned, j + 1)
                V.tensor_copy(dst[0:NM, 0, P * j:P * (j + 1)], PS[0:NM, 5, 0:P]).then_inc(copied, 1)
                V.tensor_copy(dst[:, 1:5, P * j:P * (j + 1)], PS[:, 4, :].rearrange("p (c f) -> p c f", c=4))\
                 .then_inc(copied, 1)

            def rec_step(p, i):
                b = 9 * p
                q, kk, ac = qf[p % 2], kf[p % 2], av[p % 2]

                def free(x):
                    if x == 0:
                        if p:
                            dve.wait_ge(sc_done, 8 * p - 1)
                        else:
                            dve.wait_ge(v_turned, 4)
                    elif x == 1:
                        if p:
                            dve.wait_ge(o_done, 5 * p)
                    elif x == 2:
                        dve.wait_ge(kd_turned, 2 * p + 2)
                    else:
                        dve.wait_ge(sc_done, 8 * p + x - 2)

                def sub(x):
                    free(x)
                    t = E[(b + x) % 2]
                    if x == 0:
                        dve.wait_ge(a_ready, 2 * p + 2)
                        tick(V.tensor_tensor(t[:, :, 0:NM], ac[:, :, NM - 1:NM].broadcast_to([P, 2, NM]),
                                             ac[:, :, 0:NM], ALU.subtract))
                        sv = lambda z: z[:, :, NM:400].rearrange("p h (c t) -> p h c t", t=CH)
                        V.tensor_tensor(sv(t), sv(ac)[:, :, :, CH - 1:CH].broadcast_to([P, 2, 3, CH]), sv(ac),
                                        ALU.subtract).then_inc(sub_ready, 1)
                        return
                    tl, tr_, _, shape = level_views(t, x - 1)
                    al, ar, mid, _ = level_views(ac, x - 1)
                    tick(V.tensor_tensor(tl, mid.broadcast_to(shape), al, ALU.subtract))
                    V.tensor_tensor(tr_, ar, mid.broadcast_to(shape), ALU.subtract).then_inc(sub_ready, 1)

                def mul(x):
                    dve.wait_ge(exp_ready, 8 * p + x + 1)
                    t = E[(b + x) % 2]
                    if x == 0:
                        V.tensor_tensor(t[:, :, 0:400], t[:, :, 0:400], kk[:, :, 0:400], ALU.mult).then_inc(mul_ready, 1)
                        return
                    tl, tr_, _, _ = level_views(t, x - 1)
                    ql = level_views(q, x - 1)[1]
                    kl = level_views(kk, x - 1)[0]
                    tick(V.tensor_tensor(tr_, tr_, ql, ALU.mult))
                    V.tensor_tensor(tl, tl, kl, ALU.mult).then_inc(mul_ready, 1)

                def evac(j):
                    use = 8 * p + j
                    bank = 4 + use % 2
                    dve.wait_ge(sc_done, use + 1)
                    if use:
                        dve.wait_ge(sc_copied, use)
                    if j == 0 and p:
                        dve.wait_ge(o_done, 5 * p)
                    if j == 6:
                        V.tensor_copy(scT[0:64, :, 64:P], PS[0:64, bank, :].rearrange("p (i t) -> p i t", i=8))\
                         .then_inc(sc_copied, 1)
                        return
                    if j == 7:
                        for r in range(2):
                            rows = slice(64 * r, 64 * r + 64)
                            ins = V.copy_predicated(scT[rows, :, 64 * r:64 * r + 64],
                                                    lvl[rows, 448:512].unsqueeze(1).broadcast_to([64, 8, 64]),
                                                    PS[rows, bank, :].rearrange("p (i t) -> p i t", i=8))
                            if r == 0:
                                tick(ins)
                        ins.then_inc(sc_copied, 1)
                        return
                    half, blk = 1 << j, 2 << j
                    n = P // blk
                    m = lvl[:, 64 * j:64 * j + 64].rearrange("p (n b) -> p n b", b=half).unsqueeze(1)
                    V.copy_predicated(scT[:, :, :].rearrange("p i (n b) -> p i n b", b=blk)[:, :, :, half:blk],
                                      m.broadcast_to([P, 8, n, half]),
                                      PS[:, bank, :].rearrange("p (i n b) -> p i n b", i=8, b=half)).then_inc(sc_copied, 1)

                def state(c):
                    dve.wait_ge(upd_done, 4 * p + c + 1)
                    if c == 0:
                        V.tensor_copy(Sc[:, :, 0, :], PS[:, 7, 0:P].rearrange("p (h v) -> p h v", h=2)).then_inc(s_ready, 1)
                        return
                    dve.wait_ge(s_ready, 4 * p + c)
                    for hh in range(2):
                        ins = V.scalar_tensor_tensor(out=Sc[:, hh, c, :], in0=Sc[:, hh, c - 1, :], scalar=el[:, hh, c:c + 1],
                                                     in1=PS[:, 7, 64 * hh:64 * hh + 64], op0=ALU.mult, op1=ALU.add)
                        if hh == 0:
                            tick(ins)
                    ins.then_inc(s_ready, 1)

                if i == 0:
                    for hh in range(2):
                        tile_freed(dve, ("q", 2 * p + hh))
                    sub(0)
                    mul(0)
                    sub(1)
                elif i <= 7:
                    if 2 <= i <= 5:
                        state(i - 2)
                    if i <= 6:
                        sub(i + 1)
                    mul(i)
                    if i >= 2:
                        evac(i - 2)
                elif i == 9:
                    evac(6)
                    dve.wait_ge(qd_exp, p + 1)
                    t = E[(b + 8) % 2]
                    V.tensor_tensor(t[:, :, :], t[:, :, :], q[:, :, :], ALU.mult).then_inc(qd_ready, 1)
                    evac(7)
                    for j in range(4):
                        half, blk = 1 << j, 2 << j
                        n = NM // blk
                        m = lvl[0:NM, 64 * j:64 * j + 8].rearrange("p (n b) -> p n b", b=half).unsqueeze(1)
                        tick(V.copy_predicated(
                            sc0[:, :, :].rearrange("p i (n b) -> p i n b", b=blk)[:, :, :, half:blk],
                            m.broadcast_to([NM, 2, n, half]),
                            PS[0:NM, 6, 16 * j:16 * j + 16].rearrange("p (i n b) -> p i n b", i=2, b=half)))
                        settle()
                    V.copy_predicated(sc0[:, :, :], lvl[0:NM, 448:464].unsqueeze(1).broadcast_to([NM, 2, NM]),
                                      PS[0:NM, 6, 64:96].rearrange("p (i t) -> p i t", i=2)).then_inc(c0_copied, 1)

            def pool_out(g):
                n = ("pool", g)
                dve.wait_ge(obhi_ready, g + 1)
                tile_free(V.scalar_tensor_tensor(out=halves(oblo[:, g, :]), in0=acc_full(n), scalar=col("pscale", g),
                                                 in1=halves(obhi[:, g, :].bitcast(F32)), op0=ALU.mult,
                                                 op1=ALU.subtract), n)

            def pool_prep(g):
                W_, w = T + PADC, POOL_WINDOWS[g]
                tile_freed(dve, ("pin", g))
                src = pin[:, g, :]
                cur = src
                for s in range(g + 1):
                    d = 1 << s
                    dst = pp[s % 2]
                    tick(V.tensor_tensor(dst[:, 2 * d - 1:W_], cur[:, 2 * d - 1:W_], cur[:, d - 1:W_ - d], ALU.add))
                    settle()
                    cur = dst
                dst = pp[(g + 1) % 2]
                c0 = PADC + w - 1
                tick(V.scalar_tensor_tensor(out=dst[:, c0:W_], in0=cur[:, c0:W_], scalar=1.0 / w, in1=src[:, c0:W_],
                                            op0=ALU.mult, op1=ALU.subtract))
                tick(V.tensor_tensor(dst[:, PADC:c0], cur[:, PADC:c0], inv_n[:, 0:w - 1], ALU.mult))
                settle()
                tick(V.tensor_tensor(dst[:, PADC:c0], dst[:, PADC:c0], src[:, PADC:c0], ALU.subtract))
                settle()
                if g >= 2:
                    tile_done(dve, ("pool", g - 2))
                tick(V.tensor_copy(pdhi[g % 2][:, :], dst[:, PADC:W_]))
                settle()
                V.tensor_tensor(pdlo[g % 2][:, :], dst[:, PADC:W_], pdhi[g % 2][:, :].bitcast(F32), ALU.subtract)\
                 .then_inc(pd_ready, 1)
                dve.wait_ge(pd_ready, g + 1)

            def branch_b(k):
                n = ("y", 0, k)
                tile_done(dve, n)
                tile_freed(dve, ("g", 0, k))
                tile_free(V.tensor_tensor(halves(mix[:, k, :]), acc_full(n), halves(mix[:, k, :]), ALU.mult), n)

            for idx, (name, hooks) in enumerate(order):
                kind, h = name[0:2]
                p, hh = h // 2, h % 2
                if 1 <= idx <= 4:
                    values_out(idx - 1, v_turned, v_copied, vtok1)
                for step in hooks:
                    rec_step(*step)
                if name == ("y", 0, 0):
                    branch_b(0)
                if kind == "f":
                    tile_freed(dve, name)
                    if p >= 2:
                        dve.wait_ge(o_done, 5 * (p - 1))
                    f, k_ = av[p % 2][:, hh, :], kf[p % 2][:, hh, :]
                    tick(V.tensor_scalar(f, k_, omlb[:, h:h + 1], lb[:, h:h + 1], ALU.mult, ALU.add))
                    settle()
                    V.tensor_scalar(k_, f, -1.0, 1.0, ALU.mult, ALU.add).then_inc(f_ready, 1)
                    dve.wait_ge(ln_ready, h + 1)
                    V.tensor_tensor_scan(f, rmask[:, :], f, 0.0, ALU.mult, ALU.add).then_inc(a_ready, 1)
                if name == ("q", 5):
                    dve.wait_ge(spilled, 16)
                    pool_prep(0)
                elif name == ("f", 5):
                    pool_prep(1)
                elif kind == "og" and 1 <= h <= 2:
                    pool_prep(h + 1)
                elif kind == "pool":
                    pool_out(h)

            for t in range(4):
                for k in (2 * t, 2 * t + 1):
                    if k:
                        branch_b(k)
                tile_freed(dve, ("og", t))
                dve.wait_ge(orn, t + 1)
                tick(V.scalar_tensor_tensor(out=oT[:, t, :], in0=oT[:, t, :], scalar=col("head", t),
                                            in1=E[1][:, t % 2, :], op0=ALU.mult, op1=ALU.mult))
                settle()
                V.tensor_tensor(oT[:, t, :], oT[:, t, :], og[:, t, :], ALU.mult).then_inc(on_ready, 1)
                dve.wait_ge(oahi_ready, t + 1)
                V.tensor_tensor(oalo[:, t, :], oT[:, t, :], oahi[:, t, :].bitcast(F32), ALU.subtract)\
                 .then_inc(oa_ready, 1)
            for k in range(KT):
                n = ("y", 1, k)
                tile_done(dve, n)
                tile_freed(dve, ("g", 1, k))
                if k >= 2:
                    dve.wait_ge(mix_ready, k - 1)
                tile_free(V.tensor_tensor(halves(tmp[k % 2][:, :]), acc_full(n), halves(ga(k)), ALU.mult), n)
                tile_freed(dve, n)
                V.tensor_tensor(mix[:, k, :], mix[:, k, :], tmp[k % 2][:, :], ALU.add).then_inc(mix_ready, 1)
            for k in range(KT):
                dve.wait_ge(mixhi_ready, k + 1)
                dve.wait_ge(mix_ready, k + 1)
                V.tensor_tensor(zlo[:, k, :], mix[:, k, :], zhi[:, k, :].bitcast(F32), ALU.subtract)\
                 .then_inc(mixz_ready, 1)
            dve.wait_ge(h_back, 16)
            dve.wait_ge(mixz_ready, KT)
            for k in range(KT):
                n = ("out", k)
                tile_done(dve, n)
                tile_free(V.tensor_tensor(halves(hT[:, k, :]), acc_full(n), halves(hT2[:, k, :]), ALU.add), n)
            for k in (6, 7):
                tile_freed(dve, ("out", k))
            norm_split(norm2)

            for j in range(FT // 2):
                for k in (2 * j, 2 * j + 1):
                    tile_freed(dve, ("u", k))
                    u, c = ub[k % 2], cb[k % 2][:, :]
                    if k >= 2:
                        tile_freed(dve, ("vv", k - 2))
                    tick(V.tensor_scalar(c, u[:, NM:T], col("convw", 2 * FT + k), col("convb", k), ALU.mult, ALU.add))
                    settle()
                    tick(V.scalar_tensor_tensor(out=c, in0=u[:, NM - 1:T - 1], scalar=col("convw", FT + k), in1=c,
                                                op0=ALU.mult, op1=ALU.add))
                    settle()
                    V.scalar_tensor_tensor(out=c, in0=u[:, NM - 2:T - 2], scalar=col("convw", k), in1=c,
                                           op0=ALU.mult, op1=ALU.add).then_inc(c_ready, 1)
                for k in (2 * j, 2 * j + 1):
                    n = ("vv", k)
                    tile_done(dve, n)
                    dve.wait_ge(silu_ready, k + 1)
                    if k >= 2:
                        dve.wait_ge(g_ready, k - 1)
                    tile_free(V.tensor_tensor(gt[k % 2][:, :], acc_real(n), cb[k % 2][:, :], ALU.mult), n)
                for k in (2 * j, 2 * j + 1):
                    dve.wait_ge(ghi_ready, k + 1)
                    V.tensor_tensor(glo[:, k, :], gt[k % 2][:, :], ghi[:, k, :].bitcast(F32), ALU.subtract)\
                     .then_inc(g_ready, 1)
            for k in range(KT):
                n = ("dn", k)
                tile_done(dve, n)
                tile_free(V.tensor_tensor(hT[:, k, NM:T], acc_real(n), hT[:, k, NM:T], ALU.add), n)
            for k in (6, 7):
                tile_freed(dve, ("dn", k))
            dve.wait_ge(normf.rb_ready, 1)
            for k in range(KT):
                V.scalar_tensor_tensor(out=hT[:, k, :], in0=hT[:, k, :], scalar=col("final", k), in1=nrb[:, :],
                                       op0=ALU.mult, op1=ALU.mult).then_inc(h1_ready, 1)
            dve.wait_ge(h1_ready, KT)
            dve.wait_ge(meta_turned, 1)
            V.tensor_copy(hT[:, :, 0:NM], PS[:, 5, 0:P].rearrange("p (k t) -> p k t", k=KT)).then_inc(h1_meta, 1)
            dve.wait_ge(h1_meta, 1)
            norm_split(normp)

            norm_split(normq)
            dve.wait_ge(normq.z_ready, 2)
            norm_split(normk)
            dve.wait_ge(late_in, 32)
            r_ = slice(64, P)
            t1, t2 = PT[0][r_, 0:T], PT[0][r_, T:2 * T]
            dve.wait_ge(fl_ready, 1)
            tile_done(dve, ("kpe", 1))
            tile_free(V.tensor_tensor(halves(t1), acc_full(("kpe", 0), r_), halves(trig[r_, 1, :]), ALU.mult), ("kpe", 0))
            tile_free(V.tensor_tensor(halves(t2), acc_full(("kpe", 1), r_), halves(trig[r_, 2, :]), ALU.mult), ("kpe", 1))
            tile_freed(dve, ("kpe", 0))
            tile_freed(dve, ("kpe", 1))
            tick(V.tensor_tensor(kh[0][r_, :], t1, t2, ALU.add))
            V.tensor_tensor(kh[1][r_, :], t1, t2, ALU.add).then_inc(kr_ready, 1)
            f0, f1 = fgt[0:HEADS, 0, :], fgt[0:HEADS, 1, :]
            dve.wait_ge(fl_abs, 1)
            tick(V.memset(nch[:, :].bitcast(F32), 0.0))
            tick(V.tensor_scalar(f0, f0, 0.0, None, ALU.min))
            settle()
            tick(V.tensor_tensor(f0, f0, f1, ALU.subtract))
            settle()
            tick(V.tensor_tensor_scan(f1, trig[0:HEADS, 0, :], f0, 0.0, ALU.mult, ALU.add))
            settle()
            tick(V.tensor_scalar(f0, f1, -1.0, None, ALU.mult))
            settle()
            tick(V.tensor_copy(nch[0:HEADS, :], f0))
            settle()
            V.tensor_tensor(nch[32:32 + HEADS, :], f0, nch[0:HEADS, :].bitcast(F32), ALU.subtract).then_inc(cum_ready, 1)
            for i in range(5):
                for j in range(2):
                    n = ("mv", i, j)
                    rows = NM if i == 0 else P
                    tile_done(dve, n)
                    tile_free(V.tensor_copy(vtok[0:rows, i, SEQ * j:SEQ * (j + 1)], acc_real(n, slice(0, rows))), n)

            def attention(A, project):
                for h in range(HEADS + 2):
                    project(h)
                    for i in range(4):
                        if h < HEADS:
                            dve.wait_ge(A.s_done, 4 * h + i + 1)
                            s = 4 * (h % 2) + i
                            V.tensor_reduce(negmax[:, s:s + 1], s_view(i), AX.XY if i == 3 else AX.X, ALU.max,
                                            negate=True).then_inc(A.m_ready, 1)
                        if 1 <= h <= HEADS and i % 2 == 1:
                            x = h - 1
                            dve.wait_ge(A.g_turned, 4 * x + i + 1)
                            if x >= 2:
                                dve.wait_ge(A.o_done, x - 1)
                            n = 512 if i == 1 else 384
                            V.tensor_copy(PT[x % 2][:, G_COL[i]:G_COL[i] + n], PS[:, 3, 0:n]).then_inc(A.pt_v, 1)
                    if h < HEADS:
                        dve.wait_ge(A.p_exp, 4 * h + 4)
                        s = 4 * (h % 2)
                        tick(V.reciprocal(rinv, rowsum[:, s:s + 4]))
                        settle()
                        for i in range(4):
                            t = Pm[h % 2][:, ATT_OFF[i]:ATT_OFF[i] + ATT_N[i]]
                            ins = V.tensor_scalar(t, t, rinv[:, i:i + 1], None, ALU.mult)
                            if i < 3:
                                tick(ins)
                        ins.then_inc(A.p_ready, 1)

            def mla_project(h):
                for x in ([0, 1] if h == 0 else [h + 1]):
                    if x < HEADS:
                        n = ("mq", x)
                        tile_done(dve, n)
                        if x >= 2:
                            dve.wait_ge(mla.s_done, 4 * (x - 1))
                        tile_free(V.scalar_tensor_tensor(out=qh[x % 2][:, :], in0=acc_real(n), scalar=MLA_SCALE,
                                                         in1=trig[:, 0, NM:T], op0=ALU.mult, op1=ALU.mult), n)

            attention(mla, mla_project)

            def gated(kind, A, b):
                dve.wait_ge(A.o_ready, HEADS)
                for k in range(KT):
                    tile_freed(dve, (kind, k))
                    if k >= 2:
                        dve.wait_ge(y_ready, KT * b + k - 1)
                    V.tensor_tensor(nzt[k % 2][:, 0:SEQ], omla[:, k, :], nsq[k % 2][:, 0:SEQ], ALU.mult).then_inc(ygt, 1)
                    dve.wait_ge(yhi_r, KT * b + k + 1)
                    V.tensor_tensor(ylo[:, k, :], nzt[k % 2][:, 0:SEQ], yhi[:, k, :].bitcast(F32), ALU.subtract)\
                     .then_inc(y_ready, 1)

            def gates(b):
                for k in range(KT):
                    n = ("hy", b, k)
                    tile_done(dve, n)
                    tile_freed(dve, ("hg", b, k))
                    dst = mix2[:, k, :] if b == 0 else nzt[k % 2][:, 0:SEQ]
                    if b and k >= 2:
                        dve.wait_ge(mix2_ready, k - 1)
                    tile_free(V.tensor_tensor(dst, acc_real(n), nsq[k % 2][:, 0:SEQ], ALU.mult), n)
                    if b:
                        tile_freed(dve, n)
                        V.tensor_tensor(mix2[:, k, :], mix2[:, k, :], nzt[k % 2][:, 0:SEQ], ALU.add)\
                         .then_inc(mix2_ready, 1)

            gated("mz", mla, 0)
            gates(0)
            for k in range(KT):
                values_out(k, xv_turned, xv_copied, vtok)
            attention(fox, lambda h: None)
            gated("xz", fox, 1)
            dve.wait_ge(y_ready, 2 * KT)
            gates(1)
            for k in range(KT):
                dve.wait_ge(fmixhi, k + 1)
                dve.wait_ge(mix2_ready, k + 1)
                V.tensor_tensor(zlo[:, k, 0:SEQ], mix2[:, k, :], zhi[:, k, 0:SEQ].bitcast(F32), ALU.subtract)\
                 .then_inc(fmix, 1)
            dve.wait_ge(late_in, 48)
            for j in range(4):
                cols = slice(256 * j, 256 * (j + 1))
                for i in range(QB):
                    n = ("fin", j, i)
                    dve.wait_ge(fin_sq, QB * j + i + 1)
                    tile_free(V.tensor_tensor(mtok[:, i, cols], acc_real(n, n=256), gpost[:, cols], ALU.mult), n)
            for i in range(2, QB):
                tile_freed(dve, ("fin", 3, i))
            V.tensor_reduce(ssum, fsum.rearrange("p (i j) -> p i j", i=4), AX.X, ALU.add).then_inc(fin_sum, 1)
            dve.wait_ge(fin_rstd, 1)
            for i in range(QB):
                V.scalar_tensor_tensor(out=mtok[:, i, :], in0=mtok[:, i, :], scalar=ssum[:, i:i + 1],
                                       in1=htok[:, i, :], op0=ALU.mult, op1=ALU.add).then_inc(fin_out, 1)


_OUTS = [((1, SEQ, D), "float32")]


def kernel(**inputs):
    import concourse.bacc as _bacc
    from concourse.bass_utils import run_bass_kernel_spmd as _run

    nc = _bacc.Bacc("TRN2", target_bir_lowering=False, num_devices=1)
    arrays, args = {}, {}
    every = {k: np.asarray(v) for k, v in inputs.items()}
    every.update(host_constants())
    for name, value in every.items():
        value = np.ascontiguousarray(value)
        arrays[f"in_{name}"] = value
        args[name] = nc.dram_tensor(f"in_{name}", value.shape, mybir.dt.from_np(value.dtype), kind="ExternalInput").ap()
    out = nc.dram_tensor("out_0", _OUTS[0][0], F32, kind="ExternalOutput").ap()
    build_program(nc, args, out)
    r = _run(nc, [arrays], core_ids=[0])
    return r.results[0]["out_0"]
```

```python
from contextlib import ExitStack

import numpy as np

import concourse.bass as bass
from concourse import mybir

F32 = mybir.dt.float32
F32R = mybir.dt.float32r
BF16 = mybir.dt.bfloat16
U8 = mybir.dt.uint8
ALU = mybir.AluOpType
ACT = mybir.ActivationFunctionType
AX = mybir.AxisListType

P = 128
D = 1024
KT = D // P
NM = 16
SEQ = 512
T = NM + SEQ
HALF = T // 2
EPS = 1e-6

A_VDIM = 64
D_FF = 2816
FT = D_FF // P
POOL_WINDOWS = (2, 4, 8, 16)
PADC = 16
CH = 128
LEVELS = 7
MASKC = 64 * (LEVELS + 1)

HEADS = 16
ROPE = 32
NOPE = 64
QW = NOPE + ROPE
DV = 64
QB = SEQ // P
MLA_SCALE = 1.0 / float(np.sqrt(QW))
FOX_SCALE = 1.0 / 8.0
NEG = -1.0e30

A_Q, A_F, A_V, A_OG, B_IN, G_A, G_B = 0, 1024, 2048, 2560, 3072, 3584, 4608
M_CQ, M_CKV, M_KPE, M_Z, X_Q, X_K, X_V, X_F, X_Z, H_A, H_B = (
    0, 256, 384, 416, 1440, 2464, 3488, 4512, 4528, 5552, 6576)

ROWS = {}
for _name, _n in (("norm1", 8), ("lb0", 8), ("lb1", 8), ("bf", 8), ("head", 4), ("pscale", 4), ("norm2", 8),
                  ("final", 8), ("pre", 8), ("qn", 2), ("kvn", 1)):
    ROWS[_name] = (sum(n for _, n in ROWS.values()), _n)
NROW1 = sum(n for _, n in ROWS.values())
ROWS["convw"] = (P, 3 * FT)
ROWS["convb"] = (P + 3 * FT, FT)
NROW2 = 4 * FT


def host_constants():
    s = np.arange(P)[:, None]
    mask = np.zeros((P, MASKC), np.float32)
    for j in range(LEVELS):
        half = 1 << j
        n, b = np.divmod(np.arange(64), half)
        mask[:, 64 * j:64 * j + 64] = (s // (2 * half) == n[None]) & (s % (2 * half) < half)
    mask[:, 64 * LEVELS:] = s % 64 == np.arange(64)[None]
    pos = np.arange(T, dtype=np.float32)
    half = ROPE // 2
    freq = np.float32(10000.0) ** (-np.arange(half, dtype=np.float32) / np.float32(half))
    ang = (pos[None, :] * freq[:, None].astype(np.float32)).astype(np.float64)
    cos, sin = np.cos(ang).astype(np.float32), np.sin(ang).astype(np.float32)
    trig = np.ones((P, 3, T), np.float32)
    trig[64:96, 0] = np.concatenate([cos, cos])
    trig[96:128, 0] = np.concatenate([-sin, sin])
    trig[32:64, 1] = np.concatenate([cos, cos])
    trig[64:96, 2] = np.concatenate([-sin, sin])
    inv = np.ones((P, PADC), np.float32)
    inv[:] = 1.0 / np.arange(1, PADC + 1, dtype=np.float32)
    causal = np.where(np.arange(P)[None] > np.arange(P)[:, None], np.float32(NEG), np.float32(0.0))
    e = np.zeros((P, HEADS), np.float32)
    for h in range(HEADS):
        e[h, h] = e[32 + h, h] = e[64 + h, h] = e[96 + h, h] = 1.0
    return {"c_level": mask, "c_trig": trig, "c_inv": inv, "c_causal": causal.astype(np.float32), "c_pick": e}


class Piece:

    def __init__(self, unit, col, kt, x, k0, mode, slot, first, last, name):
        self.unit, self.col, self.kt, self.x, self.k0 = unit, col, kt, x, k0
        self.mode, self.slot, self.first, self.last, self.name = mode, slot, first, last, name


class Plan:

    def __init__(self):
        self.units = []
        self.pieces = []
        self.tile = {}
        self.unit_end = []
        self.uses = [0, 0]
        self.slot, self.before = [], []
        self.last, self.next_slot = {}, 0

    def unit(self, parts, kt, cols, own_place=False):
        self.units.append((parts, kt, cols))
        self.unit_end.append(0)
        self.before.append(self.last.get(self.next_slot))
        self.slot.append(self.next_slot)
        if own_place:
            self.before[-1] = None
        else:
            self.last[self.next_slot] = len(self.units) - 1
            self.next_slot = 1 - self.next_slot
        return len(self.units) - 1

    def piece(self, name, unit, col, kt, x, mode="full", slot=0, k0=0, first=True, last=True):
        if first:
            self.tile[name] = [slot, 0, self.uses[slot]]
            self.uses[slot] += 1
        self.pieces.append(Piece(unit, col, kt, x, k0, mode, slot, first, last, name))
        self.tile[name][1] = len(self.pieces)
        self.unit_end[unit] = len(self.pieces)


def make_plan():
    pl = Plan()
    n = 0

    def two(names, w, col0, x, kt=KT, mode="full"):
        nonlocal n
        u = pl.unit([(w, 0, col0, 256, 0)], kt, 256)
        for i, name in enumerate(names):
            pl.piece(name, u, 128 * i, kt, x, mode, slot=n % 2)
            n += 1

    def pair(kind, col0, j):
        two([(kind, 2 * j), (kind, 2 * j + 1)], "w_in", col0 + 256 * j, "z")

    def gate(b, j):
        two([("g", b, 2 * j), ("g", b, 2 * j + 1)], "w_in", (G_B, G_A)[b] + 256 * j, "z")

    def branch(b, j):
        two([("y", b, 2 * j), ("y", b, 2 * j + 1)], ("w_branch_b", "w_branch_a")[b], 256 * j, ("ob", "oa")[b], kt=4)

    for j in range(2):
        pair("v", A_V, j)
    for p in range(2):
        pair("q", A_Q, p)
        pair("f", A_F, p)
    for j in range(2):
        pair("pin", B_IN, j)
    pair("q", A_Q, 2)
    pair("f", A_F, 2)
    pl.pool_unit = pl.unit([("w_pool", 0, 0, 512, 0)], 1, 512, own_place=True)
    for j in range(2):
        u = pl.unit([("w_in", 0, A_OG + 256 * j, 256, 0)], KT, 256)
        for m in range(2):
            g = 2 * j + m
            pl.piece(("og", g), u, 128 * m, KT, "z", slot=n % 2)
            pl.piece(("pool", g), pl.pool_unit, 128 * g, 1, "pd", slot=(n + 1) % 2, k0=g)
            n += 2
    pair("q", A_Q, 3)
    pair("f", A_F, 3)
    for j in range(4):
        gate(0, j)
    for j in range(2):
        gate(1, j)
    for j in range(4):
        branch(0, j)
    for j in range(2, 4):
        gate(1, j)
    for j in range(4):
        branch(1, j)
    for j in range(4):
        two([("out", 2 * j), ("out", 2 * j + 1)], "w_out", 256 * j, "z")
    for j in range(FT // 2):
        two([("u", 2 * j), ("u", 2 * j + 1)], "w_up", 256 * j, "z")
        two([("vv", 2 * j), ("vv", 2 * j + 1)], "w_up", D_FF + 256 * j, "z", mode="real")
    for j in range(4):
        for i, (k0, kt) in enumerate(((0, 8), (8, 8), (16, 6))):
            u = pl.unit([("w_down", k0 * P, 256 * j, 256, 0)], kt, 256)
            for m in range(2):
                pl.piece(("dn", 2 * j + m), u, 128 * m, kt, "g", "real", slot=m, k0=k0, first=i == 0, last=i == 2)
    n = 0
    two([("cq", 0), ("cq", 1)], "w_in_2", M_CQ, "z")
    h = ROPE // 2
    u = pl.unit([("w_in_2", 0, M_CKV, 128, 0), ("w_in_2", 0, X_F, 32, 128), ("w_in_2", 0, M_KPE, ROPE, 160),
                 ("w_in_2", 0, M_KPE + h, h, 192), ("w_in_2", 0, M_KPE, h, 208), ("w_in_2", 0, M_KPE, ROPE, 224)],
                KT, 256)
    for i, name in enumerate((("ckv", 0), ("kpe", 0))):
        pl.piece(name, u, 128 * i, KT, "z", "full", slot=n % 2)
        n += 1
    pl.ukv = pl.unit([("w_ukv_2", 0, 0, 2048, 0)], 1, 2048)
    pl.uq = [pl.unit([("w_uq", 0)], 2, 1024)]
    pl.next_slot = 1 - pl.next_slot
    pl.uq.append(pl.unit([("w_uq", 8)], 2, 1024))
    for i in range(5):
        for j in range(2):
            pl.piece(("mv", i, j), pl.ukv, j, 1, "ckv", "values", slot=j, k0=i)
    for hd in range(HEADS):
        pl.piece(("mq", hd), pl.uq[hd // 8], 128 * (hd % 8), 2, "cq", "real", slot=0)
        pl.piece(("mk", hd), pl.ukv, 128 * hd, 1, "ckv", "full", slot=0)
    n = 0
    for j in range(4):
        two([("mz", 2 * j), ("mz", 2 * j + 1)], "w_in_2", M_Z + 256 * j, "z", mode="real")
    for j in range(4):
        two([("hg", 0, 2 * j), ("hg", 0, 2 * j + 1)], "w_in_2", H_A + 256 * j, "z", mode="real")
        two([("hy", 0, 2 * j), ("hy", 0, 2 * j + 1)], "w_br_mla_2", 256 * j, "y", mode="real512")
    for j in range(4):
        two([("xv", 2 * j), ("xv", 2 * j + 1)], "w_in_2", X_V + 256 * j, "z")
    order = [("xq", 0), ("xk", 0)]
    for x in range(1, KT):
        order += [("xq", x), ("xk", x)]
    for kind, x in order:
        if x % 2 == 0:
            u = pl.unit([("w_in_2", 0, (X_Q if kind == "xq" else X_K) + 128 * x, 256, 0)], KT, 256)
            unit_of = {**(unit_of if x or kind == "xk" else {}), kind: u}
        pl.piece((kind, x), unit_of[kind], 128 * (x % 2), KT, "z", "real" if kind == "xq" else "full", slot=0)
    n = 0
    for j in range(4):
        two([("xz", 2 * j), ("xz", 2 * j + 1)], "w_in_2", X_Z + 256 * j, "z", mode="real")
    for j in range(4):
        two([("hg", 1, 2 * j), ("hg", 1, 2 * j + 1)], "w_in_2", H_B + 256 * j, "z", mode="real")
        two([("hy", 1, 2 * j), ("hy", 1, 2 * j + 1)], "w_br_fox_2", 256 * j, "y", mode="real512")
    for j in range(4):
        u = pl.unit([("w_out_2", 0, 256 * j, 256, 0)], KT, 256)
        for i in range(QB):
            pl.piece(("fin", j, i), u, 0, KT, "mx", "tokens", slot=n % 2, k0=i)
            n += 1
    return pl


def build_program(nc: bass.Bass, a, out):
    pl = make_plan()
    NU = len(pl.units)
    ctx = ExitStack()
    with ctx:
        def at(name, shape, dt, offset):
            size = int(np.prod(shape[1:])) * {F32: 4, F32R: 4, BF16: 2, U8: 1}[dt]
            return nc.alloc_sbuf_tensor_at(name, shape, dt, offset=offset), offset + size

        def sem(name):
            return ctx.enter_context(nc.semaphore(name))

        o = 16512
        raw, hi, lo = [], [], []
        for i in range(2):
            t, o = at(f"raw{i}", [P, 2048], F32, o)
            raw.append(t)
        for i in range(2):
            t, o = at(f"whi{i}", [P, 2048], F32R, o)
            hi.append(t)
        for i in range(2):
            t, o = at(f"wlo{i}", [P, 2048], F32R, o)
            lo.append(t)
        prm, o = at("prm", [P, 256], F32, o)
        ident, o = at("ident", [P, P], F32, o)
        ones, o = at("ones", [P, P], F32, o)
        pair1, o = at("pair1", [P, P], F32, o)
        identb, o = at("identb", [P, P], BF16, o)
        causalb, o = at("causalb", [P, P], BF16, o)
        small, o = at("small", [P, 128], F32, o)
        inv_n, o = at("inv_n", [P, PADC], F32, o)
        pick, o = at("pick", [P, HEADS], F32R, o)
        lvl, o = at("lvl", [P, MASKC], U8, o)
        A = (o + 31) // 32 * 32
        B = A + KT * T * 4
        C = B + 2 * KT * T * 4

        hT, _ = at("hT", [P, KT, T], F32, A)
        mix, _ = at("mix", [P, KT, T], F32, A)
        omla, _ = at("omla", [P, KT, SEQ], F32, A)
        zhi, e = at("zhi", [P, KT, T], F32R, B)
        zlo, _ = at("zlo", [P, KT, T], F32R, e)
        xt, e = at("xt", [P, QB, D], F32, C)
        xm, e = at("xm", [NM, D], F32, e)
        prow, e = at("prow", [P, 2, P], F32, e)
        sq = [None, None]
        sq[0], e = at("sq0", [P, T], F32, e)
        sq[1], e = at("sq1", [P, T], F32, e)
        zt = [None, None]
        zt[0], e = at("zt0", [P, T], F32, e)
        zt[1], e = at("zt1", [P, T], F32, e)
        rb, e = at("rb", [P, T], F32, e)
        cstage, e = at("cstage", [P, P + HEADS + MASKC], F32, e)
        vtok1, e = at("vtok1", [P, 5, 512], F32, C)
        qf = [at(f"qf{i}", [P, 2, T], F32, e + i * 2 * T * 4)[0] for i in range(2)]
        e += 4 * T * 4
        kf = [at(f"kf{i}", [P, 2, T], F32, e + i * 2 * T * 4)[0] for i in range(2)]
        e += 4 * T * 4
        av = [at(f"av{i}", [P, 2, T], F32, e + i * 2 * T * 4)[0] for i in range(2)]
        AVOFF = e
        e += 4 * T * 4
        E = [at(f"E{i}", [P, 2, T], F32, e + i * 2 * T * 4)[0] for i in range(2)]
        e += 4 * T * 4
        rmask, e = at("rmask", [P, T], F32, e)
        og, e = at("og", [P, 4, T], F32, e)
        pin, e = at("pin", [P, 4, T + PADC], F32, e)
        obhi, e = at("obhi", [P, 4, T], F32R, e)
        oblo, e = at("oblo", [P, 4, T], F32R, e)
        oT, e = at("oT", [P, 4, T], F32, e)
        Sc, e = at("Sc", [P, 2, 4, DV], F32, e)
        scT, e = at("scT", [P, 8, P], F32, e)
        sc0, e = at("sc0", [NM, 2, NM], F32, e)
        kdt, e = at("kdt", [P, 2, 4, P], F32, e)
        GOFF = e
        tmp = [at(f"tmp{i}", [P, T], F32, GOFF + (2 + i) * T * 4)[0] for i in range(2)]
        pp = [at(f"pp{i}", [P, T + PADC], F32, GOFF + i * (T + PADC) * 4)[0] for i in range(2)]
        P1_END = GOFF + 4 * T * 4 + 256
        assert P1_END <= nc.sbuf_usable_end, (P1_END, nc.sbuf_usable_end)
        wphi, e2 = at("wphi", [P, 512], F32R, A)
        wplo, e2 = at("wplo", [P, 512], F32R, e2)
        pdhi = [at(f"pdhi{i}", [P, T], F32R, e2 + i * T * 4)[0] for i in range(2)]
        pdlo = [at(f"pdlo{i}", [P, T], F32R, e2 + (2 + i) * T * 4)[0] for i in range(2)]
        assert e2 + 4 * T * 4 <= B
        ga2, _ = at("ga2", [P, 4, T], F32, C)
        ga = lambda k: pin[:, k, 0:T] if k < 4 else ga2[:, k - 4, :]
        oahi, e2 = at("oahi", [P, 4, T], F32R, C + 10240)
        oalo, e2 = at("oalo", [P, 4, T], F32R, e2)
        hT2, _ = at("hT2", [P, KT, T], F32, AVOFF)
        ghi, e = at("ghi", [P, FT, SEQ], F32R, C)
        glo, e = at("glo", [P, FT, SEQ], F32R, e)
        ub = [at(f"ub{i}", [P, T], F32, e + i * T * 4)[0] for i in range(2)]
        e += 2 * T * 4
        cb = [at(f"cb{i}", [P, SEQ], F32, e + i * SEQ * 4)[0] for i in range(2)]
        e += 2 * SEQ * 4
        gt = [at(f"gt{i}", [P, SEQ], F32, e + i * SEQ * 4)[0] for i in range(2)]
        e += 2 * SEQ * 4
        assert e <= nc.sbuf_usable_end, e
        e = C + 2 * FT * SEQ * 4
        qa = [at(f"qa{i}", [P, SEQ], F32, e + i * SEQ * 4)[0] for i in range(2)]
        qb = [at(f"qb{i}", [P, SEQ], F32, e + (2 + i) * SEQ * 4)[0] for i in range(2)]
        e += 4 * SEQ * 4
        suma, e = at("suma", [P, SEQ], F32, e)
        sumb, e = at("sumb", [P, SEQ], F32, e)
        xm2, e = at("xm2", [NM, D], F32, e)
        sqm, e = at("sqm", [P, KT, NM], F32, e)
        zm, e = at("zm", [P, KT, NM], F32, e)
        rm, e = at("rm", [P, NM], F32, e)
        assert e <= nc.sbuf_usable_end, e
        N0 = C + 97728
        nsq = [at(f"nsq{i}", [P, T], F32, N0 + i * T * 4)[0] for i in range(2)]
        nzt = [at(f"nzt{i}", [P, T], F32, N0 + (2 + i) * T * 4)[0] for i in range(2)]
        nrb, e = at("nrb", [P, T], F32, N0 + 4 * T * 4)
        assert e <= nc.sbuf_usable_end, e
        r1, _ = at("r1", [P, SEQ], F32, N0)
        r1l, _ = at("r1l", [P, SEQ], F32, C + 2 * FT * SEQ * 4)
        r2t, _ = at("r2t", [P, SEQ], F32, C + (2 * FT + 1) * SEQ * 4)
        htok, e = at("htok", [P, QB, D], F32, C)
        vtok, e = at("vtok", [P, 5, D], F32, e)
        YOFF = e
        Pm = [at(f"Pm{i}", [P, 1344], F32, e + i * 1344 * 4)[0] for i in range(2)]
        e += 2 * 1344 * 4
        PT = [at(f"PT{i}", [P, 14 * P], F32, e + i * 14 * P * 4)[0] for i in range(2)]
        e += 2 * 14 * P * 4
        cqhi, e = at("cqhi", [P, 2, T], F32R, e)
        cqlo, e = at("cqlo", [P, 2, T], F32R, e)
        ckhi, e = at("ckhi", [P, T], F32R, e)
        cklo, e = at("cklo", [P, T], F32R, e)
        qh = [at(f"qh{i}", [P, SEQ], F32, e + i * SEQ * 4)[0] for i in range(2)]
        e += 2 * SEQ * 4
        kh = [at(f"kh{i}", [P, T], F32, e + i * T * 4)[0] for i in range(2)]
        e += 2 * T * 4
        trig, e = at("trig", [P, 3, T], F32, e)
        cqT, e = at("cqT", [P, 3, T], F32, e)
        nch, e = at("nch", [P, T], F32R, e)
        fgt, _ = at("fgt", [64, 2, T], F32, N0)
        assert e <= N0, (e, N0)
        yhi, e = at("yhi", [P, KT, SEQ], F32R, YOFF)
        ylo, e = at("ylo", [P, KT, SEQ], F32R, e)
        MIXOFF = e
        mix2, e = at("mix2", [P, KT, SEQ], F32, e)
        xka = [at(f"xka{i}", [P, T], F32R, e + i * T * 4)[0] for i in range(2)]
        xkb = [at(f"xkb{i}", [P, T], F32R, e + (2 + i) * T * 4)[0] for i in range(2)]
        e += 4 * T * 4
        assert e <= C + 95616, e - C
        xqa = [at(f"xqa{i}", [P, SEQ], F32R, N0 + i * T * 4)[0] for i in range(2)]
        xqb = [at(f"xqb{i}", [P, SEQ], F32R, N0 + (2 + i) * T * 4)[0] for i in range(2)]
        e2 = YOFF + 2 * (1344 + 14 * P) * 4
        fq = [at(f"fq{i}", [P, SEQ], F32, e2 + i * SEQ * 4)[0] for i in range(2)]
        fk, e2 = at("fk", [P, T], F32, e2 + 2 * SEQ * 4)
        assert e2 <= MIXOFF
        mtok, _ = at("mtok", [P, QB, D], F32, C + 16384)
        fjunk, _ = at("fjunk", [P, 4, QB, 256], F32, YOFF)
        gpost, _ = at("gpost", [P, D], F32, C + 32768)

        PS = ctx.enter_context(nc.psum_tensor("PS", [P, 8, 512], F32))
        el = small[:, 0:8].rearrange("p (h c) -> p h c", h=2)
        lb, omlb, lbe, epst, fbias = small[:, 8:16], small[:, 16:24], small[:, 24:40], small[:, 40:41], small[:, 41:42]
        negmax, rowsum, rinv, ssum, lbt = small[:, 48:56], small[:, 56:64], small[:, 64:68], small[:, 72:76], small[:, 80:96]
        fsum, g12 = small[:, 96:112], small[:, 112:120]

        def col(name, k):
            r = ROWS[name][0]
            return prm[:, r + k:r + k + 1]

        w_landed = [sem(f"w_landed{i}") for i in range(2)]
        w_split = sem("w_split")
        pe_mark = sem("pe_mark")
        acc_free = [sem(f"acc_free{i}") for i in range(2)]
        act_step, dve_step = sem("act_step"), sem("dve_step")
        x2_in = sem("x2_in")
        x_in, prm_in, const_in, late_in = sem("x_in"), sem("prm_in"), sem("const_in"), sem("late_in")
        const_ready, prm_turned = sem("const_ready"), sem("prm_turned")
        x_turned, h_copied = sem("x_turned"), sem("h_copied")
        lb_sub, lb_exp = sem("lb_sub"), sem("lb_exp")
        v_turned, v_copied = sem("v_turned"), sem("v_copied")
        f_ready, ln_ready, a_ready = sem("f_ready"), sem("ln_ready"), sem("a_ready")
        sub_ready, exp_ready, mul_ready = sem("sub_ready"), sem("exp_ready"), sem("mul_ready")
        qd_exp, qd_ready = sem("qd_exp"), sem("qd_ready")
        kd_turned, kdt_ready, upd_done, s_ready = sem("kd_turned"), sem("kdt_ready"), sem("upd_done"), sem("s_ready")
        sc_done, sc_copied, c0_copied = sem("sc_done"), sem("sc_copied"), sem("c0_copied")
        o_done, o_copied = sem("o_done"), sem("o_copied")
        pd_ready, obhi_ready = sem("pd_ready"), sem("obhi_ready")
        osq, ossd, orn, on_ready, oahi_ready, oa_ready = (sem("osq"), sem("ossd"), sem("orn"), sem("on_ready"),
                                                          sem("oahi_ready"), sem("oa_ready"))
        spilled, h_back = sem("spilled"), sem("h_back")
        mix_ready, mix2_ready = sem("mix_ready"), sem("mix2_ready")
        mixhi_ready, mixz_ready = sem("mixhi_ready"), sem("mixz_ready")
        c_ready, silu_ready, ghi_ready, g_ready = sem("c_ready"), sem("silu_ready"), sem("ghi_ready"), sem("g_ready")
        h1_ready, meta_turned, h1_meta = sem("h1_ready"), sem("meta_turned"), sem("h1_meta")
        ht_turned, ht_copied = sem("ht_turned"), sem("ht_copied")
        fl_ready, fl_abs, kr_ready = sem("fl_ready"), sem("fl_abs"), sem("kr_ready")
        fox_hi, fox_lo = sem("fox_hi"), sem("fox_lo")
        xv_turned, xv_copied = sem("xv_turned"), sem("xv_copied")
        ygt, yhi_r, y_ready = sem("ygt"), sem("yhi_r"), sem("y_ready")
        fmixhi, fmix = sem("fmixhi"), sem("fmix")
        fin_sq, fin_sum, fin_rstd, fin_out, out_done = sem("fin_sq"), sem("fin_sum"), sem("fin_rstd"), sem("fin_out"), sem("out_done")

        class Norm:

            def __init__(self, name, src, K, n, width, sqb, ztb, rbb, gain, dst, lhs=None):
                self.src, self.K, self.n, self.width = src, K, n, width
                self.sqb, self.ztb, self.rbb, self.gain, self.dst = sqb, ztb, rbb, gain, dst
                self.lhs = lhs
                self.sq_ready, self.sq_used, self.added = sem(name + "_sq"), sem(name + "_sqd"), sem(name + "_add")
                self.summed = name == "n2"
                self.rb_ready, self.zt_ready = sem(name + "_rb"), sem(name + "_zt")
                self.zhi_ready, self.z_ready = sem(name + "_zhi"), sem(name + "_z")

        zpair = lambda k: (zhi[:, k, :], zlo[:, k, :])
        h_src = lambda k: hT[:, k, :]
        norm1 = Norm("n1", h_src, KT, T, D, sq, zt, rb, "norm1", zpair)
        norm2 = Norm("n2", h_src, KT, T, D, nsq, nzt, nrb, "norm2", zpair)
        fsq, fadd, fsum_done, fm_sq, fm_done, fm_rb, fm_z, fm_hi = (
            sem("fsq"), sem("fadd"), sem("fsum_done"), sem("fm_sq"), sem("fm_done"), sem("fm_rb"), sem("fm_z"),
            sem("fm_hi"))
        r1sq, r2in, r2log, r1_log, r1_ready, rz_ready = (sem("r1sq"), sem("r2in"), sem("r2log"), sem("r1_log"),
                                                          sem("r1_ready"), sem("rz_ready"))
        h1_z, h1_hi, h1_lo = sem("h1_z"), sem("h1_hi"), sem("h1_lo")
        normq = Norm("nq", lambda k: cqT[:, k, :], 2, T, 256, nsq, nzt, nrb, "qn",
                     lambda k: (cqhi[:, k, :], cqlo[:, k, :]))
        normk = Norm("nk", lambda k: cqT[:, 2, :], 1, T, 128, nsq, nzt, nrb, "kvn", lambda k: (ckhi[:, :], cklo[:, :]))

        class Attn:
            def __init__(self, name):
                self.s_done, self.m_ready = sem(name + "s_done"), sem(name + "m_ready")
                self.p_exp, self.p_ready = sem(name + "p_exp"), sem(name + "p_ready")
                self.g_turned, self.pt_a, self.pt_v = sem(name + "g_turned"), sem(name + "pt_a"), sem(name + "pt_v")
                self.o_done, self.o_ready = sem(name + "o_done"), sem(name + "o_ready")

        mla, fox = Attn("mla_"), Attn("fox_")
        hspill = nc.dram_tensor("hspill", [P, KT * T], F32, kind="Internal").ap()

        def acc_full(name, rows=slice(0, P)):
            s = 2 * pl.tile[name][0]
            return PS[rows, s:s + 2, 0:HALF]

        def acc_real(name, rows=slice(0, P), n=SEQ):
            return PS[rows, 2 * pl.tile[name][0], 0:n]

        def halves(t):
            return t.rearrange("p (a b) -> p a b", a=2)

        def tile_done(eng, name):
            eng.wait_ge(pe_mark, pl.tile[name][1])

        def tile_free(ins, name):
            ins.then_inc(acc_free[pl.tile[name][0]], 1)

        def tile_freed(eng, name):
            slot, _, uses = pl.tile[name]
            eng.wait_ge(acc_free[slot], uses + 1)

        def chunk(c):
            return (0, NM) if c == 0 else (NM + CH * (c - 1), CH)

        order = [(("v", j), []) for j in range(4)] + [(n, []) for n in (("q", 0), ("q", 1), ("f", 0), ("f", 1))]
        qf_tiles = [[("q", 2 * p), ("q", 2 * p + 1), ("f", 2 * p), ("f", 2 * p + 1)] for p in range(4)]
        beside = (qf_tiles[1] + [("pin", g) for g in range(4)], qf_tiles[2] + [("og", g) for g in range(4)],
                  qf_tiles[3] + [("g", 0, k) for k in range(4)],
                  [("g", 0, k) for k in range(4, 8)] + [("g", 1, k) for k in range(4)])
        for p, tiles in enumerate(beside):
            for i, n in enumerate(tiles):
                steps = [(p, i)]
                if i == 0 and p:
                    steps = [(p - 1, 9), (p, 0)]
                elif i == 7:
                    steps = [(p, 7), (p, 8)]
                order.append((n, steps))
                if n[0] == "og":
                    order.append((("pool", n[1]), []))
        order.append((("y", 0, 0), [(3, 9)]))

        ROW_LOADS = (("norm1_g", 0, "norm1"), ("lb_logits", 0, "lb0"), ("b_f", 0, "bf"), ("head_norm_g", 0, "head"),
                     ("pool_scale", 0, "pscale"), ("norm2_g", 0, "norm2"), ("final_norm_g", 0, "final"),
                     ("pre_norm_g_2", 0, "pre"), ("mla_q_norm_g_2", 0, "qn"), ("mla_kv_norm_g_2", 0, "kvn"),
                     ("conv_w", 1, "convw"), ("conv_b", 1, "convb"))
        PRM_DMAS = 16 * len(ROW_LOADS)

        def level_views(t, j):
            half, blk = 1 << j, 2 << j
            if blk <= NM:
                v = t.rearrange("p h (n b) -> p (h n) b", b=blk)
                return v[:, :, 0:half], v[:, :, half:blk], v[:, :, half - 1:half], [P, 2 * T // blk, half]
            v = t[:, :, NM:T].rearrange("p h (n b) -> p h n b", b=blk)
            return v[:, :, :, 0:half], v[:, :, :, half:blk], v[:, :, :, half - 1:half], [P, 2, SEQ // blk, half]

        ATT_OFF = [0, 144, 416, 816]
        ATT_N = [144, 272, 400, 528]
        GROUPS = [[(0, i) for i in range(4)], [(1, i) for i in range(4)], [(2, 1), (2, 2), (2, 3)],
                  [(3, 2), (3, 3), (4, 3)]]
        G_COL = [0, 512, 1024, 1408]

        def s_view(i):
            if i == 3:
                return PS[:, 5:7, 0:264]
            return PS[:, 4 if i % 2 == 0 else 5, 0:ATT_N[i]]

        block = ctx.enter_context(nc.Block())

        @block.sync
        def _(sp):
            sp.dma_start(xm[:, :], a["meta_tokens"]).then_inc(x_in, 16)
            for cols in (slice(0, D // 2), slice(D // 2, D)):
                for i in range(QB):
                    sp.dma_start(xt[:, i, cols], a["x"][0, P * i:P * (i + 1), cols])\
                      .then_inc(x_in if cols.start == 0 else x2_in, 16)
            landed = [0, 0]

            def dram(name):
                t = a[name]
                return t if len(t.shape) == 2 else t.rearrange("l k n -> (l k) n")

            def load(u):
                parts, kt, cols = pl.units[u]
                s = u % 2
                if u >= 2:
                    sp.wait_ge(w_split, 2 * (u - 1))
                for part in parts:
                    if part[0] == "w_uq":
                        src = a["w_uq_2"][0].rearrange("(k p) (h c) -> p k h c", p=P, c=QW)
                        dst = raw[s][:, :].rearrange("p (k h c) -> p k h c", k=2, h=8)
                        hs = slice(part[1], part[1] + 8)
                        for k in range(2):
                            for d0, s0, n in ((0, 0, QW), (96, NOPE + 16, 16), (112, NOPE, 16)):
                                sp.dma_start(dst[:, k, :, d0:d0 + n], src[:, k, hs, s0:s0 + n])\
                                  .then_inc(w_landed[s], 16)
                                landed[s] += 16
                        continue
                    name, row0, col0, n, d0 = part
                    if name == "w_pool":
                        src = a["w_pool"][0].rearrange("g c d -> c g d")
                        dst = raw[s][:, 0:512].rearrange("p (g d) -> p g d", g=4)
                    else:
                        src = dram(name)[row0:row0 + kt * P, col0:col0 + n].rearrange("(k p) c -> p k c", p=P)
                        dst = raw[s][:, 0:kt * cols].rearrange("p (k c) -> p k c", k=kt)[:, :, d0:d0 + n]
                    sp.dma_start(dst, src).then_inc(w_landed[s], 16)
                    landed[s] += 16

            spill_at = 3
            back_at = next(p.unit for p in pl.pieces if p.name == ("y", 1, 0))
            meta_at = next(p.unit for p in pl.pieces if p.name == ("dn", 0)) + 1
            trig_at = next(p.unit for p in pl.pieces if p.name == ("dn", 6)) + 2
            gpost_at = next(p.unit for p in pl.pieces if p.name == ("hy", 1, 6))
            for u in range(NU):
                load(u)
                if u == 0:
                    for name, half, dst in ROW_LOADS:
                        src = a[name]
                        flat = {1: "(t p) -> t p", 2: "l (t p) -> (l t) p", 3: "l w (t p) -> (l w t) p"}[len(src.shape)]
                        r0, n = ROWS[dst]
                        n = 16 if name == "lb_logits" else n
                        r0 -= P * half
                        sp.dma_start(prow[r0:r0 + n, half, :], src.rearrange(flat, p=P)).then_inc(prm_in, 16)
                if u == 1:
                    sp.dma_start(cstage[:, 0:P], a["c_causal"]).then_inc(const_in, 16)
                    sp.dma_start(cstage[:, P:P + HEADS], a["c_pick"]).then_inc(const_in, 16)
                    sp.dma_start(cstage[:, P + HEADS:], a["c_level"]).then_inc(const_in, 16)
                    sp.dma_start(inv_n[:, :], a["c_inv"]).then_inc(const_in, 16)
                    with nc.allow_non_contiguous_dma(reason="sixteen biases, one for each of sixteen partitions"):
                        sp.dma_start(fbias[0:HEADS, :], a["fox_forget_b_2"].rearrange("l (h o) -> (l h) o", o=1))\
                           .then_inc(const_in, 16)
                if u == spill_at:
                    sp.wait_ge(norm1.z_ready, KT)
                    sp.dma_start(hspill, hT[:, :, :].rearrange("p k t -> p (k t)")).then_inc(spilled, 16)
                if u == back_at:
                    sp.wait_ge(oa_ready, 4)
                    sp.wait_ge(spilled, 16)
                    sp.dma_start(hT2[:, :, :].rearrange("p k t -> p (k t)"), hspill).then_inc(h_back, 16)
                if u == gpost_at:
                    sp.wait_ge(fox.o_done, HEADS)
                    sp.dma_start(gpost[:, :], a["post_norm_g_2"].broadcast_to([P, D])).then_inc(late_in, 16)
                if u == meta_at:
                    sp.wait_ge(norm2.z_ready, KT)
                    sp.wait_ge(g_ready, FT)
                    sp.dma_start(xm2[:, :], a["meta_tokens_2"]).then_inc(late_in, 16)
                if u == trig_at:
                    sp.wait_ge(pe_mark, pl.tile[("dn", 7)][1])
                    sp.dma_start(trig[:, :, :], a["c_trig"]).then_inc(late_in, 16)
            for i in range(QB):
                sp.wait_ge(fin_out, i + 1)
                sp.dma_start(out[0, P * i:P * (i + 1), :], mtok[:, i, :]).then_inc(out_done, 16)
            sp.wait_ge(out_done, 16 * QB)

        @block.gpsimd
        def _(pool):
            nc.gpsimd.memset(ident[:, :], 0.0).then_inc(const_ready, 1)
            nc.gpsimd.memset(ones[:, :], 1.0).then_inc(const_ready, 1)
            nc.gpsimd.memset(pair1[:, :], 0.0).then_inc(const_ready, 1)
            pool.wait_ge(const_ready, 3)
            nc.gpsimd.affine_select(out=ident[:, :], in_=ident[:, :], compare_op=ALU.not_equal, fill=1.0,
                                    base=0, pattern=[[-1, P]], channel_multiplier=1).then_inc(const_ready, 1)
            pool.wait_ge(const_ready, 4)
            nc.gpsimd.memset(pair1[0:64, 0:64], 1.0).then_inc(const_ready, 1)
            pool.wait_ge(const_ready, 5)
            nc.gpsimd.memset(pair1[64:P, 64:P], 1.0).then_inc(const_ready, 1)
            pool.wait_ge(const_ready, 6)
            landed = [0, 0]
            for u in range(NU):
                parts, kt, cols = pl.units[u]
                s, n = u % 2, kt * cols
                landed[s] += 16 * sum(6 if p[0] == "w_uq" else 1 for p in parts)
                pool.wait_ge(w_landed[s], landed[s])
                if pl.before[u] is not None:
                    pool.wait_ge(pe_mark, pl.unit_end[pl.before[u]])
                hi_, lo_ = hi[pl.slot[u]], lo[pl.slot[u]]
                if u == pl.pool_unit:
                    pool.wait_ge(spilled, 16)
                    hi_, lo_ = wphi, wplo
                nc.gpsimd.tensor_scalar(hi_[:, 0:n], raw[s][:, 0:n], 1.0, 1.0, ALU.mult, ALU.mult)\
                  .then_inc(w_split, 1)
                pool.wait_ge(w_split, 2 * u + 1)
                nc.gpsimd.tensor_tensor(lo_[:, 0:n], raw[s][:, 0:n], hi_[:, 0:n].bitcast(F32), ALU.subtract)\
                  .then_inc(w_split, 1)

        @block.tensor
        def _(pe):
            mm, tr = nc.tensor.matmul, nc.tensor.transpose
            X = {"z": (zhi, zlo), "ob": (obhi, oblo), "oa": (oahi, oalo), "g": (ghi, glo), "cq": (cqhi, cqlo),
                 "y": (yhi, ylo), "mx": (zhi, zlo)}
            at_piece = [0]

            def gemm_pair(names, x_wait):
                parts = [gemm_steps(name) for name in names]
                for k in range(KT):
                    pe.wait_ge(x_wait, k + 1)
                    ends = [step(k) for step in parts]
                for ins in ends:
                    ins.then_inc(pe_mark, 1)

            def gemm(name, x_wait=None):
                step = gemm_steps(name)
                p = pl.pieces[at_piece[0] - 1]
                for k in range(p.kt):
                    if x_wait is not None:
                        pe.wait_ge(x_wait, p.k0 + k + 1)
                    ins = step(k)
                ins.then_inc(pe_mark, 1)

            def gemm_steps(name):
                p = pl.pieces[at_piece[0]]
                assert p.name == name, (p.name, name)
                at_piece[0] += 1
                parts, kt, cols = pl.units[p.unit]
                s = pl.slot[p.unit]
                pe.wait_ge(w_split, 2 * p.unit + 2)
                slot, _, uses = pl.tile[name]
                if p.first and uses:
                    pe.wait_ge(acc_free[slot], uses)
                W = [t[:, 0:kt * cols].rearrange("p (k c) -> p k c", k=kt)
                     for t in ((wphi, wplo) if p.x == "pd" else (hi[s], lo[s]))]

                def step(k):
                    for w, x in ((0, 0), (0, 1), (1, 0)):
                        first = p.first and k == 0 and w == 0 and x == 0
                        last = p.last and k == p.kt - 1 and w == 1
                        if p.mode == "values":
                            t0, _ = chunk(p.k0)
                            lhs = (ckhi, cklo)[x][:, t0:t0 + P]
                            rhs = (hi, lo)[w][s][:, :].rearrange("p (h two c) -> p h two c", two=2, c=64)[
                                :, 8 * p.col:8 * p.col + 8, 1, :]
                            outs = [(PS[:, 2 * slot, :], lhs, rhs)]
                        elif p.mode == "tokens":
                            lhs = X["mx"][x][:, k, P * p.k0:P * p.k0 + P]
                            outs = [(PS[:, 2 * slot, 0:256], lhs, W[w][:, k, :])]
                        else:
                            lhs = W[w][:, k, p.col:p.col + P]
                            if p.x == "pd":
                                xs = (pdhi, pdlo)[x][p.k0 % 2][:, :]
                            elif p.x == "ckv":
                                xs = (ckhi, cklo)[x][:, :]
                            else:
                                xs = X[p.x][x][:, p.k0 + k, :]
                            if p.mode == "full":
                                outs = [(PS[:, 2 * slot + b, 0:HALF], lhs, xs[:, HALF * b:HALF * (b + 1)])
                                        for b in range(2)]
                            else:
                                t0 = NM if p.mode == "real" and p.x != "g" else 0
                                outs = [(PS[:, 2 * slot, :], lhs, xs[:, t0:t0 + SEQ])]
                        for o_, l_, r_ in outs:
                            ins = mm(o_, l_, r_, start=first, stop=last)
                    return ins

                return step

            def stats(n, lhs):
                if n.summed:
                    pe.wait_ge(n.added, n.K - 1)
                    for b in range(2):
                        ins = mm(PS[:, 6 + b, 0:HALF], lhs[:, :], n.rbb[:, HALF * b:HALF * (b + 1)],
                                 start=True, stop=True)
                    ins.then_inc(n.sq_used, 1)
                    return
                for k in range(n.K):
                    stats_of(n, lhs, k)

            def stats_of(n, lhs, k):
                pe.wait_ge(n.sq_ready, k + 1)
                for b in range(2):
                    ins = mm(PS[:, 6 + b, 0:HALF], lhs[:, :], n.sqb[k % 2][:, HALF * b:HALF * (b + 1)],
                             start=k == 0, stop=k == n.K - 1)
                ins.then_inc(n.sq_used, 1)

            pe.wait_ge(const_ready, 6)
            pe.wait_ge(x_in, 16 * (QB + 1))
            for k in range(KT):
                ins = tr(PS[:, 5, NM * k:NM * (k + 1)], xm[:, P * k:P * (k + 1)], ident[0:NM, 0:NM])
            ins.then_inc(x_turned, 1)
            for k in range(KT):
                if k == KT // 2:
                    pe.wait_ge(x2_in, 16 * QB)
                if k >= 4:
                    pe.wait_ge(h_copied, k - 4 + 2)
                for i in range(QB):
                    ins = tr(PS[:, k % 4, P * i:P * (i + 1)], xt[:, i, P * k:P * (k + 1)], ident[:, :])
                ins.then_inc(x_turned, 1)
                if k >= 3:
                    stats_of(norm1, ones, k - 3)
            pe.wait_ge(prm_in, PRM_DMAS)
            tr(PS[:, 4, 0:NROW1], prow[0:NROW1, 0, :], ident[0:NROW1, 0:NROW1])
            tr(PS[:, 4, P:P + NROW2], prow[0:NROW2, 1, :], ident[0:NROW2, 0:NROW2]).then_inc(prm_turned, 1)
            for k in range(KT - 3, KT):
                stats_of(norm1, ones, k)
            pe.wait_ge(h_copied, KT + 1)

            def turn_values(src, j, turned, copied, tile_name):
                tile_freed(pe, tile_name)
                if j:
                    pe.wait_ge(copied, 2 * j)
                tr(PS[0:NM, 5, 0:P], src[:, 0:NM], ident[:, :])
                for c in range(1, 5):
                    t0, n = chunk(c)
                    ins = tr(PS[:, 4, P * (c - 1):P * c], src[:, t0:t0 + n], ident[:, :])
                ins.then_inc(turned, 1)

            def rec_step(p, i):
                b = 9 * p
                if i == 0:
                    pe.wait_ge(mul_ready, 8 * p + 1)
                    e = E[b % 2]
                    for hh in range(2):
                        bank = 7 - hh
                        if p:
                            if hh == 0:
                                pe.wait_ge(s_ready, 4 * p)
                            pe.wait_ge(o_copied, 5 * p)
                        else:
                            pe.wait_ge(norm1.rb_ready, 1)
                        for c in range(4):
                            t0, n = chunk(c)
                            ins = tr(PS[0:n, bank, P * c:P * (c + 1)], e[:, hh, t0:t0 + n], ident[:, :])
                        ins.then_inc(kd_turned, 1)
                    return
                if 1 <= i <= 7:
                    j = i - 1
                    half, blk = 1 << j, 2 << j
                    e = E[(b + i) % 2]
                    use = 8 * p + j
                    bank = 4 + use % 2
                    pe.wait_ge(mul_ready, 8 * p + i + 1)
                    if use >= 2:
                        pe.wait_ge(sc_copied, use - 1)
                    elif use == 0:
                        pe.wait_ge(v_copied, 8)
                    if blk <= NM:
                        if j == 0:
                            pe.wait_ge(kdt_ready, 2 * p + 2)
                        for hh in range(2):
                            rhs = e[:, hh, 0:NM].rearrange("p (n b) -> p n b", b=blk)[:, :, half:blk]
                            mm(PS[0:NM, 6, 16 * j + 8 * hh:16 * j + 8 * hh + 8].rearrange("p (n b) -> p n b", b=half),
                               e[:, hh, 0:NM], rhs, start=True, stop=True)
                    for hh in range(2):
                        for c in range(1, 5):
                            t0, n = chunk(c)
                            it = 4 * hh + c - 1
                            m = 64 if j == 6 else P
                            rhs = e[:, hh, t0:t0 + n].rearrange("p (n b) -> p n b", b=blk)[:, :, half:blk]
                            ins = mm(PS[0:m, bank, 64 * it:64 * it + 64].rearrange("p (n b) -> p n b", b=half),
                                     e[:, hh, t0:t0 + m], rhs, start=True, stop=True)
                    ins.then_inc(sc_done, 1)
                    if i <= 4:
                        c = i - 1
                        t0, n = chunk(c)
                        if c == 0:
                            pe.wait_ge(kdt_ready, 2 * p + 2)
                        else:
                            pe.wait_ge(s_ready, 4 * p + c)
                        for hh in range(2):
                            h = 2 * p + hh
                            ins = mm(PS[:, 7, 64 * hh:64 * hh + 64], kdt[0:n, hh, c, :],
                                     vtok1[0:n, c, 64 * h:64 * h + 64], start=True, stop=True)
                        ins.then_inc(upd_done, 1)
                    return
                if i == 8:
                    use = 8 * p + 7
                    pe.wait_ge(sc_copied, use - 1)
                    q, k = qf[p % 2], kf[p % 2]
                    for hh in range(2):
                        mm(PS[0:NM, 6, 64 + 16 * hh:80 + 16 * hh], k[:, hh, 0:NM], q[:, hh, 0:NM], start=True, stop=True)
                        for c in range(1, 5):
                            t0, n = chunk(c)
                            it = 4 * hh + c - 1
                            for r in range(2):
                                ins = mm(PS[64 * r:64 * r + 64, 4 + use % 2, 64 * it:64 * it + 64],
                                         k[:, hh, t0 + 64 * r:t0 + 64 * r + 64],
                                         q[:, hh, t0 + 64 * r:t0 + 64 * r + 64], start=True, stop=True)
                    ins.then_inc(sc_done, 1)
                    return
                pe.wait_ge(qd_ready, p + 1)
                e = E[(b + 8) % 2]
                for c in range(5):
                    t0, n = chunk(c)
                    bank = 6 + c % 2
                    if c == 0:
                        pe.wait_ge(c0_copied, p + 1)
                    elif c == 1:
                        pe.wait_ge(s_ready, 4 * p + 4)
                        pe.wait_ge(sc_copied, 8 * p + 8)
                    else:
                        pe.wait_ge(o_copied, 5 * p + c - 1)
                    for hh in range(2):
                        h = 2 * p + hh
                        sc = sc0[:, hh, :] if c == 0 else scT[:, 4 * hh + c - 1, :]
                        dst = PS[64 * hh:64 * hh + 64, bank, 0:n]
                        ins = mm(dst, vtok1[0:n, c, 64 * h:64 * h + 64], sc, start=True, stop=c == 0)
                        if c:
                            ins = mm(dst, Sc[:, hh, c - 1, :], e[:, hh, t0:t0 + n], start=False, stop=True)
                    ins.then_inc(o_done, 1)

            pending = None
            for n, steps in order:
                if n[0] == "pool":
                    pe.wait_ge(pd_ready, n[1] + 1)
                if n == ("v", 0):
                    gemm_pair([("v", 0), ("v", 1)], norm1.z_ready)
                elif n != ("v", 1):
                    gemm(n)
                if pending is not None:
                    j = pending
                    turn_values(E[j % 2][:, 0, :], j, v_turned, v_copied, ("v", j))
                    pending = None
                if n[0] == "v":
                    pending = n[1]
                for p, i in steps:
                    rec_step(p, i)
            for t in range(4):
                for m in range(2):
                    if t + m:
                        gemm(("y", 0, 2 * t + m))
                pe.wait_ge(osq, t + 1)
                if t:
                    pe.wait_ge(orn, t)
                for r in range(2):
                    ins = mm(PS[:, 6 + r, 0:HALF], pair1[:, :], E[0][:, t % 2, HALF * r:HALF * (r + 1)],
                             start=True, stop=True)
                ins.then_inc(ossd, 1)
            for k in range(4, KT):
                gemm(("g", 1, k))
            pe.wait_ge(oa_ready, 4)
            for k in range(KT):
                gemm(("y", 1, k))
            gemm_pair([("out", 0), ("out", 1)], mixz_ready)
            for k in range(2, KT):
                gemm(("out", k))
            stats(norm2, ones)
            for j in range(FT // 2):
                if j == 0:
                    gemm_pair([("u", 0), ("u", 1)], norm2.z_ready)
                else:
                    for m in range(2):
                        gemm(("u", 2 * j + m))
                for m in range(2):
                    gemm(("vv", 2 * j + m))
            pe.wait_ge(g_ready, FT)
            for j in range(4):
                for i in range(3):
                    for m in range(2):
                        gemm(("dn", 2 * j + m))
                if j == 0:
                    pe.wait_ge(late_in, 16)
                    for k in range(KT):
                        ins = tr(PS[:, 5, NM * k:NM * (k + 1)], xm2[:, P * k:P * (k + 1)], ident[0:NM, 0:NM])
                    ins.then_inc(meta_turned, 1)
                if j == 1:
                    pe.wait_ge(fm_sq, 1)
                    mm(PS[:, 4, 0:P], ones[:, :], sqm[:, :, :].rearrange("p k t -> p (k t)"), start=True, stop=True)\
                        .then_inc(fm_done, 1)
            pe.wait_ge(fadd, 2 * (KT - 1))
            mm(PS[:, 6, :], ones[:, :], suma[:, :], start=True, stop=True).then_inc(fsum_done, 1)
            mm(PS[:, 7, :], ones[:, :], sumb[:, :], start=True, stop=True).then_inc(fsum_done, 1)
            tile_freed(pe, ("dn", 6))
            tile_freed(pe, ("dn", 7))

            def turn_h(*rs):
                for r in rs:
                    if r >= 2:
                        pe.wait_ge(ht_copied, r - 1)
                    for k in range(4):
                        ins = tr(PS[:, 4 + r % 2, P * k:P * (k + 1)],
                                 hT[:, 4 * (r % 2) + k, NM + P * (r // 2):NM + P * (r // 2 + 1)], ident[:, :])
                    ins.then_inc(ht_turned, 1)

            pe.wait_ge(fm_z, 2)
            gemm_pair([("cq", 0), ("cq", 1)], h1_lo)
            pe.wait_ge(h1_ready, KT)
            turn_h(0, 1)
            turn_h(2, 3)
            gemm(("ckv", 0))
            stats(normq, ones)
            turn_h(4, 5)
            pe.wait_ge(normq.rb_ready, 1)
            stats(normk, ones)
            gemm(("kpe", 0))
            turn_h(6, 7)
            for i in range(5):
                for j in range(2):
                    gemm(("mv", i, j), normk.z_ready if i + j == 0 else None)

            def scores(A, h, i):
                if 4 * h + i >= 2:
                    pe.wait_ge(A.p_exp, 4 * h + i - 1)
                if i == 0:
                    if A is mla:
                        tile_freed(pe, ("mk", h))
                    else:
                        pe.wait_ge(fox_lo, 3 * (h + 1))
                t0, n = P * i, ATT_N[i]
                if i == 3:
                    cuts, tail = [(PS[:, 5, 0:264], 0), (PS[:, 6, 0:136], 264)], PS[:, 6, 136:264]
                else:
                    bank = 4 if i % 2 == 0 else 5
                    cuts, tail = [(PS[:, bank, 0:n - P], 0)], PS[:, bank, n - P:n]
                for dst, c0 in cuts + [(tail, n - P)]:
                    last = dst is tail
                    c1 = c0 + dst.shape[-1]
                    if A is mla:
                        ins = mm(dst, qh[h % 2][:, t0:t0 + P], kh[h % 2][:, c0:c1], start=True, stop=not last)
                    else:
                        i_ = h % 2
                        mm(dst, xqa[i_][:, t0:t0 + P], xka[i_][:, c0:c1], start=True, stop=False)
                        ins = mm(dst, xqb[i_][:, t0:t0 + P], xkb[i_][:, c0:c1], start=False, stop=not last)
                    if last:
                        ins = mm(dst, identb[:, :], causalb[:, :], start=False, stop=True)
                ins.then_inc(A.s_done, 1)

            def turn(A, h, g):
                if g == 0:
                    pe.wait_ge(A.p_ready, h + 1)
                done = A.pt_a if g % 2 == 0 else A.pt_v
                if 2 * h + g // 2:
                    pe.wait_ge(done, 2 * h + g // 2)
                for x, (j, i) in enumerate(GROUPS[g]):
                    o_ = ATT_OFF[i] + (0 if j == 0 else NM + P * (j - 1))
                    n = NM if j == 0 else P
                    ins = tr(PS[0:n, 2 + g % 2, P * x:P * (x + 1)], Pm[h % 2][:, o_:o_ + n], ident[:, :])
                ins.then_inc(A.g_turned, 1)

            def weigh(A, h):
                pe.wait_ge(A.pt_a, 2 * h + 2)
                pe.wait_ge(A.pt_v, 2 * h + 2)
                if h:
                    pe.wait_ge(A.o_ready, h)
                r = 64 * (h % 2)
                for j, (c0, q0, n) in enumerate(((0, 0, 512), (512, 0, 512), (1024, 128, 384), (1408, 256, 256),
                                                 (1664, 384, 128))):
                    rows = NM if j == 0 else P
                    ins = mm(PS[r:r + 64, 7, q0:q0 + n], vtok[0:rows, j, 64 * h:64 * h + 64],
                             PT[h % 2][0:rows, c0:c0 + n], start=j == 0, stop=j == 4, skip_group_check=True)
                ins.then_inc(A.o_done, 1)

            def attention(A, project, between):
                for h in range(HEADS + 2):
                    project(h)
                    if h < HEADS:
                        scores(A, h, 0)
                        scores(A, h, 1)
                    if h >= 2:
                        weigh(A, h - 2)
                    between(h)
                    for i in range(4):
                        if 1 <= h <= HEADS:
                            turn(A, h - 1, i)
                        if h < HEADS and i < 2:
                            scores(A, h, i + 2)

            def mla_project(h):
                for x in ([0, 1] if h == 0 else [h + 1]):
                    if x < HEADS:
                        gemm(("mq", x), normq.z_ready if x == 0 else None)
                        if h == 0:
                            gemm(("mk", x))

            def mla_between(h):
                if 1 <= h < HEADS - 1:
                    gemm(("mk", h + 1))

            pe.wait_ge(ht_copied, 8)
            pe.wait_ge(kr_ready, 1)
            for i, j in ((4, 0), (4, 1)):
                tile_freed(pe, ("mv", i, j))
            attention(mla, mla_project, mla_between)
            pe.wait_ge(mla.pt_a, 2 * HEADS)
            pe.wait_ge(mla.pt_v, 2 * HEADS)
            for k in range(KT):
                gemm(("mz", k))

            def gates(b):
                for j in range(4):
                    for m in range(2):
                        gemm(("hg", b, 2 * j + m))
                    if j == 0:
                        pe.wait_ge(y_ready, KT * (b + 1))
                    for m in range(2):
                        gemm(("hy", b, 2 * j + m))

            gates(0)
            for k in range(KT):
                gemm(("xv", k))
                if k:
                    turn_values(nzt[(k - 1) % 2][:, :], k - 1, xv_turned, xv_copied, ("xv", k - 1))
            turn_values(nzt[(KT - 1) % 2][:, :], KT - 1, xv_turned, xv_copied, ("xv", KT - 1))
            pe.wait_ge(xv_copied, 2 * KT)

            def fox_project(h):
                if h == 0:
                    gemm(("xq", 0))
                    gemm(("xk", 0))
                    gemm(("xq", 1))

            def fox_between(h):
                x = h // 2 + 1 + h % 2
                if x < KT:
                    gemm((("xk", "xq")[h % 2], x))

            pe.wait_ge(acc_free[1], pl.tile[("xv", KT - 1)][2] + 1)
            attention(fox, fox_project, fox_between)
            pe.wait_ge(fox.pt_a, 2 * HEADS)
            pe.wait_ge(fox.pt_v, 2 * HEADS)
            for k in range(KT):
                gemm(("xz", k))
            gates(1)
            gemm_pair([("fin", 0, 0), ("fin", 0, 1)], fmix)
            for j in range(4):
                for i in range(QB):
                    if j or i >= 2:
                        gemm(("fin", j, i))
            assert at_piece[0] == len(pl.pieces)

        @block.scalar
        def _(act):
            steps, table = [0], [None]

            def A_(out_, in_, func, **kw):
                if func in (ACT.Silu, ACT.Sigmoid):
                    table[0] = func
                assert func not in (ACT.Exp, ACT.Ln) or table[0] == "log_exp"
                return nc.scalar.activation(out_, in_, func, **kw)

            def log_exp():
                if table[0] != "log_exp":
                    nc.scalar.preload_act_table_set("natural_log_exp_and_others")
                table[0] = "log_exp"

            def tick(ins):
                steps[0] += 1
                ins.then_inc(act_step, 1)

            def settle():
                act.wait_ge(act_step, steps[0])

            def norm_sq(n, k):
                dst = n.sqb[k % 2]
                if n.summed:
                    if k == 0:
                        dst = n.rbb
                    elif k >= 3:
                        act.wait_ge(n.added, k - 2)
                elif k >= 2:
                    act.wait_ge(n.sq_used, k - 1)
                A_(dst[:, :], n.src(k), ACT.Square).then_inc(n.sq_ready, 1)

            def norm_rb(n):
                log_exp()
                act.wait_ge(n.sq_used, 1 if n.summed else n.K)
                tick(A_(halves(n.rbb[:, :]), PS[:, 6:8, 0:HALF], ACT.Ln, scale=1.0 / n.width, bias=epst))
                settle()
                A_(n.rbb[:, :], n.rbb[:, :], ACT.Exp, scale=-0.5).then_inc(n.rb_ready, 1)

            def norm_hi(n, k):
                act.wait_ge(n.zt_ready, k + 1)
                A_(n.dst(k)[0], n.ztb[k % 2][:, :], ACT.Copy).then_inc(n.zhi_ready, 1)

            for k in range(KT):
                act.wait_ge(h_copied, k + 2)
                norm_sq(norm1, k)
            log_exp()
            act.wait_ge(lb_sub, 1)
            A_(lbe, lbt, ACT.Exp).then_inc(lb_exp, 1)
            norm_rb(norm1)
            for k in range(KT):
                norm_hi(norm1, k)

            def rec_step(p, i):
                b = 9 * p

                def level_exp(x):
                    log_exp()
                    act.wait_ge(sub_ready, 8 * p + x + 1)
                    t = E[(b + x) % 2]
                    v = t[:, :, 0:400] if x == 0 else t[:, :, NM:T] if x - 1 >= 4 else t[:, :, :]
                    A_(v, v, ACT.Exp).then_inc(exp_ready, 1)

                if i == 0:
                    log_exp()
                    act.wait_ge(a_ready, 2 * p + 2)
                    if p:
                        act.wait_ge(s_ready, 4 * p)
                    tick(A_(el, av[p % 2][:, :, NM - 1:400:P], ACT.Exp))
                    level_exp(0)
                elif i <= 6:
                    level_exp(i + 1)
                elif i == 7:
                    log_exp()
                    act.wait_ge(sc_done, 8 * p + 6)
                    A_(E[(b + 8) % 2][:, :, :], av[p % 2][:, :, :], ACT.Exp).then_inc(qd_exp, 1)
                elif i == 9:
                    for c in range(5):
                        t0, n = chunk(c)
                        act.wait_ge(o_done, 5 * p + c + 1)
                        A_(oT[:, p, t0:t0 + n], PS[:, 6 + c % 2, 0:n], ACT.Copy).then_inc(o_copied, 1)

            def rec_after(p):
                log_exp()
                act.wait_ge(sub_ready, 8 * p + 2)
                t = E[(9 * p + 1) % 2][:, :, :]
                A_(t, t, ACT.Exp).then_inc(exp_ready, 1)
                for hh in range(2):
                    act.wait_ge(kd_turned, 2 * p + hh + 1)
                    tick(A_(kdt[0:NM, hh, 0, :], PS[0:NM, 7 - hh, 0:P], ACT.Copy))
                    A_(kdt[:, hh, 1:4, :], PS[:, 7 - hh, P:4 * P].rearrange("p (c k) -> p c k", c=3), ACT.Copy)\
                        .then_inc(kdt_ready, 1)

            for name, hooks in order:
                kind, h = name[0:2]
                p, hh = h // 2, h % 2
                for step in sorted(hooks, reverse=True):
                    rec_step(*step)
                if kind == "y":
                    continue
                tile_done(act, name)
                src = acc_full(name)
                if kind == "v":
                    if h >= 2:
                        act.wait_ge(v_turned, h - 1)
                    tile_free(A_(halves(E[h % 2][:, 0, :]), src, ACT.Copy), name)
                elif kind == "q":
                    if p >= 2:
                        act.wait_ge(o_done, 5 * (p - 1))
                    tile_free(A_(halves(qf[p % 2][:, hh, :]), src, ACT.Silu), name)
                elif kind == "f":
                    if p >= 2:
                        act.wait_ge(o_done, 5 * (p - 1))
                    tile_free(A_(halves(kf[p % 2][:, hh, :]), src, ACT.Sigmoid, bias=col("bf", h)), name)
                    log_exp()
                    act.wait_ge(f_ready, h + 1)
                    t = av[p % 2][:, hh, :]
                    A_(t, t, ACT.Ln).then_inc(ln_ready, 1)
                elif kind == "og":
                    tile_free(A_(halves(og[:, h, :]), src, ACT.Silu), name)
                elif kind == "pool":
                    A_(halves(obhi[:, h, :]), src, ACT.Copy, scale=col("pscale", h)).then_inc(obhi_ready, 1)
                elif kind == "g":
                    if name == ("g", 0, 0):
                        tile_done(act, ("pool", 3))
                    if name == ("g", 1, 0):
                        act.wait_ge(pd_ready, 4)
                    dst = mix[:, name[2], :] if h == 0 else ga(name[2])
                    tile_free(A_(halves(dst), src, ACT.Sigmoid), name)
                else:
                    tile_free(A_(halves(pin[:, h, PADC:]), src, ACT.Copy), name)
                if hooks and hooks[-1][1] == 0:
                    rec_after(hooks[-1][0])

            act.wait_ge(o_copied, 20)
            for t in range(2):
                A_(E[0][:, t, :], oT[:, t, :], ACT.Square).then_inc(osq, 1)
            log_exp()
            for t in range(4):
                act.wait_ge(ossd, t + 1)
                if t >= 2:
                    act.wait_ge(on_ready, t - 1)
                tick(A_(halves(E[1][:, t % 2, :]), PS[:, 6:8, 0:HALF], ACT.Ln, scale=1.0 / A_VDIM, bias=epst))
                settle()
                A_(E[1][:, t % 2, :], E[1][:, t % 2, :], ACT.Exp, scale=-0.5).then_inc(orn, 1)
                act.wait_ge(on_ready, t + 1)
                A_(oahi[:, t, :], oT[:, t, :], ACT.Copy).then_inc(oahi_ready, 1)
                if t < 2:
                    A_(E[0][:, t, :], oT[:, t + 2, :], ACT.Square).then_inc(osq, 1)
            for k in range(4, KT):
                tile_done(act, ("g", 1, k))
                tile_free(A_(halves(ga(k)), acc_full(("g", 1, k)), ACT.Sigmoid), ("g", 1, k))

            for k in range(KT):
                act.wait_ge(mix_ready, k + 1)
                A_(zhi[:, k, :], mix[:, k, :], ACT.Copy).then_inc(mixhi_ready, 1)
            for k in range(KT):
                tile_freed(act, ("out", k))
                norm_sq(norm2, k)
            norm_rb(norm2)
            for k in range(KT):
                norm_hi(norm2, k)

            for j in range(FT // 2):
                for k in (2 * j, 2 * j + 1):
                    tile_done(act, ("u", k))
                    if k >= 2:
                        act.wait_ge(c_ready, k - 1)
                    tile_free(A_(halves(ub[k % 2][:, :]), acc_full(("u", k)), ACT.Copy), ("u", k))
                for k in (2 * j, 2 * j + 1):
                    act.wait_ge(c_ready, k + 1)
                    A_(cb[k % 2][:, :], cb[k % 2][:, :], ACT.Silu).then_inc(silu_ready, 1)
                for k in (2 * j, 2 * j + 1):
                    tile_freed(act, ("vv", k))
                    A_(ghi[:, k, :], gt[k % 2][:, :], ACT.Copy).then_inc(ghi_ready, 1)

            log_exp()
            for k in range(KT):
                tile_freed(act, ("dn", k))
                if k >= 3:
                    act.wait_ge(fadd, 2 * (k - 2))
                A_((qa[k % 2] if k else suma)[:, :], hT[:, k, NM:T], ACT.Square).then_inc(fsq, 1)
                A_((qb[k % 2] if k else sumb)[:, :], hT[:, k, NM:T], ACT.Square, scale=col("final", k)).then_inc(fsq, 1)
                if k == 2:
                    act.wait_ge(h1_meta, 1)
                    A_(sqm[:, :, :], hT[:, :, 0:NM], ACT.Square).then_inc(fm_sq, 1)
                if k == 4:
                    act.wait_ge(fm_done, 2)
                    tick(A_(rm[:, :], rm[:, :], ACT.Ln, scale=1.0 / D, bias=epst))
                    settle()
                    A_(rm[:, :], rm[:, :], ACT.Exp, scale=-0.5).then_inc(fm_rb, 1)
                if k == 5:
                    act.wait_ge(fm_z, 1)
                    A_(zhi[:, :, 0:NM], zm[:, :, :], ACT.Copy).then_inc(fm_hi, 1)
            act.wait_ge(fsum_done, 1)
            A_(r1l[:, :], PS[:, 6, :], ACT.Ln, scale=1.0 / D, bias=epst).then_inc(r1_log, 1)
            act.wait_ge(r1_log, 1)
            A_(r2t[:, :], r1l[:, :], ACT.Exp, scale=-1.0).then_inc(r1sq, 1)
            act.wait_ge(r2in, 1)
            A_(r2t[:, :], r2t[:, :], ACT.Ln, scale=1.0 / D, bias=epst).then_inc(r2log, 1)
            act.wait_ge(r2in, 2)
            A_(nrb[:, NM:T], r2t[:, :], ACT.Exp, scale=-0.5).then_inc(rz_ready, 1)
            A_(r1[:, :], r1l[:, :], ACT.Exp, scale=-0.5).then_inc(r1_ready, 1)
            for k in range(KT):
                act.wait_ge(h1_z, k + 1)
                A_(zhi[:, k, NM:T], nzt[k % 2][:, NM:T], ACT.Copy).then_inc(h1_hi, 1)

            def h_out(*rs):
                for r in rs:
                    act.wait_ge(ht_turned, r + 1)
                    A_(htok[:, r // 2, SEQ * (r % 2):SEQ * (r % 2 + 1)], PS[:, 4 + r % 2, :], ACT.Copy)\
                        .then_inc(ht_copied, 1)

            def compressed(k, name):
                tile_done(act, name)
                tile_free(A_(halves(cqT[:, k, :]), acc_full(name), ACT.Copy), name)
                tile_freed(act, name)

            for k in range(2):
                compressed(k, ("cq", k))
                act.wait_ge(h1_ready, KT)
                norm_sq(normq, k)
                h_out(2 * k, 2 * k + 1)
            compressed(2, ("ckv", 0))
            norm_rb(normq)
            norm_sq(normk, 0)
            h_out(4, 5)
            act.wait_ge(normq.zt_ready, 2)
            norm_rb(normk)
            for k in range(2):
                norm_hi(normq, k)
            norm_hi(normk, 0)
            tile_done(act, ("kpe", 0))
            f0, f1 = fgt[0:HEADS, 0, :], fgt[0:HEADS, 1, :]
            A_(halves(f0), acc_full(("kpe", 0), slice(0, HEADS)), ACT.Identity, bias=fbias[0:HEADS, :])\
                .then_inc(fl_ready, 1)
            act.wait_ge(fl_ready, 1)
            tick(A_(f1, f0, ACT.Abs))
            settle()
            tick(A_(f1, f1, ACT.Exp, scale=-1.0))
            settle()
            A_(f1, f1, ACT.Ln, bias=ones[0:HEADS, 0:1]).then_inc(fl_abs, 1)
            h_out(6, 7)

            def k_out(x):
                tile_done(act, ("mk", x))
                if x >= 2:
                    act.wait_ge(mla.s_done, 4 * (x - 1))
                tile_free(A_(halves(kh[x % 2][0:NOPE, :]), acc_full(("mk", x), slice(0, NOPE)), ACT.Copy), ("mk", x))

            def attention(A, project, ahead, after):
                log_exp()
                for h in range(HEADS + 2):
                    project(h)
                    for i in range(4):
                        if h < HEADS:
                            if h >= 2 and i == 0:
                                act.wait_ge(A.g_turned, 4 * (h - 1))
                            act.wait_ge(A.m_ready, 4 * h + i + 1)
                            s = 4 * (h % 2) + i
                            dst = Pm[h % 2][:, ATT_OFF[i]:ATT_OFF[i] + ATT_N[i]]
                            dst = halves(dst) if i == 3 else dst
                            A_(dst, s_view(i), ACT.Exp, bias=negmax[:, s:s + 1],
                               accum_out=rowsum[:, s:s + 1]).then_inc(A.p_exp, 1)
                        if i == 1:
                            ahead(h)
                        if h >= 2 and i == 1:
                            x, r = h - 2, 64 * (h % 2)
                            act.wait_ge(A.o_done, x + 1)
                            A_(omla[r:r + 64, x // 2, :], PS[r:r + 64, 7, :], ACT.Copy).then_inc(A.o_ready, 1)
                        if 1 <= h <= HEADS and i in (1, 3):
                            x, g = h - 1, i - 1
                            act.wait_ge(A.g_turned, 4 * x + g + 1)
                            if x >= 2:
                                act.wait_ge(A.o_done, x - 1)
                            rows, n = (NM, 512) if g == 0 else (P, 384)
                            A_(PT[x % 2][0:rows, G_COL[g]:G_COL[g] + n], PS[0:rows, 2, 0:n], ACT.Copy)\
                                .then_inc(A.pt_a, 1)
                        if i == 2:
                            after(h)

            def mla_project(h):
                if h == 0:
                    k_out(0)
                    k_out(1)

            def mla_after(h):
                if 1 <= h < HEADS - 1:
                    k_out(h + 1)

            attention(mla, mla_project, lambda h: None, mla_after)

            def gated(kind, A, b):
                act.wait_ge(A.o_ready, HEADS)
                for k in range(KT):
                    tile_done(act, (kind, k))
                    if k >= 2:
                        act.wait_ge(ygt, KT * b + k - 1)
                    tile_free(A_(nsq[k % 2][:, 0:SEQ], acc_real((kind, k)), ACT.Silu), (kind, k))
                    act.wait_ge(ygt, KT * b + k + 1)
                    A_(yhi[:, k, :], nzt[k % 2][:, 0:SEQ], ACT.Copy).then_inc(yhi_r, 1)

            def gates(b):
                act.wait_ge(y_ready, KT * (b + 1))
                for k in range(KT):
                    if k >= 2:
                        tile_freed(act, ("hy", b, k - 2))
                    tile_done(act, ("hg", b, k))
                    tile_free(A_(nsq[k % 2][:, 0:SEQ], acc_real(("hg", b, k)), ACT.Sigmoid), ("hg", b, k))

            gated("mz", mla, 0)
            gates(0)
            for k in range(KT):
                tile_done(act, ("xv", k))
                if k >= 2:
                    act.wait_ge(xv_turned, k - 1)
                tile_free(A_(halves(nzt[k % 2][:, :]), acc_full(("xv", k)), ACT.Copy), ("xv", k))

            def fq_out(x):
                tile_done(act, ("xq", x))
                if x >= 2:
                    act.wait_ge(fox_lo, 3 * (2 * x - 2))
                tile_free(A_(fq[x % 2][:, :], acc_real(("xq", x)), ACT.Copy, scale=FOX_SCALE), ("xq", x))

            def fk_out(x):
                tile_done(act, ("xk", x))
                if x:
                    act.wait_ge(fox_lo, 3 * 2 * x)
                tile_free(A_(halves(fk[:, :]), acc_full(("xk", x)), ACT.Copy), ("xk", x))

            def split_hi(h):
                i, r = h % 2, slice(64 * (h % 2), 64 * (h % 2) + 64)
                o = slice(64 - r.start, 128 - r.start)
                if h >= 2:
                    act.wait_ge(fox.s_done, 4 * (h - 1))
                tile_freed(act, ("xq", h // 2))
                tile_freed(act, ("xk", h // 2))
                q = fq[h // 2 % 2]
                A_(xqa[i][r, :], q[r, :], ACT.Copy).then_inc(fox_hi, 1)
                A_(xka[i][r, :], fk[r, :], ACT.Copy).then_inc(fox_hi, 1)
                A_(xqb[i][r, :], q[r, :], ACT.Copy).then_inc(fox_hi, 1)
                A_(xka[i][o, :], fk[r, :], ACT.Copy).then_inc(fox_hi, 1)

            def fox_project(h):
                if h == 0:
                    act.wait_ge(xv_turned, KT)
                    fq_out(0)
                    fk_out(0)
                    split_hi(0)
                    fq_out(1)

            def fox_ahead(h):
                if h < HEADS - 1:
                    split_hi(h + 1)

            def fox_after(h):
                x = h // 2 + 1 + h % 2
                if x < KT:
                    (fk_out, fq_out)[h % 2](x)

            attention(fox, fox_project, fox_ahead, fox_after)
            gated("xz", fox, 1)
            gates(1)
            tile_done(act, ("hg", 1, 7))
            for k in range(KT):
                act.wait_ge(mix2_ready, k + 1)
                A_(zhi[:, k, 0:SEQ], mix2[:, k, :], ACT.Copy).then_inc(fmixhi, 1)
            log_exp()
            for j in range(4):
                for i in range(QB):
                    n = ("fin", j, i)
                    tile_done(act, n)
                    A_(fjunk[:, j, i, :], acc_real(n, n=256), ACT.Square, accum_out=fsum[:, 4 * i + j:4 * i + j + 1])\
                        .then_inc(fin_sq, 1)
                    if j == 3:
                        v = ssum[:, i:i + 1]
                        act.wait_ge(fin_sum, i + 1)
                        tick(A_(v, v, ACT.Ln, scale=1.0 / D, bias=epst))
                        settle()
                        A_(v, v, ACT.Exp, scale=-0.5).then_inc(fin_rstd, 1)

        @block.vector
        def _(dve):
            V = nc.vector
            steps = [0]

            def tick(ins):
                steps[0] += 1
                ins.then_inc(dve_step, 1)

            def settle():
                dve.wait_ge(dve_step, steps[0])

            def norm_add(n, k):
                if k:
                    dve.wait_ge(n.sq_ready, k + 1)
                    if k > 1:
                        dve.wait_ge(n.added, k - 1)
                    V.tensor_tensor(n.rbb[:, :], n.rbb[:, :], n.sqb[k % 2][:, :], ALU.add).then_inc(n.added, 1)

            tick(V.memset(epst, EPS))
            tick(V.memset(rmask[:, :], 1.0))
            tick(V.memset(pin[:, :, 0:PADC], 0.0))
            tick(V.memset(scT[:, :, :], 0.0))
            tick(V.memset(sc0[:, :, :], 0.0))
            settle()
            for c in range(5):
                tick(V.memset(rmask[:, chunk(c)[0]:chunk(c)[0] + 1], 0.0))
            dve.wait_ge(x_turned, 1)
            V.tensor_copy(hT[:, :, 0:NM], PS[:, 5, 0:P].rearrange("p (k t) -> p k t", k=KT)).then_inc(h_copied, 1)
            for k in range(KT):
                dve.wait_ge(x_turned, k + 2)
                V.tensor_copy(hT[:, k, NM:T], PS[:, k % 4, :]).then_inc(h_copied, 1)
            dve.wait_ge(prm_turned, 1)
            tick(V.tensor_copy(prm[:, 0:NROW1], PS[:, 4, 0:NROW1]))
            tick(V.tensor_copy(prm[:, P:P + NROW2], PS[:, 4, P:P + NROW2]))
            settle()
            l0, l1 = prm[:, 8:16], prm[:, 16:24]
            tick(V.tensor_tensor(lb, l0, l1, ALU.max))
            settle()
            tick(V.tensor_tensor(lbt[:, 0:8], l0, lb, ALU.subtract))
            V.tensor_tensor(lbt[:, 8:16], l1, lb, ALU.subtract).then_inc(lb_sub, 1)
            dve.wait_ge(lb_exp, 1)
            tick(V.tensor_tensor(omlb, lbe[:, 0:8], lbe[:, 8:16], ALU.add))
            settle()
            tick(V.reciprocal(omlb, omlb))
            settle()
            tick(V.tensor_tensor(lb, lbe[:, 0:8], omlb, ALU.mult))
            settle()
            tick(V.tensor_scalar(lb, lb, 2.0 ** -63, None, ALU.max))
            settle()
            tick(V.tensor_scalar(omlb, lb, -1.0, 1.0, ALU.mult, ALU.add))
            dve.wait_ge(const_in, 16 * 5)
            dve.wait_ge(const_ready, 6)
            tick(V.tensor_copy(causalb[:, :], cstage[:, 0:P]))
            tick(V.tensor_copy(identb[:, :], ident[:, :]))
            tick(V.tensor_copy(pick[:, :], cstage[:, P:P + HEADS]))
            tick(V.tensor_copy(lvl[:, :], cstage[:, P + HEADS:]))
            settle()

            def norm_zt(n, k):
                if k == 0:
                    dve.wait_ge(n.rb_ready, 1)
                V.scalar_tensor_tensor(out=n.ztb[k % 2][:, :], in0=n.src(k), scalar=col(n.gain, k),
                                       in1=n.rbb[:, :], op0=ALU.mult, op1=ALU.mult).then_inc(n.zt_ready, 1)

            def norm_lo(n, k):
                dve.wait_ge(n.zhi_ready, k + 1)
                h_, l_ = n.dst(k)
                V.tensor_tensor(l_, n.ztb[k % 2][:, :], h_.bitcast(F32), ALU.subtract).then_inc(n.z_ready, 1)

            def norm_split(n):
                for k in range(n.K + 1):
                    if k < n.K:
                        if k >= 2:
                            dve.wait_ge(n.z_ready, k - 1)
                        norm_zt(n, k)
                    if k >= 1:
                        norm_lo(n, k - 1)

            norm_split(norm1)

            def values_out(j, turned, copied, dst):
                dve.wait_ge(turned, j + 1)
                V.tensor_copy(dst[0:NM, 0, P * j:P * (j + 1)], PS[0:NM, 5, 0:P]).then_inc(copied, 1)
                V.tensor_copy(dst[:, 1:5, P * j:P * (j + 1)], PS[:, 4, :].rearrange("p (c f) -> p c f", c=4))\
                 .then_inc(copied, 1)

            def rec_step(p, i):
                b = 9 * p
                q, kk, ac = qf[p % 2], kf[p % 2], av[p % 2]

                def free(x):
                    if x == 0:
                        if p:
                            dve.wait_ge(sc_done, 8 * p - 1)
                        else:
                            dve.wait_ge(v_turned, 4)
                    elif x == 1:
                        if p:
                            dve.wait_ge(o_done, 5 * p)
                    elif x == 2:
                        dve.wait_ge(kd_turned, 2 * p + 2)
                    else:
                        dve.wait_ge(sc_done, 8 * p + x - 2)

                def sub(x):
                    free(x)
                    t = E[(b + x) % 2]
                    if x == 0:
                        dve.wait_ge(a_ready, 2 * p + 2)
                        tick(V.tensor_tensor(t[:, :, 0:NM], ac[:, :, NM - 1:NM].broadcast_to([P, 2, NM]),
                                             ac[:, :, 0:NM], ALU.subtract))
                        sv = lambda z: z[:, :, NM:400].rearrange("p h (c t) -> p h c t", t=CH)
                        V.tensor_tensor(sv(t), sv(ac)[:, :, :, CH - 1:CH].broadcast_to([P, 2, 3, CH]), sv(ac),
                                        ALU.subtract).then_inc(sub_ready, 1)
                        return
                    tl, tr_, _, shape = level_views(t, x - 1)
                    al, ar, mid, _ = level_views(ac, x - 1)
                    tick(V.tensor_tensor(tl, mid.broadcast_to(shape), al, ALU.subtract))
                    V.tensor_tensor(tr_, ar, mid.broadcast_to(shape), ALU.subtract).then_inc(sub_ready, 1)

                def mul(x):
                    dve.wait_ge(exp_ready, 8 * p + x + 1)
                    t = E[(b + x) % 2]
                    if x == 0:
                        V.tensor_tensor(t[:, :, 0:400], t[:, :, 0:400], kk[:, :, 0:400], ALU.mult).then_inc(mul_ready, 1)
                        return
                    tl, tr_, _, _ = level_views(t, x - 1)
                    ql = level_views(q, x - 1)[1]
                    kl = level_views(kk, x - 1)[0]
                    tick(V.tensor_tensor(tr_, tr_, ql, ALU.mult))
                    V.tensor_tensor(tl, tl, kl, ALU.mult).then_inc(mul_ready, 1)

                def evac(j):
                    use = 8 * p + j
                    bank = 4 + use % 2
                    dve.wait_ge(sc_done, use + 1)
                    if use:
                        dve.wait_ge(sc_copied, use)
                    if j == 0 and p:
                        dve.wait_ge(o_done, 5 * p)
                    if j == 6:
                        V.tensor_copy(scT[0:64, :, 64:P], PS[0:64, bank, :].rearrange("p (i t) -> p i t", i=8))\
                         .then_inc(sc_copied, 1)
                        return
                    if j == 7:
                        for r in range(2):
                            rows = slice(64 * r, 64 * r + 64)
                            ins = V.copy_predicated(scT[rows, :, 64 * r:64 * r + 64],
                                                    lvl[rows, 448:512].unsqueeze(1).broadcast_to([64, 8, 64]),
                                                    PS[rows, bank, :].rearrange("p (i t) -> p i t", i=8))
                            if r == 0:
                                tick(ins)
                        ins.then_inc(sc_copied, 1)
                        return
                    half, blk = 1 << j, 2 << j
                    n = P // blk
                    m = lvl[:, 64 * j:64 * j + 64].rearrange("p (n b) -> p n b", b=half).unsqueeze(1)
                    V.copy_predicated(scT[:, :, :].rearrange("p i (n b) -> p i n b", b=blk)[:, :, :, half:blk],
                                      m.broadcast_to([P, 8, n, half]),
                                      PS[:, bank, :].rearrange("p (i n b) -> p i n b", i=8, b=half)).then_inc(sc_copied, 1)

                def state(c):
                    dve.wait_ge(upd_done, 4 * p + c + 1)
                    if c == 0:
                        V.tensor_copy(Sc[:, :, 0, :], PS[:, 7, 0:P].rearrange("p (h v) -> p h v", h=2)).then_inc(s_ready, 1)
                        return
                    dve.wait_ge(s_ready, 4 * p + c)
                    for hh in range(2):
                        ins = V.scalar_tensor_tensor(out=Sc[:, hh, c, :], in0=Sc[:, hh, c - 1, :], scalar=el[:, hh, c:c + 1],
                                                     in1=PS[:, 7, 64 * hh:64 * hh + 64], op0=ALU.mult, op1=ALU.add)
                        if hh == 0:
                            tick(ins)
                    ins.then_inc(s_ready, 1)

                if i == 0:
                    for hh in range(2):
                        tile_freed(dve, ("q", 2 * p + hh))
                    sub(0)
                    mul(0)
                    sub(1)
                elif i <= 7:
                    if 2 <= i <= 5:
                        state(i - 2)
                    if i <= 6:
                        sub(i + 1)
                    mul(i)
                    if i >= 2:
                        evac(i - 2)
                elif i == 9:
                    evac(6)
                    dve.wait_ge(qd_exp, p + 1)
                    t = E[(b + 8) % 2]
                    V.tensor_tensor(t[:, :, :], t[:, :, :], q[:, :, :], ALU.mult).then_inc(qd_ready, 1)
                    evac(7)
                    for j in range(4):
                        half, blk = 1 << j, 2 << j
                        n = NM // blk
                        m = lvl[0:NM, 64 * j:64 * j + 8].rearrange("p (n b) -> p n b", b=half).unsqueeze(1)
                        tick(V.copy_predicated(
                            sc0[:, :, :].rearrange("p i (n b) -> p i n b", b=blk)[:, :, :, half:blk],
                            m.broadcast_to([NM, 2, n, half]),
                            PS[0:NM, 6, 16 * j:16 * j + 16].rearrange("p (i n b) -> p i n b", i=2, b=half)))
                        settle()
                    V.copy_predicated(sc0[:, :, :], lvl[0:NM, 448:464].unsqueeze(1).broadcast_to([NM, 2, NM]),
                                      PS[0:NM, 6, 64:96].rearrange("p (i t) -> p i t", i=2)).then_inc(c0_copied, 1)

            def pool_out(g):
                n = ("pool", g)
                dve.wait_ge(obhi_ready, g + 1)
                tile_free(V.scalar_tensor_tensor(out=halves(oblo[:, g, :]), in0=acc_full(n), scalar=col("pscale", g),
                                                 in1=halves(obhi[:, g, :].bitcast(F32)), op0=ALU.mult,
                                                 op1=ALU.subtract), n)

            def pool_prep(g):
                W_, w = T + PADC, POOL_WINDOWS[g]
                tile_freed(dve, ("pin", g))
                src = pin[:, g, :]
                cur = src
                for s in range(g + 1):
                    d = 1 << s
                    dst = pp[s % 2]
                    tick(V.tensor_tensor(dst[:, 2 * d - 1:W_], cur[:, 2 * d - 1:W_], cur[:, d - 1:W_ - d], ALU.add))
                    settle()
                    cur = dst
                dst = pp[(g + 1) % 2]
                c0 = PADC + w - 1
                tick(V.scalar_tensor_tensor(out=dst[:, c0:W_], in0=cur[:, c0:W_], scalar=1.0 / w, in1=src[:, c0:W_],
                                            op0=ALU.mult, op1=ALU.subtract))
                tick(V.tensor_tensor(dst[:, PADC:c0], cur[:, PADC:c0], inv_n[:, 0:w - 1], ALU.mult))
                settle()
                tick(V.tensor_tensor(dst[:, PADC:c0], dst[:, PADC:c0], src[:, PADC:c0], ALU.subtract))
                settle()
                if g >= 2:
                    tile_done(dve, ("pool", g - 2))
                tick(V.tensor_copy(pdhi[g % 2][:, :], dst[:, PADC:W_]))
                settle()
                V.tensor_tensor(pdlo[g % 2][:, :], dst[:, PADC:W_], pdhi[g % 2][:, :].bitcast(F32), ALU.subtract)\
                 .then_inc(pd_ready, 1)
                dve.wait_ge(pd_ready, g + 1)

            def branch_b(k):
                n = ("y", 0, k)
                tile_done(dve, n)
                tile_freed(dve, ("g", 0, k))
                tile_free(V.tensor_tensor(halves(mix[:, k, :]), acc_full(n), halves(mix[:, k, :]), ALU.mult), n)

            for idx, (name, hooks) in enumerate(order):
                kind, h = name[0:2]
                p, hh = h // 2, h % 2
                if 1 <= idx <= 4:
                    values_out(idx - 1, v_turned, v_copied, vtok1)
                for step in hooks:
                    rec_step(*step)
                if name == ("y", 0, 0):
                    branch_b(0)
                if kind == "f":
                    tile_freed(dve, name)
                    if p >= 2:
                        dve.wait_ge(o_done, 5 * (p - 1))
                    f, k_ = av[p % 2][:, hh, :], kf[p % 2][:, hh, :]
                    tick(V.tensor_scalar(f, k_, omlb[:, h:h + 1], lb[:, h:h + 1], ALU.mult, ALU.add))
                    settle()
                    V.tensor_scalar(k_, f, -1.0, 1.0, ALU.mult, ALU.add).then_inc(f_ready, 1)
                    dve.wait_ge(ln_ready, h + 1)
                    V.tensor_tensor_scan(f, rmask[:, :], f, 0.0, ALU.mult, ALU.add).then_inc(a_ready, 1)
                if name == ("q", 5):
                    dve.wait_ge(spilled, 16)
                    pool_prep(0)
                elif name == ("f", 5):
                    pool_prep(1)
                elif kind == "og" and 1 <= h <= 2:
                    pool_prep(h + 1)
                elif kind == "pool":
                    pool_out(h)

            for t in range(4):
                for k in (2 * t, 2 * t + 1):
                    if k:
                        branch_b(k)
                tile_freed(dve, ("og", t))
                dve.wait_ge(orn, t + 1)
                tick(V.scalar_tensor_tensor(out=oT[:, t, :], in0=oT[:, t, :], scalar=col("head", t),
                                            in1=E[1][:, t % 2, :], op0=ALU.mult, op1=ALU.mult))
                settle()
                V.tensor_tensor(oT[:, t, :], oT[:, t, :], og[:, t, :], ALU.mult).then_inc(on_ready, 1)
                dve.wait_ge(oahi_ready, t + 1)
                V.tensor_tensor(oalo[:, t, :], oT[:, t, :], oahi[:, t, :].bitcast(F32), ALU.subtract)\
                 .then_inc(oa_ready, 1)
            for k in range(KT):
                n = ("y", 1, k)
                tile_done(dve, n)
                tile_freed(dve, ("g", 1, k))
                if k >= 2:
                    dve.wait_ge(mix_ready, k - 1)
                tile_free(V.tensor_tensor(halves(tmp[k % 2][:, :]), acc_full(n), halves(ga(k)), ALU.mult), n)
                tile_freed(dve, n)
                V.tensor_tensor(mix[:, k, :], mix[:, k, :], tmp[k % 2][:, :], ALU.add).then_inc(mix_ready, 1)
            for k in range(KT):
                dve.wait_ge(mixhi_ready, k + 1)
                dve.wait_ge(mix_ready, k + 1)
                V.tensor_tensor(zlo[:, k, :], mix[:, k, :], zhi[:, k, :].bitcast(F32), ALU.subtract)\
                 .then_inc(mixz_ready, 1)
            dve.wait_ge(h_back, 16)
            dve.wait_ge(mixz_ready, KT)
            for k in range(KT):
                n = ("out", k)
                tile_done(dve, n)
                tile_free(V.tensor_tensor(halves(hT[:, k, :]), acc_full(n), halves(hT2[:, k, :]), ALU.add), n)
                if k:
                    norm_add(norm2, k - 1)
            norm_add(norm2, KT - 1)
            for k in (6, 7):
                tile_freed(dve, ("out", k))
            norm_split(norm2)

            for j in range(FT // 2):
                for k in (2 * j, 2 * j + 1):
                    tile_freed(dve, ("u", k))
                    u, c = ub[k % 2], cb[k % 2][:, :]
                    if k >= 2:
                        tile_freed(dve, ("vv", k - 2))
                    tick(V.tensor_scalar(c, u[:, NM:T], col("convw", 2 * FT + k), col("convb", k), ALU.mult, ALU.add))
                    settle()
                    tick(V.scalar_tensor_tensor(out=c, in0=u[:, NM - 1:T - 1], scalar=col("convw", FT + k), in1=c,
                                                op0=ALU.mult, op1=ALU.add))
                    settle()
                    V.scalar_tensor_tensor(out=c, in0=u[:, NM - 2:T - 2], scalar=col("convw", k), in1=c,
                                           op0=ALU.mult, op1=ALU.add).then_inc(c_ready, 1)
                for k in (2 * j, 2 * j + 1):
                    n = ("vv", k)
                    tile_done(dve, n)
                    dve.wait_ge(silu_ready, k + 1)
                    if k >= 2:
                        dve.wait_ge(g_ready, k - 1)
                    tile_free(V.tensor_tensor(gt[k % 2][:, :], acc_real(n), cb[k % 2][:, :], ALU.mult), n)
                for k in (2 * j, 2 * j + 1):
                    dve.wait_ge(ghi_ready, k + 1)
                    V.tensor_tensor(glo[:, k, :], gt[k % 2][:, :], ghi[:, k, :].bitcast(F32), ALU.subtract)\
                     .then_inc(g_ready, 1)
            tick(V.tensor_tensor(g12, prm[:, ROWS["final"][0]:ROWS["final"][0] + KT],
                                 prm[:, ROWS["pre"][0]:ROWS["pre"][0] + KT], ALU.mult))

            def sums_add(k):
                for x, (sq_, acc) in enumerate(((qa, suma), (qb, sumb))):
                    dve.wait_ge(fsq, 2 * k + x + 1)
                    if k > 1:
                        dve.wait_ge(fadd, 2 * (k - 2) + x + 1)
                    V.tensor_tensor(acc[:, :], acc[:, :], sq_[k % 2][:, :], ALU.add).then_inc(fadd, 1)

            for j in range(4):
                for k in (2 * j, 2 * j + 1):
                    n = ("dn", k)
                    tile_done(dve, n)
                    tile_free(V.tensor_tensor(hT[:, k, NM:T], acc_real(n), hT[:, k, NM:T], ALU.add), n)
                for k in (2 * j, 2 * j + 1):
                    if k:
                        sums_add(k)
                if j == 0:
                    dve.wait_ge(meta_turned, 1)
                    V.tensor_copy(hT[:, :, 0:NM], PS[:, 5, 0:P].rearrange("p (k t) -> p k t", k=KT))\
                     .then_inc(h1_meta, 1)
                    dve.wait_ge(h1_meta, 1)
                if j == 1:
                    dve.wait_ge(fm_done, 1)
                    V.tensor_reduce(rm[:, :], PS[:, 4, 0:P].rearrange("p (k t) -> p t k", k=KT), AX.X, ALU.add)\
                     .then_inc(fm_done, 1)
                if j == 2:
                    dve.wait_ge(fm_rb, 1)
                    tick(V.tensor_tensor(zm[:, :, :], hT[:, :, 0:NM], rm[:, :].unsqueeze(1).broadcast_to([P, KT, NM]),
                                         ALU.mult))
                    settle()
                    p0 = ROWS["pre"][0]
                    V.tensor_tensor(zm[:, :, :], zm[:, :, :], prm[:, p0:p0 + KT].unsqueeze(2).broadcast_to([P, KT, NM]),
                                    ALU.mult).then_inc(fm_z, 1)
                    dve.wait_ge(fm_hi, 1)
                    V.tensor_tensor(zlo[:, :, 0:NM], zm[:, :, :], zhi[:, :, 0:NM].bitcast(F32), ALU.subtract)\
                     .then_inc(fm_z, 1)
            dve.wait_ge(fsum_done, 2)
            dve.wait_ge(r1sq, 1)
            V.tensor_tensor(r2t[:, :], PS[:, 7, :], r2t[:, :], ALU.mult).then_inc(r2in, 1)
            dve.wait_ge(r2log, 1)
            V.tensor_tensor(r2t[:, :], r2t[:, :], r1l[:, :], ALU.add).then_inc(r2in, 1)
            dve.wait_ge(rz_ready, 1)
            for k in range(KT + 1):
                if k < KT:
                    if k == 0:
                        settle()
                    if k >= 2:
                        dve.wait_ge(h1_lo, k - 1)
                    V.scalar_tensor_tensor(out=nzt[k % 2][:, NM:T], in0=hT[:, k, NM:T], scalar=g12[:, k:k + 1],
                                           in1=nrb[:, NM:T], op0=ALU.mult, op1=ALU.mult).then_inc(h1_z, 1)
                if k:
                    dve.wait_ge(h1_hi, k)
                    V.tensor_tensor(zlo[:, k - 1, NM:T], nzt[(k - 1) % 2][:, NM:T], zhi[:, k - 1, NM:T].bitcast(F32),
                                    ALU.subtract).then_inc(h1_lo, 1)
            dve.wait_ge(r1_ready, 1)
            for k in range(KT):
                V.scalar_tensor_tensor(out=hT[:, k, NM:T], in0=hT[:, k, NM:T], scalar=col("final", k), in1=r1[:, :],
                                       op0=ALU.mult, op1=ALU.mult).then_inc(h1_ready, 1)

            norm_split(normq)
            dve.wait_ge(normq.z_ready, 2)
            norm_split(normk)
            dve.wait_ge(late_in, 32)
            r_ = slice(64, P)
            t1, t2 = PT[0][r_, 0:T], PT[0][r_, T:2 * T]
            tile_done(dve, ("kpe", 0))
            dve.wait_ge(fl_ready, 1)
            for i in range(2):
                for t_, rows, x in ((t1, slice(32, 64), 1), (t2, slice(64, 96), 2)):
                    ins = V.tensor_tensor(halves(t_[32 * i:32 * i + 32, :]), acc_full(("kpe", 0), rows),
                                          halves(trig[rows, x, :]), ALU.mult)
                    if i + x < 3:
                        tick(ins)
            tile_free(ins, ("kpe", 0))
            tile_freed(dve, ("kpe", 0))
            tick(V.tensor_tensor(kh[0][r_, :], t1, t2, ALU.add))
            V.tensor_tensor(kh[1][r_, :], t1, t2, ALU.add).then_inc(kr_ready, 1)
            for i in range(5):
                for j in range(2):
                    n = ("mv", i, j)
                    rows = NM if i == 0 else P
                    tile_done(dve, n)
                    tile_free(V.tensor_copy(vtok[0:rows, i, SEQ * j:SEQ * (j + 1)], acc_real(n, slice(0, rows))), n)

            def attention(A, project, between):
                for h in range(HEADS + 2):
                    project(h)
                    for i in range(4):
                        if h < HEADS:
                            dve.wait_ge(A.s_done, 4 * h + i + 1)
                            s = 4 * (h % 2) + i
                            V.tensor_reduce(negmax[:, s:s + 1], s_view(i), AX.XY if i == 3 else AX.X, ALU.max,
                                            negate=True).then_inc(A.m_ready, 1)
                        if i == 1:
                            between(h)
                        if 1 <= h <= HEADS and i >= 2:
                            x, g = h - 1, 2 * i - 3
                            dve.wait_ge(A.g_turned, 4 * x + g + 1)
                            if x >= 2:
                                dve.wait_ge(A.o_done, x - 1)
                            n = 512 if g == 1 else 384
                            V.tensor_copy(PT[x % 2][:, G_COL[g]:G_COL[g] + n], PS[:, 3, 0:n]).then_inc(A.pt_v, 1)
                    if h < HEADS:
                        dve.wait_ge(A.p_exp, 4 * h + 4)
                        s = 4 * (h % 2)
                        tick(V.reciprocal(rinv, rowsum[:, s:s + 4]))
                        settle()
                        for i in range(4):
                            t = Pm[h % 2][:, ATT_OFF[i]:ATT_OFF[i] + ATT_N[i]]
                            ins = V.tensor_scalar(t, t, rinv[:, i:i + 1], None, ALU.mult)
                            if i < 3:
                                tick(ins)
                        ins.then_inc(A.p_ready, 1)

            def gate_sums(i):
                f0, f1 = fgt[0:HEADS, 0, :], fgt[0:HEADS, 1, :]
                settle()
                if i == 0:
                    dve.wait_ge(fl_abs, 1)
                    tick(V.tensor_scalar(f0, f0, 0.0, None, ALU.min))
                elif i == 1:
                    tick(V.tensor_tensor(f0, f0, f1, ALU.subtract))
                elif i == 2:
                    tick(V.tensor_tensor_scan(f1, trig[0:HEADS, 0, :], f0, 0.0, ALU.mult, ALU.add))
                elif i == 3:
                    tick(V.tensor_scalar(f0, f1, -1.0, None, ALU.mult))
                elif i == 4:
                    tick(V.memset(nch[:, :].bitcast(F32), 0.0))
                elif i == 5:
                    tick(V.tensor_copy(nch[0:HEADS, :], f0))
                elif i == 6:
                    tick(V.tensor_tensor(nch[32:32 + HEADS, :], f0, nch[0:HEADS, :].bitcast(F32), ALU.subtract))
                elif i == 7:
                    tick(V.tensor_copy(nch[64:P, :], nch[0:64, :].bitcast(F32)))

            def mla_project(h):
                if h >= 2:
                    gate_sums(h - 2)
                for x in ([0, 1] if h == 0 else [h + 1]):
                    if x < HEADS:
                        n = ("mq", x)
                        tile_done(dve, n)
                        if x >= 2:
                            dve.wait_ge(mla.s_done, 4 * (x - 1))
                        tile_free(V.scalar_tensor_tensor(out=qh[x % 2][:, :], in0=acc_real(n), scalar=MLA_SCALE,
                                                         in1=trig[:, 0, NM:T], op0=ALU.mult, op1=ALU.mult), n)

            attention(mla, mla_project, lambda h: None)

            def gated(kind, A, b):
                dve.wait_ge(A.o_ready, HEADS)
                for k in range(KT):
                    tile_freed(dve, (kind, k))
                    if k >= 2:
                        dve.wait_ge(y_ready, KT * b + k - 1)
                    V.tensor_tensor(nzt[k % 2][:, 0:SEQ], omla[:, k, :], nsq[k % 2][:, 0:SEQ], ALU.mult).then_inc(ygt, 1)
                    dve.wait_ge(yhi_r, KT * b + k + 1)
                    V.tensor_tensor(ylo[:, k, :], nzt[k % 2][:, 0:SEQ], yhi[:, k, :].bitcast(F32), ALU.subtract)\
                     .then_inc(y_ready, 1)

            def gates(b):
                for k in range(KT):
                    n = ("hy", b, k)
                    tile_done(dve, n)
                    tile_freed(dve, ("hg", b, k))
                    dst = mix2[:, k, :] if b == 0 else nzt[k % 2][:, 0:SEQ]
                    if b and k >= 2:
                        dve.wait_ge(mix2_ready, k - 1)
                    tile_free(V.tensor_tensor(dst, acc_real(n), nsq[k % 2][:, 0:SEQ], ALU.mult), n)
                    if b:
                        tile_freed(dve, n)
                        V.tensor_tensor(mix2[:, k, :], mix2[:, k, :], nzt[k % 2][:, 0:SEQ], ALU.add)\
                         .then_inc(mix2_ready, 1)

            gated("mz", mla, 0)
            gates(0)
            for k in range(KT):
                values_out(k, xv_turned, xv_copied, vtok)
            settle()
            for i in range(2):
                o = slice(64 - 64 * i, P - 64 * i)
                tick(V.tensor_copy(xkb[i][o, :], nch[o, :].bitcast(F32)))
            settle()

            def split_lo(h):
                i, r = h % 2, slice(64 * (h % 2), 64 * (h % 2) + 64)
                o = slice(64 - r.start, 128 - r.start)
                dve.wait_ge(fox_hi, 4 * (h + 1))
                q = fq[h // 2 % 2]
                V.tensor_tensor(xqa[i][o, :], q[r, :], xqa[i][r, :].bitcast(F32), ALU.subtract).then_inc(fox_lo, 1)
                V.tensor_tensor(xkb[i][r, :], fk[r, :], xka[i][r, :].bitcast(F32), ALU.subtract).then_inc(fox_lo, 1)
                V.tensor_copy(xqb[i][o, :], pick[o, h:h + 1].bitcast(F32).broadcast_to([64, SEQ])).then_inc(fox_lo, 1)

            attention(fox, lambda h: split_lo(0) if h == 0 else None, lambda h: split_lo(h + 1) if h < HEADS - 1 else None)
            gated("xz", fox, 1)
            dve.wait_ge(y_ready, 2 * KT)
            gates(1)
            for k in range(KT):
                dve.wait_ge(fmixhi, k + 1)
                dve.wait_ge(mix2_ready, k + 1)
                V.tensor_tensor(zlo[:, k, 0:SEQ], mix2[:, k, :], zhi[:, k, 0:SEQ].bitcast(F32), ALU.subtract)\
                 .then_inc(fmix, 1)
            dve.wait_ge(late_in, 48)
            for j in range(4):
                cols = slice(256 * j, 256 * (j + 1))
                for i in range(QB):
                    n = ("fin", j, i)
                    dve.wait_ge(fin_sq, QB * j + i + 1)
                    if j == 3:
                        V.tensor_reduce(ssum[:, i:i + 1], fsum[:, 4 * i:4 * i + 4], AX.X, ALU.add).then_inc(fin_sum, 1)
                    tile_free(V.tensor_tensor(mtok[:, i, cols], acc_real(n, n=256), gpost[:, cols], ALU.mult), n)
                    if j == 3:
                        tile_freed(dve, n)
                        dve.wait_ge(fin_rstd, i + 1)
                        V.scalar_tensor_tensor(out=mtok[:, i, :], in0=mtok[:, i, :], scalar=ssum[:, i:i + 1],
                                               in1=htok[:, i, :], op0=ALU.mult, op1=ALU.add).then_inc(fin_out, 1)


_OUTS = [((1, SEQ, D), "float32")]


def kernel(**inputs):
    import concourse.bacc as _bacc
    from concourse.bass_utils import run_bass_kernel_spmd as _run

    nc = _bacc.Bacc("TRN2", target_bir_lowering=False, num_devices=1)
    arrays, args = {}, {}
    every = {k: np.asarray(v) for k, v in inputs.items()}
    every.update(host_constants())
    for name, value in every.items():
        value = np.ascontiguousarray(value)
        arrays[f"in_{name}"] = value
        args[name] = nc.dram_tensor(f"in_{name}", value.shape, mybir.dt.from_np(value.dtype), kind="ExternalInput").ap()
    out = nc.dram_tensor("out_0", _OUTS[0][0], F32, kind="ExternalOutput").ap()
    build_program(nc, args, out)
    r = _run(nc, [arrays], core_ids=[0])
    return r.results[0]["out_0"]
```
